# Optimizing a Trainium2 kernel written in Bass

```python
import numpy as np
import jax
import jax.numpy as jnp
from jax import lax

D_MODEL = 2048
BATCH = 1
SEQ = 256
DEPTH = 2

HEAD_DIM = 128
A_GROUPS = 8
A_WIDTH = A_GROUPS * HEAD_DIM
A_CHUNK = 128
B_HEADS = 8
B_KV_HEADS = 2
B_GROUP = B_HEADS // B_KV_HEADS
B_WIDTH = B_HEADS * HEAD_DIM
KV_WIDTH = B_KV_HEADS * HEAD_DIM
CMP_LEN = 32
CMP_STRIDE = 16
CMP_HIDDEN = 256
SLC_BLOCK = 64
TOP_N = 8
WINDOW = 512
Q_BLOCK = 128
SLC_Q_BLOCK = 32
EVEN_IN = 3 * A_WIDTH + 2 * B_WIDTH + 6 * KV_WIDTH + 3 * B_HEADS
C_HEADS = 16
C_KDIM = 128
C_VDIM = 128
C_KW = C_HEADS * C_KDIM
C_WIDTH = C_HEADS * C_VDIM
C_CHUNK = 64
ODD_IN = 2 * C_KW + 2 * C_WIDTH

N_EVEN = (DEPTH + 1) // 2
N_ODD = DEPTH // 2
EPS = 1e-6
NEG_INF = -1e30
FORCE_SCORE = 1e6

kernel_name = "hybrid_gmlp_nsa_hgrn2_trunk"

def rms_norm(x, g):
    xf = x.astype(jnp.float32)
    y = xf * lax.rsqrt(jnp.mean(xf * xf, axis=-1, keepdims=True) + EPS)
    return (y * g.astype(jnp.float32)).astype(x.dtype)

def layer_norm(x, g, b):
    xf = x.astype(jnp.float32)
    mu = jnp.mean(xf, axis=-1, keepdims=True)
    var = jnp.mean(jnp.square(xf - mu), axis=-1, keepdims=True)
    y = (xf - mu) * lax.rsqrt(var + EPS)
    return (y * g.astype(jnp.float32) + b.astype(jnp.float32)).astype(x.dtype)

def masked_softmax(s, valid):
    s = jnp.where(valid, s.astype(jnp.float32), NEG_INF)
    m = jnp.max(s, axis=-1, keepdims=True)
    e = jnp.where(valid, jnp.exp(s - m), 0.0)
    return e / jnp.maximum(jnp.sum(e, axis=-1, keepdims=True), 1e-30)

def alibi_slopes():
    h = jnp.arange(1, B_HEADS + 1, dtype=jnp.float32)
    return jnp.exp2(-8.0 * h / B_HEADS).reshape(B_KV_HEADS, B_GROUP)

def cmp_to_slc_overlap(n_cmp, n_slc):
    cs = np.arange(n_cmp)[:, None] * CMP_STRIDE
    ss = np.arange(n_slc)[None, :] * SLC_BLOCK
    ov = np.clip(np.minimum(cs + CMP_LEN, ss + SLC_BLOCK) - np.maximum(cs, ss), 0, None) / CMP_LEN
    return jnp.asarray(ov, dtype=jnp.float32)

def compress(k, blk_idx, pos, w1, b1, w2):
    B = k.shape[0]
    n_cmp = blk_idx.shape[0]
    blocks = k[:, blk_idx] + pos[:, None, :]
    flat = blocks.transpose(0, 1, 3, 2, 4).reshape(B, n_cmp, B_KV_HEADS, CMP_LEN * HEAD_DIM)
    return jax.nn.gelu(flat @ w1 + b1) @ w2

def nsa_attention(q, k_cmp, v_cmp, k_slc, v_slc, k_win, v_win, gates,
                  q_gain, k_gain, cmp_pos, cmp_w1, cmp_b1, cmp_w2):
    B, S = q.shape[:2]
    slopes = alibi_slopes()
    q = rms_norm(q, q_gain) * (HEAD_DIM ** -0.5)
    t = jnp.arange(S)

    n_cmp = (S - CMP_LEN) // CMP_STRIDE + 1
    blk_idx = np.arange(n_cmp)[:, None] * CMP_STRIDE + np.arange(CMP_LEN)[None, :]
    kc = rms_norm(compress(k_cmp, blk_idx, cmp_pos[0], cmp_w1[0], cmp_b1[0], cmp_w2[0]), k_gain[0])
    vc = compress(v_cmp, blk_idx, cmp_pos[1], cmp_w1[1], cmp_b1[1], cmp_w2[1])
    end = jnp.asarray(blk_idx[:, -1])
    dist_c = t[:, None] - end[None, :]
    s_c = jnp.einsum('bskgd,bnkd->bkgsn', q, kc)
    s_c = s_c - slopes[:, :, None, None] * dist_c.astype(jnp.float32)
    p_cmp = masked_softmax(s_c, dist_c >= 0)
    o_cmp = jnp.einsum('bkgsn,bnkd->bskgd', p_cmp.astype(vc.dtype), vc)

    n_slc = S // SLC_BLOCK
    n_sel = min(TOP_N, n_slc)
    imp = jnp.einsum('bkgsn,nj->bksj', p_cmp, cmp_to_slc_overlap(n_cmp, n_slc))
    j = jnp.arange(n_slc)[None, :]
    cur = (t // SLC_BLOCK)[:, None]
    valid_blk = j * SLC_BLOCK <= t[:, None]
    forced = (j == 0) | (j == cur) | (j == cur - 1)
    imp = jnp.where(forced, FORCE_SCORE, jnp.where(valid_blk, imp, -1.0))
    _, sel = lax.top_k(imp, n_sel)

    ks_blocks = rms_norm(k_slc, k_gain[1]).reshape(B, n_slc, SLC_BLOCK, B_KV_HEADS, HEAD_DIM).transpose(0, 3, 1, 2, 4)
    vs_blocks = v_slc.reshape(B, n_slc, SLC_BLOCK, B_KV_HEADS, HEAD_DIM).transpose(0, 3, 1, 2, 4)
    nqb = S // SLC_Q_BLOCK
    q_sb = q.reshape(B, nqb, SLC_Q_BLOCK, B_KV_HEADS, B_GROUP, HEAD_DIM).swapaxes(0, 1)
    sel_b = sel.reshape(B, B_KV_HEADS, nqb, SLC_Q_BLOCK, n_sel).transpose(2, 0, 1, 3, 4)
    t_b = t.reshape(nqb, SLC_Q_BLOCK)
    b_ix = jnp.arange(B)[:, None, None, None]
    k_ix = jnp.arange(B_KV_HEADS)[None, :, None, None]
    n_keys = n_sel * SLC_BLOCK

    def slc_block(args):
        qb, sb, tb = args
        kg = ks_blocks[b_ix, k_ix, sb]
        vg = vs_blocks[b_ix, k_ix, sb].reshape(B, B_KV_HEADS, SLC_Q_BLOCK, n_keys, HEAD_DIM)
        kpos = sb[..., None] * SLC_BLOCK + jnp.arange(SLC_BLOCK)
        dist = (tb[None, None, :, None, None] - kpos).reshape(B, B_KV_HEADS, 1, SLC_Q_BLOCK, n_keys)
        sc = jnp.einsum('bqkgd,bkqnjd->bkgqnj', qb, kg).reshape(B, B_KV_HEADS, B_GROUP, SLC_Q_BLOCK, n_keys)
        sc = sc - slopes[None, :, :, None, None] * dist.astype(jnp.float32)
        p = masked_softmax(sc, dist >= 0)
        return jnp.einsum('bkgqm,bkqmd->bqkgd', p.astype(vg.dtype), vg)

    o_slc = lax.map(slc_block, (q_sb, sel_b, t_b)).swapaxes(0, 1).reshape(B, S, B_KV_HEADS, B_GROUP, HEAD_DIM)

    pad = ((0, 0), (WINDOW, 0), (0, 0), (0, 0))
    kw_p = jnp.pad(rms_norm(k_win, k_gain[2]), pad)
    vw_p = jnp.pad(v_win, pad)
    nwb = S // Q_BLOCK
    span = WINDOW + Q_BLOCK
    q_wb = q.reshape(B, nwb, Q_BLOCK, B_KV_HEADS, B_GROUP, HEAD_DIM).swapaxes(0, 1)

    def win_block(args):
        i, qb = args
        kb = lax.dynamic_slice_in_dim(kw_p, i * Q_BLOCK, span, axis=1)
        vb = lax.dynamic_slice_in_dim(vw_p, i * Q_BLOCK, span, axis=1)
        tq = i * Q_BLOCK + jnp.arange(Q_BLOCK)
        kpos = i * Q_BLOCK - WINDOW + jnp.arange(span)
        dist = tq[:, None] - kpos[None, :]
        valid = (kpos[None, :] >= 0) & (dist >= 0) & (dist < WINDOW)
        sc = jnp.einsum('bqkgd,bmkd->bkgqm', qb, kb) - slopes[:, :, None, None] * dist.astype(jnp.float32)
        p = masked_softmax(sc, valid)
        return jnp.einsum('bkgqm,bmkd->bqkgd', p.astype(vb.dtype), vb)

    o_win = lax.map(win_block, (jnp.arange(nwb), q_wb)).swapaxes(0, 1).reshape(B, S, B_KV_HEADS, B_GROUP, HEAD_DIM)

    o = (gates[:, :, 0, :, :, None] * o_cmp + gates[:, :, 1, :, :, None] * o_slc
         + gates[:, :, 2, :, :, None] * o_win)
    return o.reshape(B, S, B_WIDTH)

def even_layer(x, norm_g, w_in, ln_g, ln_b, sgu_w, sgu_b, q_gain, k_gain,
               cmp_pos, cmp_w1, cmp_b1, cmp_w2, w_out):
    B, S, _ = x.shape
    z = rms_norm(x, norm_g) @ w_in
    cuts = (A_WIDTH, 2 * A_WIDTH, 3 * A_WIDTH, 3 * A_WIDTH + B_WIDTH,
            3 * A_WIDTH + 2 * B_WIDTH, 3 * A_WIDTH + 2 * B_WIDTH + 6 * KV_WIDTH)
    a_u, a_v, a_gate, b_q, b_gate, b_kv, b_g = jnp.split(z, cuts, axis=-1)

    u = jax.nn.gelu(a_u)
    v = layer_norm(jax.nn.gelu(a_v), ln_g, ln_b)
    nca = S // A_CHUNK
    v = v.reshape(B, nca, A_CHUNK, A_GROUPS, HEAD_DIM)
    w_s = jnp.where(np.tril(np.ones((A_CHUNK, A_CHUNK), dtype=bool)), sgu_w, 0.0)
    v = jnp.einsum('gts,bnsgc->bntgc', w_s, v) + sgu_b.T[:, :, None]
    a_out = u * v.reshape(B, S, A_WIDTH) * jax.nn.silu(a_gate)

    q = b_q.reshape(B, S, B_KV_HEADS, B_GROUP, HEAD_DIM)
    kv = b_kv.reshape(B, S, 6, B_KV_HEADS, HEAD_DIM)
    gates = jax.nn.sigmoid(b_g.reshape(B, S, 3, B_KV_HEADS, B_GROUP))
    b_out = nsa_attention(q, kv[:, :, 0], kv[:, :, 1], kv[:, :, 2], kv[:, :, 3], kv[:, :, 4], kv[:, :, 5],
                          gates, q_gain, k_gain, cmp_pos, cmp_w1, cmp_b1, cmp_w2)
    b_out = b_out * jax.nn.silu(b_gate)

    return x + jnp.concatenate([a_out, b_out], axis=-1) @ w_out

def hgrn2_chunked(q, k, g, v):
    B, S, _ = q.shape
    nc = S // C_CHUNK

    def heads(a, d):
        return a.reshape(B, nc, C_CHUNK, C_HEADS, d).transpose(0, 3, 1, 2, 4)

    q, k, g, v = heads(q, C_KDIM), heads(k, C_KDIM), heads(g, C_KDIM), heads(v, C_VDIM)
    G = jnp.cumsum(g, axis=3)
    G_mid = G[:, :, :, C_CHUNK // 2 - 1:C_CHUNK // 2]
    G_end = G[:, :, :, -1:]
    attn = jnp.einsum('bhntd,bhnsd->bhnts', q * jnp.exp(G - G_mid), k * jnp.exp(G_mid - G))
    attn = jnp.where(np.tril(np.ones((C_CHUNK, C_CHUNK), dtype=bool)), attn, 0.0)
    o_intra = jnp.einsum('bhnts,bhnsv->bhntv', attn, v)
    q_in = jnp.moveaxis(q * jnp.exp(G), 2, 0)
    k_st = jnp.moveaxis(k * jnp.exp(G_end - G), 2, 0)
    v_c = jnp.moveaxis(v, 2, 0)
    decay = jnp.moveaxis(jnp.exp(G_end[:, :, :, 0]), 2, 0)

    def step(state, xs):
        qn, kn, vn, dn = xs
        o = jnp.einsum('bhtd,bhdv->bhtv', qn, state)
        state = dn[..., None] * state + jnp.einsum('bhsd,bhsv->bhdv', kn, vn)
        return state, o

    init = jnp.zeros((B, C_HEADS, C_KDIM, C_VDIM), q.dtype)
    _, o_inter = lax.scan(step, init, (q_in, k_st, v_c, decay))
    o = o_intra + jnp.moveaxis(o_inter, 0, 2)
    return o.transpose(0, 2, 3, 1, 4).reshape(B, S, C_HEADS, C_VDIM)

def odd_layer(x, layer, norm_g, w_in, lb_logits, out_g, w_out):
    B, S, _ = x.shape
    z = rms_norm(x, norm_g) @ w_in
    q, f_logit, i_in, gate = jnp.split(z, (C_KW, 2 * C_KW, 2 * C_KW + C_WIDTH), axis=-1)
    p = jax.nn.softmax(lb_logits.astype(jnp.float32), axis=0)
    lb = (jnp.cumsum(p, axis=0) - p[0])[layer]
    f = lb + (1.0 - lb) * jax.nn.sigmoid(f_logit.astype(jnp.float32))
    o = hgrn2_chunked(q.astype(jnp.float32), 1.0 - f, jnp.log(f), i_in.astype(jnp.float32))
    o = rms_norm(o, out_g).reshape(B, S, C_WIDTH).astype(x.dtype) * jax.nn.silu(gate)
    return x + o @ w_out

def setup_inputs(seed: int = 0) -> dict:
    key = jax.random.key(seed)
    ks = jax.random.split(key, 20)

    def nrm(k, shape, scale):
        return scale * jax.random.normal(k, shape, jnp.float32)

    ab = A_WIDTH + B_WIDTH
    return {
        "x": nrm(ks[0], (BATCH, SEQ, D_MODEL), 1.0),
        "even_norm": 1.0 + nrm(ks[1], (N_EVEN, D_MODEL), 0.02),
        "even_w_in": nrm(ks[2], (N_EVEN, D_MODEL, EVEN_IN), D_MODEL ** -0.5),
        "sgu_ln_g": 1.0 + nrm(ks[3], (N_EVEN, A_WIDTH), 0.02),
        "sgu_ln_b": nrm(ks[4], (N_EVEN, A_WIDTH), 0.02),
        "sgu_w": nrm(ks[5], (N_EVEN, A_GROUPS, A_CHUNK, A_CHUNK), A_CHUNK ** -0.5),
        "sgu_b": 1.0 + nrm(ks[6], (N_EVEN, A_GROUPS, A_CHUNK), 0.1),
        "nsa_q_gain": 1.0 + nrm(ks[7], (N_EVEN, HEAD_DIM), 0.02),
        "nsa_k_gain": 1.0 + nrm(ks[8], (N_EVEN, 3, HEAD_DIM), 0.02),
        "cmp_pos": nrm(ks[9], (N_EVEN, 2, CMP_LEN, HEAD_DIM), 0.02),
        "cmp_w1": nrm(ks[10], (N_EVEN, 2, CMP_LEN * HEAD_DIM, CMP_HIDDEN), (CMP_LEN * HEAD_DIM) ** -0.5),
        "cmp_b1": nrm(ks[11], (N_EVEN, 2, CMP_HIDDEN), 0.01),
        "cmp_w2": nrm(ks[12], (N_EVEN, 2, CMP_HIDDEN, HEAD_DIM), CMP_HIDDEN ** -0.5),
        "even_w_out": nrm(ks[13], (N_EVEN, ab, D_MODEL), ab ** -0.5),
        "odd_norm": 1.0 + nrm(ks[14], (N_ODD, D_MODEL), 0.02),
        "odd_w_in": nrm(ks[15], (N_ODD, D_MODEL, ODD_IN), D_MODEL ** -0.5),
        "hgrn_lb": nrm(ks[16], (DEPTH, C_KW), 0.1),
        "hgrn_out_gain": 1.0 + nrm(ks[17], (N_ODD, C_VDIM), 0.02),
        "odd_w_out": nrm(ks[18], (N_ODD, C_WIDTH, D_MODEL), C_WIDTH ** -0.5),
    }

def reference(x, even_norm, even_w_in, sgu_ln_g, sgu_ln_b, sgu_w, sgu_b, nsa_q_gain, nsa_k_gain,
              cmp_pos, cmp_w1, cmp_b1, cmp_w2, even_w_out, odd_norm, odd_w_in, hgrn_lb,
              hgrn_out_gain, odd_w_out):
    for layer in range(DEPTH):
        if layer % 2 == 0:
            e = layer // 2
            x = even_layer(x, even_norm[e], even_w_in[e], sgu_ln_g[e], sgu_ln_b[e], sgu_w[e], sgu_b[e],
                           nsa_q_gain[e], nsa_k_gain[e], cmp_pos[e], cmp_w1[e], cmp_b1[e], cmp_w2[e],
                           even_w_out[e])
        else:
            o = layer // 2
            x = odd_layer(x, layer, odd_norm[o], odd_w_in[o], hgrn_lb, hgrn_out_gain[o], odd_w_out[o])
    return x


_drawn_inputs = setup_inputs


def setup_inputs(seed=0):
    import zlib

    import numpy as np

    out = dict(_drawn_inputs(seed))
    spreads = {}
    factors = {'even_norm': 3.507,
     'sgu_ln_g': 8.0,
     'sgu_ln_b': 8.0,
     'nsa_q_gain': 8.0,
     'nsa_k_gain': 8.0,
     'cmp_pos': 25.068,
     'cmp_b1': 38.401,
     'odd_norm': 8.704,
     'hgrn_out_gain': 43.348}
    for name, (base, spread) in spreads.items():
        noise = np.random.default_rng([zlib.crc32(name.encode()), seed]).standard_normal(out[name].shape)
        drawn = base * np.exp(spread * noise) if base else spread * noise
        out[name] = jnp.asarray(drawn.astype(out[name].dtype))
    for name, factor in factors.items():
        out[name] = (out[name] * factor).astype(out[name].dtype)
    return out
```

```python
from contextlib import ExitStack

import concourse.bass as bass
from concourse import mybir
from concourse.alu_op_type import AluOpType as ALU

F32 = mybir.dt.float32
F32R = mybir.dt.float32r
I32 = mybir.dt.int32
ACT = mybir.ActivationFunctionType
AX = mybir.AxisListType

P = 128
D = 2048
KT = D // P
T = 256
TT = T // P
SW = 256
NQ = 4
KQ = KT // NQ
HD = 128
A_WIDTH = 1024
B_WIDTH = 1024
KV0 = 3 * A_WIDTH + 2 * B_WIDTH
NG = 24
GATE0 = KV0 + 6 * SW
NL = 32
NC = (T - NL) // 16 + 1
CW = 2 * NC
EPS = 1e-6
BIG = 1e30
CH = 64
LN_EXP = "natural_log_exp_and_others"
ARENA = 14104

S_PRE, S_ATT, S_SGU, S_OUT0, S_HGRN, S_OUT1, S_END = 0, 10, 26, 30, 38, 70, 78


class Steps:

    def __init__(self, sem, names):
        self.sem, self.names, self.n = sem, names.split(), 0
        assert len(set(self.names)) == len(self.names)

    def did(self, name):
        assert self.names[self.n % len(self.names)] == name, (self.names[self.n % len(self.names)], name)
        self.n += 1
        return 1

    def at(self, name, i=0):
        return i * len(self.names) + self.names.index(name) + 1


def trunk(nc, x, even_norm, even_w_in, sgu_ln_g, sgu_ln_b, sgu_w, sgu_b, q_gain, k_gain, cmp_pos,
          cmp_w1, cmp_b1, cmp_w2, even_w_out, odd_norm, odd_w_in, hgrn_lb, out_gain, odd_w_out, out):
    with ExitStack() as ctx:
        def sb(name, shape, dt=F32):
            return ctx.enter_context(nc.sbuf_tensor(name, shape, dt))

        def sem(name):
            return ctx.enter_context(nc.semaphore(name))

        raw = sb("raw", [P, NQ, KQ, SW])
        whl = sb("whl", [P, NQ, KQ, 2, SW], F32R)
        xhl = sb("xhl", [P, KT, 2, T], F32R)
        cathl = sb("cathl", [P, KT, 2, T], F32R)
        xT = sb("xT", [P, KT, T])
        ident = sb("ident", [P, P])
        ones = sb("ones", [P, P])
        tri64 = sb("tri64", [P, P])
        tri64_i = sb("tri64_i", [P, P], I32)
        tri_i = sb("tri_i", [P, P], I32)
        vecs = sb("vecs", [P, P])
        vT = sb("vT", [P, P])
        posr = sb("posr", [2 * NL, HD])
        posT = sb("posT", [P, 2 * NL])
        sgub = sb("sgub", [1, 8 * P])
        small = sb("small", [P, 256])
        tmp = sb("tmp", [P, 2, 2, SW])
        Z = sb("Z", [P, 4, 2, SW])
        arena = sb("arena", [P, ARENA])

        class Carve:
            def __init__(self):
                self.o = 0

            def __call__(self, n):
                self.o += n
                assert self.o <= ARENA, self.o
                return arena[:, self.o - n:self.o]

        c0 = Carve()
        gav = c0(2048).rearrange("p (a n) -> p a n", a=2)
        gu = c0(2048).rearrange("p (a n) -> p a n", a=8)
        xnat = arena[:, 0:4096].rearrange("p (a n) -> p a n", a=2)
        lngb = c0(2048).rearrange("p (a n) -> p a n", a=2)
        keysT = c0(2 * 527).rearrange("p (a n) -> p a n", a=2)
        vals = c0(1024).rearrange("p (b a n) -> p b a n", b=2, a=2)
        vcmp = c0(256).rearrange("p (a n) -> p a n", a=2)
        w_sT = c0(1024).rearrange("p (a n) -> p a n", a=8)
        dist = c0(414)
        bias = c0(828).rearrange("p (a n) -> p a n", a=2)
        prob = c0(800)[:, 0:798]
        probT = c0(1024).rearrange("p (a n) -> p a n", a=2)
        sgw = arena[:, c0.o - 1024:c0.o].rearrange("p (a n) -> p a n", a=8)
        w2 = c0(512).rearrange("p (i a n) -> p i a n", i=2, a=2)
        obuf = c0(512).rearrange("p (a n) -> p a n", a=2)
        scr = arena[:, c0.o - 512:c0.o]
        wg = prob[:, 0:KT * NG].rearrange("p (k n) -> p k n", k=KT)
        wghl = cathl[:, 8:10].rearrange("p k a n -> p (k a n)")[:, 0:KT * 2 * NG]\
            .rearrange("p (k a n) -> p k a n", k=KT, a=2)
        sgz = c0(512).rearrange("p (a n) -> p a n", a=2)
        xn = arena[:, 7150:7150 + 2048].rearrange("p (r a n) -> p r a n", r=2, a=KQ)
        kpos = arena[:, 0:960]

        c1 = Carve()
        (hF, hK, hG, hGN, hGS, hD1, hE2, hD2, hE3, hKE, hKS, hQE, hQI, hAT, hKN, hSQ, hRS, hSG, hZS,
         hO) = (c1(512) for _ in range(20))
        hST = c1(768).rearrange("p (h c v) -> p h c v", h=2, c=3)
        acc = c1(512)
        sq = c1(512)
        xn1 = arena[:, 0:2048].rearrange("p (r a n) -> p r a n", r=2, a=KQ)
        xres = arena[:, 0:1024].rearrange("p (b a n) -> p b a n", b=2, a=2)

        pp = ctx.enter_context(nc.psum_tensor("pp", [P, 4, 512], F32))
        px = ctx.enter_context(nc.psum_tensor("px", [P, 4, 512], F32))

        landed = [sem(f"landed{q}") for q in range(NQ)]
        hi_done, lo_done = sem("hi_done"), sem("lo_done")
        pe_q = sem("pe_q")
        lo_out, strip_out = sem("lo_out"), sem("strip_out")
        seen = sem("seen")
        x_in, vec_in, sg_in, misc_in = sem("x_in"), sem("vec_in"), sem("sg_in"), sem("misc_in")
        y_out = [sem("y_out0"), sem("y_out1")]

        pool0 = Steps(sem("pool0"), "ms ident ms1 triF tri64a tri64 tri64i trii id0 id1 ic0 ic1 df "
                      "sel0 sel1 selc0 selc1 zw")
        pe0 = Steps(sem("pe0"), "xT0 xT1 xT2 xT3 xT4 xT5 xT6 xT7 vT posT rs wsT0 wsT1")
        act0 = Steps(sem("act0"), "ss0 ss1 xT0 xT2 xT4 xT6 ln rs wg lbe0 lbe1")
        dve0 = Steps(sem("dve0"), "ms xT1 xT3 xT5 xT7 vT posT gain diag0 diag1 rsb wg "
                     "lbm lba lbb lbs lbr lbp0 lbp1 lbc lb omlb wsT0 wsT1")
        xn_done, xhi_done, xlo_done = sem("xn_done"), sem("xhi_done"), sem("xlo_done")
        peP = Steps(sem("peP"), "kT0 gates kT1 ck0 ck1 cv0 cv1 kcT")
        actP = Steps(sem("actP"), "kp0 kp1 ln0 rs0 ln1 rs1 gc gs hk0 hk1 hv0 hv1 lnc rsc")
        dveP = Steps(sem("dveP"), "kpa0 kpb0 kpc0 kpd0 kpl0 kpa1 kpb1 kpc1 kpd1 kpl1 "
                     "sq0 ss0 ms0 k00 k01 k02 k03 kT0 sq1 ss1 ms1 k10 k11 k12 k13 kT1 ga gb gt0 gt1 gt2 gt3 gt4 gt5 "
                     "kc sqc ssc msc kn0 kn1 kcT vc")
        peA = Steps(sem("peA"), "rms s0 t0 s1 o0 t1 o1")
        actA = Steps(sem("actA"), "sq ln rq e00 e01 e02 e03 e04 e05 pt0 pc0 e10 e11 e12 e13 e14 e15 sg av "
                     "pt1 pc1 gu cat")
        dveA = Steps(sem("dveA"), "ms a00 a01 a02 a03 m00 m01 m02 n0 r0x r0 c0 p00 p01 p02 pt0 pd0 "
                     "a10 a11 a12 a13 m10 m11 m12 n1 r1x r1 c1 p10 p11 p12 sz o0 pt1 pd1 o1 cat")
        poolA = Steps(sem("poolA"), "b0 b1")
        peG = Steps(sem("peG"), "g0 g1 g2 g3")
        actG = Steps(sem("actG"), "ln rs sg0 sg1 c1 sg2 c2 sg3 c3 c4")
        dveG = Steps(sem("dveG"), "st0 st1 st2 st3 ag0 ag1 ms v0 v1 v2 v3 v4 v5 "
                     "z0 z1 u0 w0 l0 z2 u1 w1 l1 z3 u2 w2 l2 u3 w3 l3 acc")
        actO = Steps(sem("actO"), "sqa sqb")
        dveO = Steps(sem("dveO"), "xa aa xb ab")
        peR, actR, dveR = Steps(sem("peR"), "ss"), Steps(sem("actR"), "ln rs"), Steps(sem("dveR"), "ms at0")
        peH = Steps(sem("peH"), "gT G ksT at kv o ss")
        actH = Steps(sem("actH"), "sf g gn e2 e1 e3 e4 kn sq ln rs sg cat")
        dveH = Steps(sem("dveH"), "f0 f1 k gs d1 d2 kt qe at s10 s11 s20 s21 s30 s31 ms o1 o2 lo")
        poolH = Steps(sem("poolH"), "ks qi zs")
        poolR = Steps(sem("poolR"), "ra rb")

        block = ctx.enter_context(nc.Block())

        V_N0, V_N1, V_LB, V_B1, V_QG, V_KG, V_OG = 0, 16, 32, 64, 68, 69, 72
        NV = 73
        SSX, RSX, KGQ, LB, OMLB, LBT = 0, 2, 4, 8, 24, 40
        KSS, KRS, GSUM, GTAB, RSSQ, MX, NM, SUMS, COEF = 136, 140, 0, 144, 200, 204, 210, 216, 222
        BST, BAG = 228, 252

        REGIONS = [(0, 128), (128, 256), (256, 512), (512, 768), (768, 783), (783, 798)]

        ltmp = [small[:, LBT + 16 * n:LBT + 16 * n + 16] for n in range(6)]

        def src(w, col, q, swap=False):
            q = (q + 2) % NQ if swap else q
            return w[q * KQ * P:(q + 1) * KQ * P, bass.ds(col, SW)].rearrange("(k p) n -> p k n", p=P)

        @block.sync
        def _(sp):
            def load(s, part, first=False, static=True):
                for q in range(NQ):
                    if not first:
                        sp.wait_ge(lo_done, 4 * (s - 1) + q + 1)
                        if not static:
                            sp.sem_inc(seen, 1)
                    sp.dma_start(raw[:, q], part(q)).then_inc(landed[q], 16)

            for n, g in enumerate((0, 1, 2, 3, 4, 5)):
                load(n, lambda q, g=g: src(even_w_in, KV0 + SW * (0, 1, 2, 3, 4, 5)[g], q), first=n == 0)
            for i in range(2):
                for half in range(2):
                    load(6 + 2 * i + half, lambda q, i=i, half=half: cmp_w1[
                        i, (half * 16 + q * KQ) * P:(half * 16 + (q + 1) * KQ) * P, :]
                        .rearrange("(k p) n -> p k n", p=P))
            with sp.Fori(0, 4) as p:
                for j, base in enumerate((3 * A_WIDTH, 3 * A_WIDTH + B_WIDTH, A_WIDTH, 0)):
                    load(p * 4 + (S_ATT + j), lambda q, base=base: src(even_w_in, p * SW + base, q),
                         static=False)
            for j in range(4):
                load(S_SGU + j, lambda q, j=j: src(even_w_in, 2 * A_WIDTH + SW * j, q))
            with sp.Fori(0, 4) as p:
                for j in range(2):
                    load(p * 2 + (S_OUT0 + j), lambda q, j=j: src(even_w_out, p * (2 * SW) + j * SW, q, True),
                         static=False)
            with sp.Fori(0, 8) as p:
                for j, base in enumerate((D, 0, 2 * D, 3 * D)):
                    load(p * 4 + (S_HGRN + j), lambda q, base=base: src(odd_w_in, p * SW + base, q),
                         static=False)

            def store(n, j):
                sp.wait_ge(strip_out, n * 2 + (S_OUT1 + j + 1))
                sp.sem_inc(seen, 1)
                sp.dma_start(out[:, bass.ds(n * (2 * SW) + j * SW, SW)].rearrange("(a p) n -> p a n", p=P),
                             Z[:, j]).then_inc(y_out[j], 16)

            for j in range(2):
                load(S_OUT1 + j, lambda q, j=j: src(odd_w_out, j * SW, q))
            with sp.Fori(0, 3) as p:
                for j in range(2):
                    load(p * 2 + (S_OUT1 + 2 + j), lambda q, j=j: src(odd_w_out, p * (2 * SW) + (2 + j) * SW, q),
                         static=False)
                for j in range(2):
                    store(p, j)
            for j in range(2):
                store(3, j)
            for j in range(2):
                sp.wait_ge(y_out[j], 16 * 4)

        @block.gpsimd
        def _(pool):
            pool.memset(ident[:], 0.0).then_inc(pool0.sem, pool0.did("ms"))
            pool.wait_ge(pool0.sem, pool0.at("ms"))
            pool.affine_select(out=ident[:], in_=ident[:], compare_op=ALU.not_equal, fill=1.0, base=0,
                               pattern=[[-1, P]], channel_multiplier=1).then_inc(pool0.sem, pool0.did("ident"))
            pool.memset(ones[:], 1.0).then_inc(pool0.sem, pool0.did("ms1"))
            pool.wait_ge(pool0.sem, pool0.at("ms1"))
            pool.affine_select(out=tri64[:], in_=ones[:], compare_op=ALU.is_ge, fill=0.0, base=0,
                               pattern=[[1, P]], channel_multiplier=-1).then_inc(pool0.sem, pool0.did("triF"))
            pool.wait_ge(pool0.sem, pool0.at("triF"))
            pool.tensor_copy(tri_i[:], tri64[:]).then_inc(pool0.sem, pool0.did("tri64a"))
            pool.wait_ge(pool0.sem, pool0.at("tri64a"))
            pool.memset(tri64[0:CH, CH:P], 0.0).then_inc(pool0.sem, pool0.did("tri64"))
            pool.wait_ge(pool0.sem, pool0.at("tri64"))
            pool.tensor_copy(tri64_i[:], tri64[:]).then_inc(pool0.sem, pool0.did("tri64i"))
            pool.memset(vecs[:], 0.0).then_inc(pool0.sem, pool0.did("trii"))
            pool.wait_ge(pool0.sem, pool0.at("trii"))
            for row, a in ((V_N0, even_norm.rearrange("a (k p) -> (a k) p", p=P)),
                           (V_N1, odd_norm.rearrange("a (k p) -> (a k) p", p=P)),
                           (V_LB, hgrn_lb.rearrange("a (k p) -> (a k) p", p=P)),
                           (V_B1, cmp_b1.rearrange("a (k p) -> (a k) p", p=P)),
                           (V_QG, q_gain), (V_KG, k_gain), (V_OG, out_gain)):
                pool.dma_start(vecs[row:row + a.shape[0], :], a).then_inc(vec_in, 16)
            pool.dma_start(posr[:], cmp_pos.rearrange("a l d -> (a l) d")).then_inc(vec_in, 16)
            pool.wait_ge(xlo_done, 4)
            pool.dma_start(sgw, sgu_w.rearrange("g t s -> t g s")).then_inc(sg_in, 16)
            pool.dma_start(sgub[:], sgu_b.rearrange("(a g) t -> a (g t)", a=1)).then_inc(misc_in, 16)
            pool.dma_start(w2[:], cmp_w2.rearrange("i (a p) n -> p i a n", p=P)).then_inc(misc_in, 16)
            for n, v in enumerate((sgu_ln_g, sgu_ln_b)):
                pool.dma_start(lngb[:, n, :], v.partition_broadcast(P)).then_inc(misc_in, 16)
            di = scr[:, 0:414].bitcast(I32)
            parts = (("0", 0, P, -1, 0), ("1", P, T, -1, P), ("c0", 3 * P, NC, -16, 1 - NL),
                     ("c1", 3 * P + NC, NC, -16, P + 1 - NL))
            for n, (name, at, w, step, base) in enumerate(parts):
                pool.iota(di[:, at:at + w], pattern=[[step, w]], base=base, channel_multiplier=1)\
                    .then_inc(pool0.sem, pool0.did("i" + (name if name[0] == "c" else "d" + name)))
            pool.wait_ge(pool0.sem, pool0.at("ic1"))
            pool.tensor_copy(dist, di).then_inc(pool0.sem, pool0.did("df"))
            pool.wait_ge(pool0.sem, pool0.at("df"))
            for name, at, w, step, base in parts:
                pool.affine_select(out=dist[:, at:at + w], in_=dist[:, at:at + w], compare_op=ALU.is_ge, fill=BIG,
                                   base=base, pattern=[[step, w]], channel_multiplier=1)\
                    .then_inc(pool0.sem, pool0.did("sel" + name))
            pool.memset(w_sT[:], 0.0).then_inc(pool0.sem, pool0.did("zw"))
            pool.wait_ge(pool0.sem, pool0.at("selc1"))
            for a in range(2):
                pool.tensor_scalar(bias[:, a, :], dist, -0.5 ** (a + 1), None, ALU.mult)\
                    .then_inc(poolA.sem, poolA.did(f"b{a}"))
            pool.wait_ge(poolA.sem, poolA.at("b1"))
            with pool.Fori(0, 4) as p:
                for a in range(2):
                    pool.wait_ge(dveA.sem, dveA.at(f"a{a}3", p))
                    pool.sem_inc(seen, 1)
                    pool.tensor_scalar(bias[:, a, :], bias[:, a, :], 0.25, None, ALU.mult)\
                        .then_inc(poolA.sem, poolA.did(f"b{a}"))
            with pool.Fori(0, 8) as i:
                pool.wait_ge(actH.sem, actH.at("e4", i))
                pool.tensor_tensor(hKS, hK, hD2, ALU.mult).then_inc(poolH.sem, poolH.did("ks"))
                pool.wait_ge(strip_out, i * 4 + (S_HGRN + 2))
                pool.tensor_tensor(hQI, Z[:, 1].rearrange("p a n -> p (a n)"), hE3, ALU.mult)\
                    .then_inc(poolH.sem, poolH.did("qi"))
                pool.wait_ge(actH.sem, actH.at("sg", i))
                pool.tensor_tensor(hZS, Z[:, 3].rearrange("p a n -> p (a n)"), hSG, ALU.mult)\
                    .then_inc(poolH.sem, poolH.did("zs"))
            pool.wait_ge(actH.sem, actH.at("g", 7))
            pool.wait_ge(dveH.sem, dveH.at("kt", 7))
            with pool.Fori(0, 4) as p:
                for j in range(2):
                    pool.wait_ge(pe_q, p * 8 + 4 * (S_OUT1 + j - 1))
                    pool.tensor_copy(xres[:, j], xT[:, bass.ds(p * 4 + 2 * j, 2), :])\
                        .then_inc(poolR.sem, poolR.did("ra" if j == 0 else "rb"))

        def kv_at(h, c):
            return px[:, 1, h * HD:(h + 1) * HD] if c == 1 else px[:, 0, (2 * h + c // 2) * HD:(2 * h + c // 2 + 1) * HD]

        def cast(act, s, qs, first=False):
            for q in qs:
                act.wait_ge(landed[q], s * 16 + 16)
                if not first:
                    act.wait_ge(pe_q, s * 4 + (q - 3))
                act.activation(whl[:, q, :, 0, :], raw[:, q], ACT.Copy).then_inc(hi_done, 1)

        def take_lo(act, s, par, n=1, cols=slice(256, 512), first=False):
            act.wait_ge(pe_q, s * 4 + 4)
            if not first:
                act.wait_ge(strip_out, s - 1)
            w = cols.stop - cols.start
            act.activation(tmp[:, par, :, 0:w], pp[:, 2 * par:2 * par + 2, cols], ACT.Copy).then_inc(lo_out, n)

        @block.scalar
        def _(act):
            for a in range(TT):
                act.dma_start(xnat[:, a, :], x[0, a * P:(a + 1) * P, :]).then_inc(x_in, 16)
            act.dma_start(wg[:], even_w_in[:, GATE0:GATE0 + NG].rearrange("(k p) n -> p k n", p=P)).then_inc(x_in, 16)
            act.wait_ge(x_in, 48)
            for a in range(TT):
                act.activation(cathl[:, 4 * a:4 * a + 4].rearrange("p k a n -> p (k a n)"), xnat[:, a, :], ACT.Square,
                               accum_out=small[:, SSX + a:SSX + a + 1]).then_inc(act0.sem, act0.did(f"ss{a}"))
            for b in range(0, 8, 2):
                act.wait_ge(pe0.sem, pe0.at(f"xT{b}"))
                act.activation(xT[:, 2 * b:2 * b + 2, :], (pp if b < 4 else px)[:, b % 4, :]
                               .rearrange("p (a n) -> p a n", a=2), ACT.Copy).then_inc(act0.sem, act0.did(f"xT{b}"))
            act.wait_ge(dve0.sem, dve0.at("ms"))
            act.preload_act_table_set(LN_EXP)
            act.activation(small[:, RSX:RSX + 2], small[:, SSX:SSX + 2], ACT.Ln).then_inc(act0.sem, act0.did("ln"))
            act.wait_ge(act0.sem, act0.at("ln"))
            act.activation(small[:, RSX:RSX + 2], small[:, RSX:RSX + 2], ACT.Exp, scale=-0.5)\
                .then_inc(act0.sem, act0.did("rs"))
            def xhi(layer, xn):
                for c in range(4):
                    act.wait_ge(xn_done, 16 * layer + 4 * c + 4)
                    act.activation(xhl[:, KQ * c:KQ * c + KQ, 0, :], xn[:, c % 2], ACT.Copy).then_inc(xhi_done, 1)

            xhi(0, xn)
            cast(act, S_PRE, range(NQ), first=True)
            act.activation(wghl[:, :, 0, :], wg[:], ACT.Copy).then_inc(act0.sem, act0.did("wg"))
            for n in range(2):
                act.wait_ge(dve0.sem, dve0.at("lba" if n == 0 else "lbb"))
                act.activation(ltmp[1 + n], ltmp[1 + n], ACT.Exp).then_inc(act0.sem, act0.did(f"lbe{n}"))

            def rstd(steps, names, dve, dname, ap, scale=-0.5, i=0):
                act.wait_ge(dve.sem, dve.at(dname, i))
                act.activation(ap, ap, ACT.Ln).then_inc(steps.sem, steps.did(names[0]))
                act.wait_ge(steps.sem, steps.at(names[0], i))
                act.activation(ap, ap, ACT.Exp, scale=scale).then_inc(steps.sem, steps.did(names[1]))

            kph = [cathl[:, 4 * i:4 * i + 4].rearrange("p k a n -> p (k a n)")[:, 0:NL * 2 * CW]
                   .rearrange("p (l a n) -> p l a n", l=NL, a=2) for i in range(2)]
            for s in range(S_PRE, S_ATT):
                cast(act, s + 1, range(NQ))
                if s in (6, 8):
                    continue
                take_lo(act, s, s % 2 if s < 6 else 0, n=1 if s < 6 else 2,
                        cols=slice(256, 512) if s < 6 else slice(CW, 2 * CW), first=s < 2)
                if s in (0, 1):
                    act.wait_ge(dveP.sem, dveP.at(f"kpd{s}"))
                    act.activation(kph[s][:, :, 0, :], kpos.rearrange("p (l n) -> p l n", l=NL), ACT.Copy)\
                        .then_inc(actP.sem, actP.did(f"kp{s}"))
                if s in (2, 4):
                    n = (s - 2) // 2
                    rstd(actP, (f"ln{n}", f"rs{n}"), dveP, f"ms{n}", small[:, KRS:KRS + 4])
                if s == 5:
                    act.wait_ge(peP.sem, peP.at("gates"))
                    act.activation(scr[:, 0:48].rearrange("p (a n) -> p a n", a=2),
                                   px[:, 3, 0:128].rearrange("p (a n) -> p a n", a=2)[:, :, NG:2 * NG], ACT.Copy)\
                        .then_inc(actP.sem, actP.did("gc"))
                    act.wait_ge(dveP.sem, dveP.at("ga"))
                    act.activation(scr[:, 48:96], scr[:, 48:96], ACT.Sigmoid).then_inc(actP.sem, actP.did("gs"))
                if s in (7, 9):
                    i = (s - 7) // 2
                    act.wait_ge(strip_out, s + 1)
                    for g in range(2):
                        act.activation(scr[:, 128 + 64 * i + CW * g:128 + 64 * i + CW * g + CW], Z[:, i, g, 0:CW],
                                       ACT.Gelu_apprx_tanh, bias=vT[:, V_B1 + 2 * i + g:V_B1 + 2 * i + g + 1])\
                            .then_inc(actP.sem, actP.did(f"h{'kv'[i]}{g}"))
                    if i == 1:
                        rstd(actP, ("lnc", "rsc"), dveP, "msc", small[0:NC, KRS:KRS + 2])

            with act.Fori(0, 4) as p:
                s0 = p * 4 + S_ATT

                def exps(a):
                    act.wait_ge(dveA.sem, dveA.at(f"n{a}", p))
                    for r, (lo, hi) in enumerate(REGIONS):
                        act.activation(prob[:, lo:hi], prob[:, lo:hi], ACT.Exp, bias=small[:, NM + r:NM + r + 1],
                                       accum_out=small[:, SUMS + r:SUMS + r + 1])\
                            .then_inc(actA.sem, actA.did(f"e{a}{r}"))

                def take_pT(a):
                    act.wait_ge(peA.sem, peA.at(f"t{a}", p))
                    act.activation(probT[:, 0, 0:384], px[:, 2, 0:384], ACT.Copy)\
                        .then_inc(actA.sem, actA.did(f"pt{a}"))
                    act.activation(probT[0:NC, 0, 384:512], px[0:NC, 2, 384:512], ACT.Copy)\
                        .then_inc(actA.sem, actA.did(f"pc{a}"))

                cast(act, s0 + 1, (0, 1, 2))
                take_lo(act, s0, 0)
                cast(act, s0 + 1, (3,))
                act.wait_ge(strip_out, s0 + 1)
                act.activation(obuf[:], Z[:, 0], ACT.Square).then_inc(actA.sem, actA.did("sq"))
                cast(act, s0 + 2, (0, 1))
                act.preload_act_table_set(LN_EXP)
                rstd(actA, ("ln", "rq"), dveA, "ms", small[:, RSSQ:RSSQ + 4], i=p)
                cast(act, s0 + 2, (2,))
                exps(0)
                take_lo(act, s0 + 1, 1)
                cast(act, s0 + 2, (3,))
                cast(act, s0 + 3, (0, 1))
                take_pT(0)
                cast(act, s0 + 3, (2,))
                exps(1)
                take_lo(act, s0 + 2, 0)
                act.wait_ge(strip_out, s0 + 2)
                act.activation(sgz[:], Z[:, 1], ACT.Tanh, scale=0.5).then_inc(actA.sem, actA.did("sg"))
                cast(act, s0 + 3, (3,))
                act.wait_ge(strip_out, s0 + 3)
                act.activation(gav[:, :, bass.ds(p * SW, SW)], Z[:, 2], ACT.Gelu_apprx_tanh)\
                    .then_inc(actA.sem, actA.did("av"))
                cast(act, s0 + 4, (0, 1))
                take_pT(1)
                cast(act, s0 + 4, (2,))
                take_lo(act, s0 + 3, 1)
                cast(act, s0 + 4, (3,))
                act.wait_ge(strip_out, s0 + 4)
                act.activation(gu[:, bass.ds(p * 2, 2), :], Z[:, 3], ACT.Gelu_apprx_tanh)\
                    .then_inc(actA.sem, actA.did("gu"))
                act.wait_ge(dveA.sem, dveA.at("o1", p))
                act.activation(cathl[:, bass.ds(p * 2 + 8, 2), 0, :], obuf[:], ACT.Copy)\
                    .then_inc(actA.sem, actA.did("cat"))

            for j in range(4):
                s = S_SGU + j
                if j == 0:
                    rstd(actG, ("ln", "rs"), dveG, "ms", small[:, RSX:RSX + 2])
                cast(act, s + 1, (0, 1, 2))
                take_lo(act, s, j % 2)
                cast(act, s + 1, (3,))
                act.wait_ge(strip_out, s + 1)
                act.activation(sgz[:], Z[:, j], ACT.Sigmoid).then_inc(actG.sem, actG.did(f"sg{j}"))
                if j >= 1:
                    act.wait_ge(dveG.sem, dveG.at(f"w{j - 1}"))
                    act.activation(cathl[:, 2 * j - 2:2 * j, 0, :], obuf[:], ACT.Copy)\
                        .then_inc(actG.sem, actG.did(f"c{j}"))
            act.wait_ge(dveG.sem, dveG.at("w3"))
            act.activation(cathl[:, 6:8, 0, :], obuf[:], ACT.Copy).then_inc(actG.sem, actG.did("c4"))

            with act.Fori(0, 4) as p:
                for j in range(2):
                    s = p * 2 + (S_OUT0 + j)
                    cast(act, s + 1, (0, 1, 2))
                    take_lo(act, s, j)
                    cast(act, s + 1, (3,))
                    act.wait_ge(dveO.sem, dveO.at("xa" if j == 0 else "xb", p))
                    act.activation(sq, xT[:, bass.ds(p * 4 + 2 * j, 2), :], ACT.Square)\
                        .then_inc(actO.sem, actO.did("sqa" if j == 0 else "sqb"))
            rstd(actR, ("ln", "rs"), dveR, "ms", hRS[:, 0:T])
            xhi(1, xn1)

            cast(act, S_HGRN + 1, (0, 1))
            with act.Fori(0, 8) as i:
                s0 = i * 4 + S_HGRN
                cast(act, s0 + 1, (2,))
                take_lo(act, s0, 0)
                cast(act, s0 + 1, (3,))
                act.wait_ge(strip_out, s0 + 1)
                act.activation(hF, Z[:, 0].rearrange("p a n -> p (a n)"), ACT.Sigmoid).then_inc(actH.sem, actH.did("sf"))
                act.preload_act_table_set(LN_EXP)
                act.wait_ge(dveH.sem, dveH.at("f1", i))
                act.activation(hG, hF, ACT.Ln).then_inc(actH.sem, actH.did("g"))
                cast(act, s0 + 2, (0, 1))
                act.wait_ge(peH.sem, peH.at("gT", i))
                act.activation(hGN, px[:, 0, :], ACT.Copy).then_inc(actH.sem, actH.did("gn"))
                cast(act, s0 + 2, (2, 3))
                act.wait_ge(dveH.sem, dveH.at("d1", i))
                act.activation(hE2, hD1, ACT.Exp, scale=-1.0).then_inc(actH.sem, actH.did("e2"))
                act.wait_ge(actH.sem, actH.at("e2", i))
                act.activation(hD1, hD1, ACT.Exp).then_inc(actH.sem, actH.did("e1"))
                act.activation(hE3, hGS, ACT.Exp).then_inc(actH.sem, actH.did("e3"))
                act.wait_ge(dveH.sem, dveH.at("d2", i))
                act.activation(hD2, hD2, ACT.Exp).then_inc(actH.sem, actH.did("e4"))
                take_lo(act, s0 + 1, 1)
                cast(act, s0 + 3, (0, 1, 2))
                act.wait_ge(peH.sem, peH.at("ksT", i))
                act.activation(hKN, px[:, 3, :], ACT.Copy).then_inc(actH.sem, actH.did("kn"))
                cast(act, s0 + 3, (3,))
                take_lo(act, s0 + 2, 0)
                cast(act, s0 + 4, (0, 1, 2))
                act.wait_ge(peH.sem, peH.at("o", i))
                act.activation(hSQ, px[:, 2, :], ACT.Square).then_inc(actH.sem, actH.did("sq"))
                take_lo(act, s0 + 3, 1)
                cast(act, s0 + 4, (3,))
                rstd(actH, ("ln", "rs"), dveH, "ms", hRS, i=i)
                cast(act, s0 + 5, (0,))
                act.wait_ge(strip_out, s0 + 4)
                act.activation(hSG, Z[:, 3].rearrange("p a n -> p (a n)"), ACT.Sigmoid).then_inc(actH.sem, actH.did("sg"))
                cast(act, s0 + 5, (1,))
                act.wait_ge(dveH.sem, dveH.at("o2", i))
                act.activation(cathl[:, bass.ds(i * 2, 2), 0, :], hO.rearrange("p (a n) -> p a n", a=2), ACT.Copy)\
                    .then_inc(actH.sem, actH.did("cat"))

            def out1(p, j, last=False, first=False):
                s = p * 2 + (S_OUT1 + j)
                if not last:
                    cast(act, s + 1, (2,) if first else (0, 1, 2))
                take_lo(act, s, j)
                if not last:
                    cast(act, s + 1, (3,))

            for j in range(2):
                out1(0, j, first=j == 0)
            with act.Fori(1, 3) as p:
                for j in range(2):
                    out1(p, j)
            for j in range(2):
                out1(3, j, last=j == 1)

        def lows(dve, s, qs):
            for q in qs:
                dve.wait_ge(hi_done, s * 4 + (q + 1))
                dve.tensor_tensor(whl[:, q, :, 1, :], raw[:, q], whl[:, q, :, 0, :].bitcast(F32), ALU.subtract)\
                    .then_inc(lo_done, 1)

        def take(dve, s, par, dst, n=1, w=SW):
            dve.wait_ge(lo_out, s + 1)
            dve.tensor_tensor(dst, pp[:, 2 * par:2 * par + 2, 0:w], tmp[:, par, :, 0:w], ALU.add)\
                .then_inc(strip_out, n)

        @block.vector
        def _(dve):
            dve.wait_ge(act0.sem, act0.at("ss1"))
            dve.tensor_scalar(small[:, SSX:SSX + 2], small[:, SSX:SSX + 2], 1.0 / D, EPS, ALU.mult, ALU.add)\
                .then_inc(dve0.sem, dve0.did("ms"))
            for b in range(1, 8, 2):
                dve.wait_ge(pe0.sem, pe0.at(f"xT{b}"))
                dve.tensor_copy(xT[:, 2 * b:2 * b + 2, :], (pp if b < 4 else px)[:, b % 4, :]
                                .rearrange("p (a n) -> p a n", a=2)).then_inc(dve0.sem, dve0.did(f"xT{b}"))
            dve.wait_ge(pe0.sem, pe0.at("posT"))
            dve.tensor_copy(vT[:, 0:NV], pp[:, 0, 0:NV]).then_inc(dve0.sem, dve0.did("vT"))
            dve.tensor_copy(posT[:], pp[:, 0, 128:128 + 2 * NL]).then_inc(dve0.sem, dve0.did("posT"))
            dve.wait_ge(dve0.sem, dve0.at("vT"))
            dve.tensor_scalar(small[:, KGQ:KGQ + 3], vT[:, V_KG:V_KG + 3], vT[:, V_QG:V_QG + 1], None, ALU.mult)\
                .then_inc(dve0.sem, dve0.did("gain"))
            dve.wait_ge(act0.sem, act0.at("rs"))
            for a in range(TT):
                dve.tensor_scalar(tmp[:, 0, 0, a * P:(a + 1) * P], ident[:], small[:, RSX + a:RSX + a + 1], None,
                                  ALU.mult).then_inc(dve0.sem, dve0.did(f"diag{a}"))
            dve.wait_ge(pe0.sem, pe0.at("rs"))
            dve.tensor_copy(tmp[:, 1, 0, :], pp[:, 1, 0:T]).then_inc(dve0.sem, dve0.did("rsb"))
            dve.wait_ge(dve0.sem, dve0.at("rsb"))
            dve.wait_ge(act0.sem, act0.at("xT6"))

            def norm(layer, vcol, rsb, xn):
                for c in range(4):
                    if c >= 2:
                        dve.wait_ge(xlo_done, 4 * layer + c - 1)
                    for j in range(KQ):
                        k = KQ * c + j
                        dve.scalar_tensor_tensor(xn[:, c % 2, j, :], xT[:, k, :], vT[:, vcol + k:vcol + k + 1], rsb,
                                                 ALU.mult, ALU.mult).then_inc(xn_done, 1)
                    if c >= 1:
                        lo_part(layer, c - 1, xn)
                lo_part(layer, 3, xn)

            def lo_part(layer, c, xn):
                dve.wait_ge(xhi_done, 4 * layer + c + 1)
                dve.tensor_tensor(xhl[:, KQ * c:KQ * c + KQ, 1, :], xn[:, c % 2],
                                  xhl[:, KQ * c:KQ * c + KQ, 0, :].bitcast(F32), ALU.subtract).then_inc(xlo_done, 1)

            norm(0, V_N0, tmp[:, 1, 0, :], xn)
            lows(dve, S_PRE, range(NQ))
            dve.wait_ge(act0.sem, act0.at("wg"))
            dve.tensor_tensor(wghl[:, :, 1, :], wg[:], wghl[:, :, 0, :].bitcast(F32), ALU.subtract)\
                .then_inc(dve0.sem, dve0.did("wg"))
            la, lb = vT[:, V_LB:V_LB + 16], vT[:, V_LB + 16:V_LB + 32]

            def lbstep(name, o, a, b, op):
                dve.tensor_tensor(o, a, b, op).then_inc(dve0.sem, dve0.did(name))
                dve.wait_ge(dve0.sem, dve0.at(name))

            lbstep("lbm", ltmp[0], la, lb, ALU.max)
            lbstep("lba", ltmp[1], la, ltmp[0], ALU.subtract)
            lbstep("lbb", ltmp[2], lb, ltmp[0], ALU.subtract)
            dve.wait_ge(act0.sem, act0.at("lbe1"))
            lbstep("lbs", ltmp[3], ltmp[1], ltmp[2], ALU.add)
            dve.reciprocal(ltmp[3], ltmp[3]).then_inc(dve0.sem, dve0.did("lbr"))
            dve.wait_ge(dve0.sem, dve0.at("lbr"))
            lbstep("lbp0", ltmp[1], ltmp[1], ltmp[3], ALU.mult)
            lbstep("lbp1", ltmp[2], ltmp[2], ltmp[3], ALU.mult)
            lbstep("lbc", ltmp[4], ltmp[1], ltmp[2], ALU.add)
            lbstep("lb", small[:, LB:LB + 16], ltmp[4], ltmp[1], ALU.subtract)
            dve.tensor_scalar(small[:, OMLB:OMLB + 16], small[:, LB:LB + 16], -1.0, 1.0, ALU.mult, ALU.add)\
                .then_inc(dve0.sem, dve0.did("omlb"))
            dve.wait_ge(pool0.sem, pool0.at("zw"))
            for b in range(2):
                dve.wait_ge(pe0.sem, pe0.at(f"wsT{b}"))
                dve.copy_predicated(w_sT[:, 4 * b:4 * b + 4, :], tri_i[:].unsqueeze(1).broadcast_to([P, 4, P]),
                                    px[:, b, :].rearrange("p (a n) -> p a n", a=4))\
                    .then_inc(dve0.sem, dve0.did(f"wsT{b}"))

            def key_norm(n, kz, s):
                k4 = kz.rearrange("p a (h d) -> p (a h) d", h=2)
                sq4 = scr.rearrange("p (a d) -> p a d", a=4)
                dve.wait_ge(strip_out, s + 1)
                dve.wait_ge(pool0.sem, pool0.at("df"))
                dve.tensor_tensor(sq4, k4, k4, ALU.mult).then_inc(dveP.sem, dveP.did(f"sq{n}"))
                dve.wait_ge(dveP.sem, dveP.at(f"sq{n}"))
                dve.tensor_reduce(small[:, KSS:KSS + 4], sq4, AX.X, ALU.add).then_inc(dveP.sem, dveP.did(f"ss{n}"))
                dve.wait_ge(dveP.sem, dveP.at(f"ss{n}"))
                dve.tensor_scalar(small[:, KRS:KRS + 4], small[:, KSS:KSS + 4], 1.0 / HD, EPS, ALU.mult, ALU.add)\
                    .then_inc(dveP.sem, dveP.did(f"ms{n}"))
                dve.wait_ge(actP.sem, actP.at(f"rs{n}"))
                for m in range(4):
                    dve.tensor_scalar(k4[:, m, :], k4[:, m, :], small[:, KRS + m:KRS + m + 1], None, ALU.mult)\
                        .then_inc(dveP.sem, dveP.did(f"k{n}{m}"))
                dve.wait_ge(peP.sem, peP.at(f"kT{n}"))
                dve.tensor_scalar(keysT[:, :, n * T:(n + 1) * T], px[:, n, :].rearrange("p (h t) -> p h t", h=2),
                                  small[:, KGQ + 1 + n:KGQ + 2 + n], None, ALU.mult)\
                    .then_inc(dveP.sem, dveP.did(f"kT{n}"))

            kph = [cathl[:, 4 * i:4 * i + 4].rearrange("p k a n -> p (k a n)")[:, 0:NL * 2 * CW]
                   .rearrange("p (l a n) -> p l a n", l=NL, a=2) for i in range(2)]
            kpos4 = kpos.rearrange("p (a b h n) -> p a b h n", a=2, b=16, h=2)
            for s in range(S_PRE, S_ATT):
                lows(dve, s + 1, range(NQ))
                if s in (6, 8):
                    continue
                if s in (3, 5):
                    take(dve, s, s % 2, vals[:, (s - 3) // 2])
                elif s < 6:
                    take(dve, s, s % 2, Z[:, s % 4])
                else:
                    take(dve, s, 0, Z[:, (s - 7) // 2, :, 0:CW], n=2, w=CW)
                if s in (0, 1):
                    dve.wait_ge(strip_out, s + 1)
                    if s == 1:
                        dve.wait_ge(dveP.sem, dveP.at("kpl0"))
                        dve.wait_ge(actP.sem, actP.at("kp0"))
                    for n, (a, h) in enumerate(((0, 0), (0, 1), (1, 0), (1, 1))):
                        tok = Z[:, s, h, :].rearrange("p (m b) -> p b m", b=16)[:, :, a:a + NC]
                        pos = posT[:, s * NL + 16 * a:s * NL + 16 * a + 16].unsqueeze(2).broadcast_to([P, 16, NC])
                        dve.tensor_tensor(kpos4[:, a, :, h, :], tok, pos, ALU.add)\
                            .then_inc(dveP.sem, dveP.did(f"kp{'abcd'[n]}{s}"))
                    dve.wait_ge(actP.sem, actP.at(f"kp{s}"))
                    dve.tensor_tensor(kph[s][:, :, 1, :], kpos.rearrange("p (l n) -> p l n", l=NL),
                                      kph[s][:, :, 0, :].bitcast(F32), ALU.subtract)\
                        .then_inc(dveP.sem, dveP.did(f"kpl{s}"))
                if s in (2, 4):
                    key_norm((s - 2) // 2, Z[:, s % 4], s)
                if s == 5:
                    dve.wait_ge(actP.sem, actP.at("gc"))
                    dve.tensor_tensor(scr[:, 48:96].rearrange("p (a n) -> p a n", a=2),
                                      px[:, 3, 0:128].rearrange("p (a n) -> p a n", a=2)[:, :, 0:NG],
                                      scr[:, 0:48].rearrange("p (a n) -> p a n", a=2), ALU.add)\
                        .then_inc(dveP.sem, dveP.did("ga"))
                    dve.wait_ge(actP.sem, actP.at("gs"))
                    dve.tensor_copy(scr[:, 96:97], scr[:, 48:49]).then_inc(dveP.sem, dveP.did("gb"))
                    for r, (tile, br) in enumerate(((0, 1), (0, 2), (1, 1), (1, 2), (0, 0), (1, 0))):
                        dve.tensor_copy(small[:, GTAB:GTAB + 48].rearrange("p (h r) -> p h r", r=6)[:, :, r],
                                        scr[:, 48 + tile * NG + br * 8:48 + tile * NG + br * 8 + 8])\
                            .then_inc(dveP.sem, dveP.did(f"gt{r}"))
            kc = scr[0:NC, 256:512].rearrange("p (h d) -> p h d", h=2)
            kq = obuf[0:NC]
            dve.wait_ge(peP.sem, peP.at("ck1"))
            dve.tensor_copy(kc, px[0:NC, 2, 0:2 * HD].rearrange("p (h d) -> p h d", h=2))\
                .then_inc(dveP.sem, dveP.did("kc"))
            dve.wait_ge(dveP.sem, dveP.at("kc"))
            ksq = Z[0:NC, 2, :, 0:HD]
            dve.tensor_tensor(ksq, kc, kc, ALU.mult).then_inc(dveP.sem, dveP.did("sqc"))
            dve.wait_ge(dveP.sem, dveP.at("sqc"))
            dve.tensor_reduce(small[0:NC, KSS:KSS + 2], ksq, AX.X, ALU.add).then_inc(dveP.sem, dveP.did("ssc"))
            dve.wait_ge(dveP.sem, dveP.at("ssc"))
            dve.tensor_scalar(small[0:NC, KRS:KRS + 2], small[0:NC, KSS:KSS + 2], 1.0 / HD, EPS, ALU.mult, ALU.add)\
                .then_inc(dveP.sem, dveP.did("msc"))
            dve.wait_ge(actP.sem, actP.at("rsc"))
            for h in range(2):
                dve.tensor_scalar(kc[:, h, :], kc[:, h, :], small[0:NC, KRS + h:KRS + h + 1], None, ALU.mult)\
                    .then_inc(dveP.sem, dveP.did(f"kn{h}"))
            dve.wait_ge(peP.sem, peP.at("kcT"))
            dve.tensor_scalar(keysT[:, :, 2 * T:2 * T + NC], px[:, 1, 0:2 * 16].rearrange("p (h n) -> p h n", h=2)
                              [:, :, 0:NC], small[:, KGQ:KGQ + 1], None, ALU.mult)\
                .then_inc(dveP.sem, dveP.did("kcT"))
            dve.tensor_copy(vcmp[0:NC], px[0:NC, 3, 0:2 * HD].rearrange("p (h d) -> p h d", h=2))\
                .then_inc(dveP.sem, dveP.did("vc"))

            with dve.Fori(0, 4) as p:
                s0 = p * 4 + S_ATT

                def scores(a):
                    dve.wait_ge(peA.sem, peA.at(f"s{a}", p))
                    dve.wait_ge(actA.sem, actA.at("rq", p))
                    dve.wait_ge(poolA.sem, poolA.at(f"b{a}", p))
                    if a == 1:
                        dve.wait_ge(peA.sem, peA.at("t0", p))
                    for n, (lo, hi, tile, ps, bl, bh) in enumerate((
                            (0, 256, 0, px[:, 0, 0:256], 0, 128), (256, 768, 1, px[:, 1, 0:512], 128, 384),
                            (768, 783, 0, px[:, 0, 256:271], 384, 399), (783, 798, 1, px[:, 0, 271:286], 399, 414))):
                        r = 2 if n < 2 else 1
                        w = bh - bl
                        dve.scalar_tensor_tensor(
                            prob[:, lo:hi].rearrange("p (r n) -> p r n", r=r), ps.rearrange("p (r n) -> p r n", r=r),
                            small[:, RSSQ + 2 * a + tile:RSSQ + 2 * a + tile + 1],
                            bias[:, a, bl:bh].unsqueeze(1).broadcast_to([P, r, w]), ALU.mult, ALU.add)\
                            .then_inc(dveA.sem, dveA.did(f"a{a}{n}"))
                    dve.wait_ge(dveA.sem, dveA.at(f"a{a}3", p))
                    for n, (lo, hi) in enumerate(((0, 256), (256, 768), (768, 798))):
                        dve.tensor_reduce(small[:, MX + 2 * n:MX + 2 * n + 2],
                                          prob[:, lo:hi].rearrange("p (r n) -> p r n", r=2), AX.X, ALU.max)\
                            .then_inc(dveA.sem, dveA.did(f"m{a}{n}"))
                    dve.wait_ge(dveA.sem, dveA.at(f"m{a}2", p))
                    dve.tensor_scalar(small[:, NM:NM + 6], small[:, MX:MX + 6], -1.0, 1e20, ALU.mult, ALU.min)\
                        .then_inc(dveA.sem, dveA.did(f"n{a}"))

                def weigh(a):
                    dve.wait_ge(actA.sem, actA.at(f"e{a}5", p))
                    dve.tensor_scalar(small[:, SUMS:SUMS + 6], small[:, SUMS:SUMS + 6], 1e-30, None, ALU.max)\
                        .then_inc(dveA.sem, dveA.did(f"r{a}x"))
                    dve.wait_ge(dveA.sem, dveA.at(f"r{a}x", p))
                    dve.reciprocal(small[:, SUMS:SUMS + 6], small[:, SUMS:SUMS + 6])\
                        .then_inc(dveA.sem, dveA.did(f"r{a}"))
                    dve.wait_ge(dveA.sem, dveA.at(f"r{a}", p))
                    dve.tensor_tensor(small[:, COEF:COEF + 6], small[:, SUMS:SUMS + 6],
                                      small[:, bass.ds(p * 12 + (GTAB + 6 * a), 6)], ALU.mult)\
                        .then_inc(dveA.sem, dveA.did(f"c{a}"))
                    dve.wait_ge(dveA.sem, dveA.at(f"c{a}", p))
                    for n, (lo, hi) in enumerate(((0, 256), (256, 768), (768, 798))):
                        w = (hi - lo) // 2
                        v = prob[:, lo:hi].rearrange("p (r n) -> p r n", r=2)
                        dve.tensor_tensor(v, v, small[:, COEF + 2 * n:COEF + 2 * n + 2].unsqueeze(2)
                                          .broadcast_to([P, 2, w]), ALU.mult)\
                            .then_inc(dveA.sem, dveA.did(f"p{a}{n}"))

                def take_pT(a):
                    dve.wait_ge(peA.sem, peA.at(f"t{a}", p))
                    dve.tensor_copy(probT[:, 1, 0:384], px[:, 3, 0:384]).then_inc(dveA.sem, dveA.did(f"pt{a}"))
                    dve.tensor_copy(probT[0:NC, 1, 384:512], px[0:NC, 3, 384:512])\
                        .then_inc(dveA.sem, dveA.did(f"pd{a}"))

                def gate(a):
                    dve.wait_ge(peA.sem, peA.at(f"o{a}", p))
                    dve.wait_ge(dveA.sem, dveA.at("sz", p))
                    dve.scalar_tensor_tensor(obuf[:, a, :], px[:, 2, 0:T], 0.5, sgz[:, a, :], ALU.mult, ALU.mult)\
                        .then_inc(dveA.sem, dveA.did(f"o{a}"))

                lows(dve, s0 + 1, (0, 1, 2))
                take(dve, s0, 0, Z[:, 0])
                lows(dve, s0 + 1, (3,))
                lows(dve, s0 + 2, (0,))
                dve.wait_ge(peA.sem, peA.at("rms", p))
                dve.tensor_scalar(small[:, RSSQ:RSSQ + 4], px[:, 3, 0:4], 1.0, EPS * HD, ALU.mult, ALU.add)\
                    .then_inc(dveA.sem, dveA.did("ms"))
                lows(dve, s0 + 2, (1,))
                scores(0)
                lows(dve, s0 + 2, (2,))
                weigh(0)
                take(dve, s0 + 1, 1, Z[:, 1])
                lows(dve, s0 + 2, (3,))
                lows(dve, s0 + 3, (0, 1))
                take_pT(0)
                scores(1)
                lows(dve, s0 + 3, (2,))
                weigh(1)
                take(dve, s0 + 2, 0, Z[:, 2])
                dve.wait_ge(actA.sem, actA.at("sg", p))
                dve.scalar_tensor_tensor(sgz[:], sgz[:], 1.0, Z[:, 1], ALU.add, ALU.mult)\
                    .then_inc(dveA.sem, dveA.did("sz"))
                gate(0)
                lows(dve, s0 + 3, (3,))
                lows(dve, s0 + 4, (0, 1))
                take_pT(1)
                lows(dve, s0 + 4, (2,))
                take(dve, s0 + 3, 1, Z[:, 3])
                lows(dve, s0 + 4, (3,))
                gate(1)
                dve.wait_ge(actA.sem, actA.at("cat", p))
                dve.tensor_tensor(cathl[:, bass.ds(p * 2 + 8, 2), 1, :], obuf[:],
                                  cathl[:, bass.ds(p * 2 + 8, 2), 0, :].bitcast(F32), ALU.subtract)\
                    .then_inc(dveA.sem, dveA.did("cat"))

            dve.wait_ge(actA.sem, actA.at("cat", 3))
            st = small[:, BST:BST + 24].rearrange("p (a b c) -> p a b c", a=2, b=2)
            for a in range(TT):
                for b in range(2):
                    dve.bn_stats(st[:, a, b, :], gav[:, a, 512 * b:512 * b + 512])\
                        .then_inc(dveG.sem, dveG.did(f"st{2 * a + b}"))
            dve.wait_ge(dveG.sem, dveG.at("st3"))
            mv = small[:, KSS:KSS + 4].rearrange("p (a n) -> p a n", a=2)
            for a in range(TT):
                dve.bn_aggr(mv[:, a, :], st[:, a].rearrange("p b c -> p (b c)")).then_inc(dveG.sem, dveG.did(f"ag{a}"))
            dve.wait_ge(dveG.sem, dveG.at("ag1"))
            dve.tensor_scalar(small[:, RSX:RSX + 2], mv[:, :, 1], EPS, None, ALU.add)\
                .then_inc(dveG.sem, dveG.did("ms"))
            def gain_or_bias(n):
                for a in range(TT):
                    dve.wait_ge(dveG.sem, dveG.at(f"v{2 * n + a}"))
                    dve.tensor_tensor(gav[:, a, :], gav[:, a, :], lngb[:, n, :], (ALU.mult, ALU.add)[n])\
                        .then_inc(dveG.sem, dveG.did(f"v{2 * n + 2 + a}"))

            def spatial(j):
                dve.wait_ge(peG.sem, peG.at(f"g{j}"))
                if j >= 1:
                    dve.wait_ge(dveG.sem, dveG.at(f"l{j - 1}"))
                dve.tensor_tensor(obuf[:], px[:, j, :].rearrange("p (a n) -> p a n", a=2), gu[:, 2 * j:2 * j + 2, :],
                                  ALU.mult).then_inc(dveG.sem, dveG.did(f"u{j}"))
                dve.wait_ge(dveG.sem, dveG.at(f"u{j}"))
                dve.tensor_tensor(obuf[:], obuf[:], Z[:, j], ALU.mult).then_inc(dveG.sem, dveG.did(f"w{j}"))
                dve.wait_ge(actG.sem, actG.at(f"c{j + 1}"))
                dve.tensor_tensor(cathl[:, 2 * j:2 * j + 2, 1, :], obuf[:],
                                  cathl[:, 2 * j:2 * j + 2, 0, :].bitcast(F32), ALU.subtract)\
                    .then_inc(dveG.sem, dveG.did(f"l{j}"))

            lows(dve, S_SGU + 1, (0,))
            dve.wait_ge(actG.sem, actG.at("rs"))
            dve.wait_ge(misc_in, 64)
            for a in range(TT):
                dve.tensor_scalar(gav[:, a, :], gav[:, a, :], mv[:, a, 0:1], small[:, RSX + a:RSX + a + 1],
                                  ALU.subtract, ALU.mult).then_inc(dveG.sem, dveG.did(f"v{a}"))
            lows(dve, S_SGU + 1, (1,))
            gain_or_bias(0)
            lows(dve, S_SGU + 1, (2,))
            for j in range(4):
                s = S_SGU + j
                if j >= 1:
                    lows(dve, s + 1, (0, 1, 2))
                take(dve, s, j % 2, Z[:, j])
                lows(dve, s + 1, (3,))
                if j == 0:
                    gain_or_bias(1)
                dve.wait_ge(actG.sem, actG.at(f"sg{j}"))
                dve.tensor_tensor(Z[:, j], Z[:, j], sgz[:], ALU.mult).then_inc(dveG.sem, dveG.did(f"z{j}"))
                dve.wait_ge(dveG.sem, dveG.at(f"z{j}"))
                if j >= 1:
                    spatial(j - 1)
            spatial(3)

            dve.memset(acc, 0.0).then_inc(dveG.sem, dveG.did("acc"))
            dve.wait_ge(dveG.sem, dveG.at("acc"))
            with dve.Fori(0, 4) as p:
                for j in range(2):
                    s = p * 2 + (S_OUT0 + j)
                    lows(dve, s + 1, (0, 1, 2))
                    take(dve, s, j, Z[:, j])
                    lows(dve, s + 1, (3,))
                    dve.wait_ge(strip_out, s + 1)
                    r = xT[:, bass.ds(p * 4 + 2 * j, 2), :]
                    dve.tensor_tensor(r, r, Z[:, j], ALU.add).then_inc(dveO.sem, dveO.did("xa" if j == 0 else "xb"))
                    dve.wait_ge(actO.sem, actO.at("sqa" if j == 0 else "sqb", p))
                    dve.tensor_tensor(acc, acc, sq, ALU.add).then_inc(dveO.sem, dveO.did("aa" if j == 0 else "ab"))
            dve.wait_ge(peR.sem, peR.at("ss"))
            dve.tensor_scalar(hRS[:, 0:T], px[:, 0, 0:T], 1.0 / D, EPS, ALU.mult, ALU.add)\
                .then_inc(dveR.sem, dveR.did("ms"))
            dve.wait_ge(actR.sem, actR.at("rs"))
            norm(1, V_N1, hRS[:, 0:T], xn1)
            dve.memset(hAT, 0.0).then_inc(dveR.sem, dveR.did("at0"))
            dve.wait_ge(dveR.sem, dveR.at("at0"))

            def chunks(ap):
                return ap.rearrange("p (c t) -> p c t", t=CH)

            lows(dve, S_HGRN + 1, (0, 1))
            with dve.Fori(0, 8) as i:
                s0 = i * 4 + S_HGRN
                lows(dve, s0 + 1, (2,))
                take(dve, s0, 0, Z[:, 0])
                lows(dve, s0 + 1, (3,))
                dve.wait_ge(actH.sem, actH.at("sf", i))
                for h in range(2):
                    dve.tensor_scalar(hF[:, h * T:(h + 1) * T], hF[:, h * T:(h + 1) * T],
                                      small[:, bass.ds(i * 2 + (OMLB + h), 1)], small[:, bass.ds(i * 2 + (LB + h), 1)],
                                      ALU.mult, ALU.add).then_inc(dveH.sem, dveH.did(f"f{h}"))
                dve.wait_ge(dveH.sem, dveH.at("f1", i))
                dve.tensor_scalar(hK, hF, -1.0, 1.0, ALU.mult, ALU.add).then_inc(dveH.sem, dveH.did("k"))
                lows(dve, s0 + 2, (0, 1, 2))
                dve.wait_ge(peH.sem, peH.at("G", i))
                dve.tensor_copy(hGS, px[:, 1, :]).then_inc(dveH.sem, dveH.did("gs"))
                dve.wait_ge(dveH.sem, dveH.at("gs", i))
                dve.tensor_tensor(chunks(hD1), chunks(hGS), chunks(hGS)[:, :, CH // 2 - 1:CH // 2]
                                  .broadcast_to([P, 8, CH]), ALU.subtract).then_inc(dveH.sem, dveH.did("d1"))
                dve.tensor_tensor(chunks(hD2), chunks(hGS)[:, :, CH - 1:CH].broadcast_to([P, 8, CH]), chunks(hGS),
                                  ALU.subtract).then_inc(dveH.sem, dveH.did("d2"))
                lows(dve, s0 + 2, (3,))
                take(dve, s0 + 1, 1, Z[:, 1])
                dve.wait_ge(actH.sem, actH.at("e1", i))
                dve.tensor_tensor(hKE, hK, hE2, ALU.mult).then_inc(dveH.sem, dveH.did("kt"))
                dve.wait_ge(strip_out, s0 + 2)
                dve.tensor_tensor(hQE, Z[:, 1].rearrange("p a n -> p (a n)"), hD1, ALU.mult)\
                    .then_inc(dveH.sem, dveH.did("qe"))
                lows(dve, s0 + 3, (0, 1, 2))
                dve.wait_ge(peH.sem, peH.at("at", i))
                dve.sem_inc(seen, 1)
                dve.copy_predicated(hAT.rearrange("p (b t) -> p b t", b=4),
                                    tri64_i[:].unsqueeze(1).broadcast_to([P, 4, P]),
                                    px[:, 2, :].rearrange("p (b t) -> p b t", b=4))\
                    .then_inc(dveH.sem, dveH.did("at"))
                lows(dve, s0 + 3, (3,))
                take(dve, s0 + 2, 0, Z[:, 2])
                lows(dve, s0 + 4, (0,))
                dve.wait_ge(peH.sem, peH.at("kv", i))
                for h in range(2):
                    dve.tensor_copy(hST[:, h, 0, :], kv_at(h, 0)).then_inc(dveH.sem, dveH.did(f"s1{h}"))
                for c in range(1, 3):
                    for h in range(2):
                        dve.wait_ge(dveH.sem, dveH.at(f"s{c}{h}", i))
                        end = h * T + c * CH + CH - 1
                        dve.scalar_tensor_tensor(hST[:, h, c, :], hST[:, h, c - 1, :], hE3[:, end:end + 1],
                                                 kv_at(h, c), ALU.mult, ALU.add)\
                            .then_inc(dveH.sem, dveH.did(f"s{c + 1}{h}"))
                lows(dve, s0 + 4, (1, 2))
                take(dve, s0 + 3, 1, Z[:, 3])
                lows(dve, s0 + 4, (3,))
                dve.wait_ge(peH.sem, peH.at("ss", i))
                dve.tensor_scalar(hRS, px[:, 3, :], 1.0 / HD, EPS, ALU.mult, ALU.add)\
                    .then_inc(dveH.sem, dveH.did("ms"))
                lows(dve, s0 + 5, (0,))
                dve.wait_ge(actH.sem, actH.at("rs", i))
                dve.scalar_tensor_tensor(hO, px[:, 2, :], vT[:, V_OG:V_OG + 1], hRS, ALU.mult, ALU.mult)\
                    .then_inc(dveH.sem, dveH.did("o1"))
                lows(dve, s0 + 5, (1,))
                dve.wait_ge(dveH.sem, dveH.at("o1", i))
                dve.wait_ge(poolH.sem, poolH.at("zs", i))
                dve.tensor_tensor(hO, hO, hZS, ALU.mult).then_inc(dveH.sem, dveH.did("o2"))
                dve.wait_ge(actH.sem, actH.at("cat", i))
                dve.tensor_tensor(cathl[:, bass.ds(i * 2, 2), 1, :], hO.rearrange("p (a n) -> p a n", a=2),
                                  cathl[:, bass.ds(i * 2, 2), 0, :].bitcast(F32), ALU.subtract)\
                    .then_inc(dveH.sem, dveH.did("lo"))

            def out1(p, j, last=False, first=False):
                s = p * 2 + (S_OUT1 + j)
                if not last:
                    lows(dve, s + 1, (2,) if first else (0, 1, 2))
                if not (isinstance(p, int) and p == 0):
                    dve.wait_ge(y_out[j], p * 16)
                take(dve, s, j, Z[:, j])
                if not last:
                    lows(dve, s + 1, (3,))

            for j in range(2):
                out1(0, j, first=j == 0)
            with dve.Fori(1, 3) as p:
                for j in range(2):
                    out1(p, j)
            for j in range(2):
                out1(3, j, last=j == 1)

        @block.tensor
        def _(pe):
            def strip(s, par, kind, xs, order=None, first=False, hooks=None, late=None, rhs=None):
                if not first:
                    pe.wait_ge(strip_out, s - 1)
                for q in range(NQ):
                    pe.wait_ge(lo_done, s * 4 + (q + 1))
                    for g in range(2):
                        bank = pp[:, 2 * par + g, :]
                        for k in range(KQ):
                            kt = (order or (lambda n: n))(KQ * q + k)
                            begin, end = q == 0 and k == 0, q == NQ - 1 and k == KQ - 1
                            if kind == "B":
                                full = (bank, whl[:, q, k, 0, g * P:(g + 1) * P], xs[:, kt, :, :])
                                half = (bank[:, T:], whl[:, q, k, 1, g * P:(g + 1) * P], xs[:, kt, 0, :])
                            else:
                                full = (bank, xs[:, kt, 0, g * P:(g + 1) * P], whl[:, q, k, :, :])
                                half = (bank[:, T:], xs[:, kt, 1, g * P:(g + 1) * P], whl[:, q, k, 0, :])
                            if end:
                                pe.matmul(*half, start=False, stop=False)
                                mm = pe.matmul(*full, start=False, stop=True)
                            else:
                                pe.matmul(*full, start=begin, stop=False)
                                mm = pe.matmul(*half, start=False, stop=False)
                        if late and q == NQ - 2:
                            late(g)
                    mm.then_inc(pe_q, 1)
                    if hooks and q in hooks:
                        hooks[q]()

            pe.wait_ge(pool0.sem, pool0.at("ident"))
            pe.wait_ge(x_in, 48)
            for b in range(8):
                for k in range(2):
                    for a in range(TT):
                        kt = 2 * b + k
                        mm = pe.transpose((pp if b < 4 else px)[:, b % 4, k * T + a * P:k * T + (a + 1) * P],
                                          xnat[:, a, kt * P:(kt + 1) * P], ident[:])
                mm.then_inc(pe0.sem, pe0.did(f"xT{b}"))
            pe.wait_ge(act0.sem, act0.at("xT0"))
            pe.wait_ge(vec_in, 16 * 8)
            pe.transpose(pp[:, 0, 0:P], vecs[:], ident[:]).then_inc(pe0.sem, pe0.did("vT"))
            pe.transpose(pp[:, 0, P:P + 2 * NL], posr[:], ident[0:2 * NL, 0:2 * NL])\
                .then_inc(pe0.sem, pe0.did("posT"))
            pe.wait_ge(dve0.sem, dve0.at("diag1"))
            pe.wait_ge(pool0.sem, pool0.at("ms1"))
            pe.matmul(pp[:, 1, 0:T], ones[:], tmp[:, 0, 0, :], start=True, stop=True)\
                .then_inc(pe0.sem, pe0.did("rs"))
            pe.wait_ge(dve0.sem, dve0.at("rsb"))
            pe.wait_ge(act0.sem, act0.at("xT6"))
            pe.wait_ge(xlo_done, 4)

            def spatial_weights():
                pe.wait_ge(sg_in, 16)
                for b in range(2):
                    for g in range(4):
                        mm = pe.transpose(px[:, b, g * P:(g + 1) * P], sgw[:, 4 * b + g, :], ident[:])
                    mm.then_inc(pe0.sem, pe0.did(f"wsT{b}"))

            def key_T(n):
                pe.wait_ge(dve0.sem, dve0.at("wsT1"))
                pe.wait_ge(dveP.sem, dveP.at(f"k{n}3"))
                for a in range(TT):
                    for h in range(2):
                        mm = pe.transpose(px[:, n, h * T + a * P:h * T + (a + 1) * P],
                                          Z[:, (2 + 2 * n) % 4, a, h * HD:(h + 1) * HD], ident[:])
                mm.then_inc(peP.sem, peP.did(f"kT{n}"))

            def branch_gates():
                pe.wait_ge(dve0.sem, dve0.at("wg"))
                for a in range(TT):
                    o = px[:, 3, 64 * a:64 * a + 2 * NG]
                    for k in range(KT):
                        full = (o, xhl[:, k, 0, a * P:(a + 1) * P], wghl[:, k, :, :])
                        half = (o[:, NG:], xhl[:, k, 1, a * P:(a + 1) * P], wghl[:, k, 0, :])
                        if k == KT - 1:
                            pe.matmul(*half, start=False, stop=False)
                            mm = pe.matmul(*full, start=False, stop=True)
                        else:
                            pe.matmul(*full, start=k == 0, stop=False)
                            pe.matmul(*half, start=False, stop=False)
                mm.then_inc(peP.sem, peP.did("gates"))

            def compress_out(i):
                pe.wait_ge(actP.sem, actP.at(f"h{'kv'[i]}1"))
                pe.wait_ge(misc_in, 64)
                for h in range(2):
                    for g in range(2):
                        c = 128 + 64 * i + CW * g + NC * h
                        mm = pe.matmul(px[0:NC, 2 + i, h * HD:(h + 1) * HD], scr[:, c:c + NC], w2[:, i, g, :],
                                       start=g == 0, stop=g == 1)
                    mm.then_inc(peP.sem, peP.did(f"c{'kv'[i]}{h}"))

            strip(0, 0, "B", xhl, first=True, hooks={3: spatial_weights})
            strip(1, 1, "B", xhl, first=True)
            strip(2, 0, "A", xhl)
            strip(3, 1, "A", xhl, hooks={1: lambda: key_T(0)})
            strip(4, 0, "A", xhl, hooks={3: branch_gates})
            strip(5, 1, "A", xhl, hooks={1: lambda: key_T(1)})
            kph = [cathl[:, 4 * i:4 * i + 4].rearrange("p k a n -> p (k a n)")[:, 0:NL * 2 * CW]
                   .rearrange("p (l a n) -> p l a n", l=NL, a=2) for i in range(2)]
            for i in range(2):
                pe.wait_ge(dveP.sem, dveP.at(f"kpl{i}"))
                for half in range(2):
                    s = 6 + 2 * i + half
                    if half == 0:
                        pe.wait_ge(strip_out, s - 1 if i == 0 else s)
                    for q in range(NQ):
                        pe.wait_ge(lo_done, s * 4 + q + 1)
                        for g in range(2):
                            for k in range(KQ):
                                li = 16 * half + KQ * q + k
                                full = (pp[:, g, 0:2 * CW], whl[:, q, k, 0, g * P:(g + 1) * P], kph[i][:, li, :, :])
                                part = (pp[:, g, CW:2 * CW], whl[:, q, k, 1, g * P:(g + 1) * P], kph[i][:, li, 0, :])
                                if li == NL - 1:
                                    pe.matmul(*part, start=False, stop=False)
                                    mm = pe.matmul(*full, start=False, stop=True)
                                else:
                                    pe.matmul(*full, start=li == 0, stop=False)
                                    mm = pe.matmul(*part, start=False, stop=False)
                        mm.then_inc(pe_q, 1)
                if i == 1:
                    pe.wait_ge(dveP.sem, dveP.at("gt5"))
                    compress_out(0)
            compress_out(1)
            pe.wait_ge(dveP.sem, dveP.at("kn1"))
            for h in range(2):
                mm = pe.transpose(px[:, 1, 16 * h:16 * h + NC], scr[0:NC, 256 + h * HD:256 + (h + 1) * HD],
                                  ident[0:NC, 0:NC])
            mm.then_inc(peP.sem, peP.did("kcT"))
            pe.wait_ge(dveP.sem, dveP.at("vc"))

            for kv in range(2):
                with pe.Fori(0, 2) as r:
                    p = r + 2 * kv
                    s0 = p * 4 + S_ATT
                    kT = keysT[:, kv, :]

                    def rms():
                        pe.wait_ge(actA.sem, actA.at("sq", p))
                        for h in range(2):
                            for a in range(TT):
                                mm = pe.matmul(px[:, 3, 2 * h + a:2 * h + a + 1], obuf[:, h, a * P:(a + 1) * P],
                                               ones[:, 0:1], start=True, stop=True)
                        mm.then_inc(peA.sem, peA.did("rms"))

                    def score(h):
                        if h == 1:
                            pe.wait_ge(dveA.sem, dveA.at("a03", p))
                        q0, q1 = Z[:, 0, h, 0:P], Z[:, 0, h, P:T]
                        pe.matmul(px[:, 0, 0:T].rearrange("p (b n) -> p b n", b=2), q0,
                                  kT[:, 0:2 * T].rearrange("p (b n) -> p b n", b=2)[:, :, 0:P], start=True, stop=True)
                        pe.matmul(px[:, 1, 0:2 * T], q1, kT[:, 0:2 * T], start=True, stop=True)
                        pe.matmul(px[:, 0, T:T + NC], q0, kT[:, 2 * T:2 * T + NC], start=True, stop=True)
                        pe.matmul(px[:, 0, T + NC:T + 2 * NC], q1, kT[:, 2 * T:2 * T + NC], start=True, stop=True)\
                            .then_inc(peA.sem, peA.did(f"s{h}"))

                    def turn(h):
                        pe.wait_ge(dveA.sem, dveA.at(f"p{h}2", p))
                        if h == 1:
                            pe.wait_ge(dveA.sem, dveA.at("o0", p))
                        for b, (t0, tile1) in enumerate(((0, 256), (128, 512))):
                            for n, c in enumerate((t0, tile1, tile1 + P)):
                                pe.transpose(px[:, 2 + b, n * P:(n + 1) * P], prob[:, c:c + P], ident[:])
                        pe.transpose(px[0:NC, 2, 384:512], prob[:, 768:783], ident[:])
                        pe.transpose(px[0:NC, 3, 384:512], prob[:, 783:798], ident[:])\
                            .then_inc(peA.sem, peA.did(f"t{h}"))

                    def mix(h):
                        pe.wait_ge(actA.sem, actA.at(f"pc{h}", p))
                        pe.wait_ge(dveA.sem, dveA.at(f"pd{h}", p))
                        hv = slice(kv * HD, (kv + 1) * HD)
                        for tile in range(TT):
                            terms = []
                            for b in range(2):
                                if tile == 0:
                                    terms.append((vals[:, b, 0, hv], probT[:, b, 0:P]))
                                else:
                                    terms.append((vals[:, b, 0, hv], probT[:, b, P:2 * P]))
                                    terms.append((vals[:, b, 1, hv], probT[:, b, 2 * P:3 * P]))
                            terms.append((vcmp[0:NC, kv, :], probT[0:NC, tile, 384:512]))
                            for n, (v, pr) in enumerate(terms):
                                mm = pe.matmul(px[:, 2, tile * P:(tile + 1) * P], v, pr, start=n == 0,
                                               stop=n == len(terms) - 1)
                        mm.then_inc(peA.sem, peA.did(f"o{h}"))

                    strip(s0, 0, "B", xhl)
                    strip(s0 + 1, 1, "B", xhl, hooks={1: lambda: (rms(), score(0))})
                    strip(s0 + 2, 0, "A", xhl, hooks={1: lambda: (turn(0), score(1)), 3: lambda: mix(0)})
                    strip(s0 + 3, 1, "B", xhl, hooks={2: lambda: turn(1), 3: lambda: mix(1)})

            def groups(j):
                pe.wait_ge(dveG.sem, dveG.at("v5"))
                pe.wait_ge(misc_in, 64)
                for n in range(2):
                    g = 2 * j + n
                    for a in range(TT):
                        o = px[:, j, n * T + a * P:n * T + (a + 1) * P]
                        pe.matmul(o, gav[:, a, g * P:(g + 1) * P], w_sT[:, g, :], start=True, stop=False)
                        mm = pe.matmul(o, ones[0:1, :], sgub[0:1, g * P:(g + 1) * P], start=False, stop=True)
                mm.then_inc(peG.sem, peG.did(f"g{j}"))

            strip(S_SGU, 0, "B", xhl)
            for j in range(1, 4):
                strip(S_SGU + j, j % 2, "B", xhl, hooks={2: lambda j=j: groups(j - 1)})
            groups(3)

            def swapped(k):
                return (k + KT // 2) % KT

            def wait_cat(name):
                pe.wait_ge(dveG.sem, dveG.at(name))

            pe.wait_ge(dveA.sem, dveA.at("cat", 3))
            strip(S_OUT0, 0, "B", cathl, order=swapped, hooks={1: lambda: wait_cat("l1"), 2: lambda: wait_cat("l3")})
            strip(S_OUT0 + 1, 1, "B", cathl, order=swapped)
            with pe.Fori(1, 4) as p:
                for j in range(2):
                    strip(p * 2 + (S_OUT0 + j), j, "B", cathl, order=swapped)
            pe.wait_ge(dveO.sem, dveO.at("ab", 3))
            for n in range(2):
                mm = pe.matmul(px[:, 0, 0:T], ones[:], acc[:, n * T:(n + 1) * T], start=n == 0, stop=n == 1)
            mm.then_inc(peR.sem, peR.did("ss"))
            pe.wait_ge(xlo_done, 5)

            def normed(layer):
                return {q: lambda q=q: pe.wait_ge(xlo_done, 4 * layer + q + 2) for q in range(3)}

            with pe.Fori(0, 8) as i:
                s0 = i * 4 + S_HGRN

                def turn_g():
                    pe.wait_ge(actH.sem, actH.at("g", i))
                    for b in range(4):
                        mm = pe.transpose(px[:, 0, b * P:(b + 1) * P], hG[:, b * P:(b + 1) * P], ident[:])
                    mm.then_inc(peH.sem, peH.did("gT"))

                def sum_g():
                    pe.wait_ge(actH.sem, actH.at("gn", i))
                    for b in range(4):
                        mm = pe.matmul(px[:, 1, b * P:(b + 1) * P], hGN[:, b * P:(b + 1) * P], tri64[:],
                                       start=True, stop=True)
                    mm.then_inc(peH.sem, peH.did("G"))

                def intra():
                    pe.wait_ge(poolH.sem, poolH.at("ks", i))
                    for b in range(4):
                        mm = pe.transpose(px[:, 3, b * P:(b + 1) * P], hKS[:, b * P:(b + 1) * P], ident[:])
                    mm.then_inc(peH.sem, peH.did("ksT"))
                    pe.wait_ge(dveH.sem, dveH.at("qe", i))
                    for b in range(4):
                        mm = pe.matmul(px[:, 2, b * P:(b + 1) * P], hKE[:, b * P:(b + 1) * P],
                                       hQE[:, b * P:(b + 1) * P], start=True, stop=True)
                    mm.then_inc(peH.sem, peH.did("at"))

                def chunk_kv():
                    pe.wait_ge(actH.sem, actH.at("kn", i))
                    pe.wait_ge(strip_out, s0 + 3)
                    for h in range(2):
                        for c in range(3):
                            r0, a = CH * (c % 2), c // 2
                            b = 2 * h + a
                            mm = pe.matmul(kv_at(h, c), hKN[r0:r0 + CH, b * P:(b + 1) * P],
                                           Z[r0:r0 + CH, 2, a, h * HD:(h + 1) * HD], start=True, stop=True)
                    mm.then_inc(peH.sem, peH.did("kv"))

                def outputs():
                    pe.wait_ge(dveH.sem, dveH.at("s31", i))
                    pe.wait_ge(poolH.sem, poolH.at("qi", i))
                    for h in range(2):
                        for a in range(TT):
                            b = 2 * h + a
                            pe.matmul(px[:, 2, b * P:(b + 1) * P], Z[:, 2, a, h * HD:(h + 1) * HD],
                                      hAT[:, b * P:(b + 1) * P], start=True, stop=False, skip_group_check=True)
                            for c in (1,) if a == 0 else (2, 3):
                                mm = pe.matmul(px[:, 2, h * T + c * CH:h * T + (c + 1) * CH], hST[:, h, c - 1, :],
                                               hQI[:, h * T + c * CH:h * T + (c + 1) * CH], start=False,
                                               stop=c != 2, skip_group_check=True)
                    mm.then_inc(peH.sem, peH.did("o"))

                def squares():
                    pe.wait_ge(actH.sem, actH.at("sq", i))
                    pe.matmul(px[:, 3, :], ones[:], hSQ, start=True, stop=True).then_inc(peH.sem, peH.did("ss"))

                strip(s0, 0, "B", xhl, hooks=normed(1))
                strip(s0 + 1, 1, "B", xhl, hooks={1: turn_g, 2: sum_g})
                strip(s0 + 2, 0, "A", xhl, hooks={1: intra})
                strip(s0 + 3, 1, "B", xhl, hooks={0: chunk_kv, 2: outputs, 3: squares})

            def residual(p, j):
                def late(g):
                    if g == 0:
                        pe.wait_ge(poolR.sem, poolR.at("ra" if j == 0 else "rb", p))
                    for c in range(2):
                        pe.matmul(pp[:, 2 * j + g, c * P:(c + 1) * P], xres[:, j, c, g * P:(g + 1) * P], ident[:],
                                  start=False, stop=False)
                return late

            def last_heads():
                pe.wait_ge(dveH.sem, dveH.at("lo", 7))

            pe.wait_ge(dveH.sem, dveH.at("lo", 6))
            for j in range(2):
                strip(S_OUT1 + j, j, "A", cathl, late=residual(0, j), hooks={2: last_heads} if j == 0 else None)
            with pe.Fori(1, 4) as p:
                for j in range(2):
                    strip(p * 2 + (S_OUT1 + j), j, "A", cathl, late=residual(p, j))


_INS = ['x', 'even_norm', 'even_w_in', 'sgu_ln_g', 'sgu_ln_b', 'sgu_w', 'sgu_b', 'nsa_q_gain', 'nsa_k_gain',
        'cmp_pos', 'cmp_w1', 'cmp_b1', 'cmp_w2', 'even_w_out', 'odd_norm', 'odd_w_in', 'hgrn_lb',
        'hgrn_out_gain', 'odd_w_out']
_ONE = {'even_w_in', 'sgu_w', 'sgu_b', 'nsa_k_gain', 'cmp_pos', 'cmp_w1', 'cmp_b1', 'cmp_w2', 'even_w_out',
        'odd_w_in', 'odd_w_out', 'sgu_ln_g', 'sgu_ln_b'}


def kernel(**inputs):
    import numpy as _np
    import concourse.bacc as _bacc
    from concourse import mybir as _mybir
    from concourse.bass_utils import run_bass_kernel_spmd as _run

    nc = _bacc.Bacc("TRN2", target_bir_lowering=False, num_devices=1)
    arrays, args = {}, []
    for name in _INS:
        a = _np.ascontiguousarray(inputs[name])
        if name in _ONE:
            a = a[0]
        arrays[f"in_{name}"] = a
        args.append(nc.dram_tensor(f"in_{name}", a.shape, _mybir.dt.from_np(a.dtype), kind="ExternalInput").ap())
    out = nc.dram_tensor("out_y", (T, D), F32, kind="ExternalOutput").ap()
    trunk(nc, *args, out)
    r = _run(nc, [arrays], core_ids=[0])
    return r.results[0]["out_y"].reshape(1, T, D)
```

```python
from contextlib import ExitStack

import concourse.bass as bass
from concourse import mybir
from concourse.alu_op_type import AluOpType as ALU

F32 = mybir.dt.float32
F32R = mybir.dt.float32r
I32 = mybir.dt.int32
ACT = mybir.ActivationFunctionType
AX = mybir.AxisListType

P = 128
D = 2048
KT = D // P
T = 256
TT = T // P
SW = 256
NQ = 4
KQ = KT // NQ
HD = 128
A_WIDTH = 1024
B_WIDTH = 1024
KV0 = 3 * A_WIDTH + 2 * B_WIDTH
NG = 24
GATE0 = KV0 + 6 * SW
NL = 32
NC = (T - NL) // 16 + 1
CW = 2 * NC
EPS = 1e-6
BIG = 1e30
CH = 64
LN_EXP = "natural_log_exp_and_others"
ARENA = 14104

S_PRE, S_ATT, S_SGU, S_OUT0, S_HGRN, S_OUT1, S_END = 0, 10, 26, 30, 38, 70, 78


class Steps:

    def __init__(self, sem, names):
        self.sem, self.names, self.n = sem, names.split(), 0
        assert len(set(self.names)) == len(self.names)

    def did(self, name):
        assert self.names[self.n % len(self.names)] == name, (self.names[self.n % len(self.names)], name)
        self.n += 1
        return 1

    def at(self, name, i=0):
        return i * len(self.names) + self.names.index(name) + 1


def trunk(nc, x, even_norm, even_w_in, sgu_ln_g, sgu_ln_b, sgu_w, sgu_b, q_gain, k_gain, cmp_pos,
          cmp_w1, cmp_b1, cmp_w2, even_w_out, odd_norm, odd_w_in, hgrn_lb, out_gain, odd_w_out, out):
    with ExitStack() as ctx:
        def sb(name, shape, dt=F32):
            return ctx.enter_context(nc.sbuf_tensor(name, shape, dt))

        def sem(name):
            return ctx.enter_context(nc.semaphore(name))

        raw = sb("raw", [P, NQ, KQ, SW])
        whl = sb("whl", [P, NQ, KQ, 2, SW], F32R)
        xhl = sb("xhl", [P, KT, 2, T], F32R)
        cathl = sb("cathl", [P, KT, 2, T], F32R)
        xT = sb("xT", [P, KT, T])
        ident = sb("ident", [P, P])
        ones = sb("ones", [P, P])
        tri64 = sb("tri64", [P, P])
        tri64_i = sb("tri64_i", [P, P], I32)
        tri_i = sb("tri_i", [P, P], I32)
        fold = sb("fold", [2 * CW, CW])
        vecs = sb("vecs", [P, P])
        vT = sb("vT", [P, P])
        posr = sb("posr", [2 * NL, HD])
        posT = sb("posT", [P, 2 * NL])
        sgub = sb("sgub", [1, 8 * P])
        small = sb("small", [P, 256])
        tmp = sb("tmp", [P, 2, 2, SW])
        Z = sb("Z", [P, 4, 2, SW])
        arena = sb("arena", [P, ARENA])

        class Carve:
            def __init__(self):
                self.o = 0

            def __call__(self, n):
                self.o += n
                assert self.o <= ARENA, self.o
                return arena[:, self.o - n:self.o]

        c0 = Carve()
        gav = c0(2048).rearrange("p (a n) -> p a n", a=2)
        gu = c0(2048).rearrange("p (a n) -> p a n", a=8)
        xnat = arena[:, 0:4096].rearrange("p (a n) -> p a n", a=2)
        lngb = c0(2048).rearrange("p (a n) -> p a n", a=2)
        keysT = c0(2 * 527).rearrange("p (a n) -> p a n", a=2)
        vals = c0(1024).rearrange("p (b a n) -> p b a n", b=2, a=2)
        vcmp = c0(256).rearrange("p (a n) -> p a n", a=2)
        w_sT = c0(1024).rearrange("p (a n) -> p a n", a=8)
        dist = c0(414)
        bias = c0(828).rearrange("p (a n) -> p a n", a=2)
        prob = c0(800)[:, 0:798]
        probT = c0(1024).rearrange("p (a n) -> p a n", a=2)
        sgw = arena[:, c0.o - 1024:c0.o].rearrange("p (a n) -> p a n", a=8)
        w2 = c0(512).rearrange("p (i a n) -> p i a n", i=2, a=2)
        obuf = c0(512).rearrange("p (a n) -> p a n", a=2)
        scr = arena[:, c0.o - 512:c0.o]
        wg = prob[:, 0:KT * NG].rearrange("p (k n) -> p k n", k=KT)
        wghl = cathl[:, 8:10].rearrange("p k a n -> p (k a n)")[:, 0:KT * 2 * NG]\
            .rearrange("p (k a n) -> p k a n", k=KT, a=2)
        sgz = c0(512).rearrange("p (a n) -> p a n", a=2)
        xn = arena[:, 0:4096].rearrange("p (r a n) -> p r a n", r=4, a=KQ)
        kpos = arena[:, 0:960]

        c1 = Carve()
        (hF, hK, hG, hGN, hGS, hD1, hE2, hD2, hE3, hKE, hKS, hQE, hQI, hAT, hKN, hSQ, hRS, hSG, hZS,
         hO) = (c1(512) for _ in range(20))
        hST = c1(768).rearrange("p (h c v) -> p h c v", h=2, c=3)
        acc = c1(512)
        sq = c1(512)
        xres = arena[:, 0:1024].rearrange("p (b a n) -> p b a n", b=2, a=2)

        pp = ctx.enter_context(nc.psum_tensor("pp", [P, 4, 512], F32))
        px = ctx.enter_context(nc.psum_tensor("px", [P, 4, 512], F32))

        landed = [sem(f"landed{q}") for q in range(NQ)]
        hi_done, lo_done = sem("hi_done"), sem("lo_done")
        pe_q = sem("pe_q")
        lo_pool = sem("lo_pool")
        lo_out, strip_out = sem("lo_out"), sem("strip_out")
        seen = sem("seen")
        x_in = [sem("x_in0"), sem("x_in1")]
        wg_in, gain_in, vec_in, sg_in, misc_in = sem("wg_in"), sem("gain_in"), sem("vec_in"), sem("sg_in"), sem("misc_in")
        y_out = [sem("y_out0"), sem("y_out1")]

        pool0 = Steps(sem("pool0"), "ms ident ms1 vecs fz fold0 fold1 triF tri64a tri64 tri64i id0 id1 ic0 ic1 df "
                      "sel0 sel1 selc0 selc1 zw")
        pe0 = Steps(sem("pe0"), "xT0 xT1 xT2 xT3 xT4 xT5 xT6 xT7 rs gT vT posT wsT0 wsT1")
        act0 = Steps(sem("act0"), "ss0 ss1 xT0 ln rs xT2 xT4 xT6 wg lbe0 lbe1")
        dve0 = Steps(sem("dve0"), "xT1 ms xT3 xT5 xT7 diag0 diag1 gT rsb vT posT gain "
                     "wsT0 wsT1 wg lbm lba lbb lbs lbr lbp0 lbp1 lbc lb omlb")
        xn_done, xhi_done, xlo_done, xlo_pool = sem("xn_done"), sem("xhi_done"), sem("xlo_done"), sem("xlo_pool")
        peP = Steps(sem("peP"), "fk fv ck0 ck1 cv0 cv1 kcT kT0 kT1 gates")
        actP = Steps(sem("actP"), "kp0 kp1 hk0 hk1 hv0 hv1 lnc rsc ln0 rs0 ln1 rs1 gc gs")
        dveP = Steps(sem("dveP"), "kpa0 kpb0 kpc0 kpd0 kpl0 kpa1 kpb1 kpc1 kpd1 kpl1 "
                     "kc sqc ssc msc kn0 kn1 kcT vc sq0 ss0 ms0 k00 k01 k02 k03 kT0 sq1 ss1 ms1 k10 k11 k12 k13 kT1 "
                     "ga gb gt0 gt1 gt2 gt3 gt4 gt5")
        peA = Steps(sem("peA"), "rms s0 t0 s1 o0 t1 o1")
        actA = Steps(sem("actA"), "sq ln rq e00 e01 e02 e03 e04 e05 pt0 pc0 e10 e11 e12 e13 e14 e15 sg av "
                     "pt1 pc1 gu cat")
        dveA = Steps(sem("dveA"), "ms a00 a01 a02 a03 m00 m01 m02 n0 r0x r0 c0 p00 p01 p02 pt0 pd0 "
                     "a10 a11 a12 a13 m10 m11 m12 n1 r1x r1 c1 p10 p11 p12 sz o0 pt1 pd1 o1 cat")
        poolA = Steps(sem("poolA"), "b0 b1")
        peG = Steps(sem("peG"), "g0 g1 g2 g3")
        actG = Steps(sem("actG"), "ln rs sg0 sg1 c1 sg2 c2 sg3 c3 c4")
        dveG = Steps(sem("dveG"), "st0 st1 st2 st3 ag0 ag1 ms v0 v1 v2 v3 v4 v5 "
                     "z0 z1 u0 w0 l0 z2 u1 w1 l1 z3 u2 w2 l2 u3 w3 l3 acc")
        actO = Steps(sem("actO"), "sqa sqb")
        dveO = Steps(sem("dveO"), "xa aa xb ab")
        peR, actR, dveR = Steps(sem("peR"), "ss"), Steps(sem("actR"), "ln rs"), Steps(sem("dveR"), "ms at0")
        peH = Steps(sem("peH"), "gT G ksT at kv o ss")
        actH = Steps(sem("actH"), "sf g gn e2 e1 e3 e4 kn sq ln rs sg cat")
        dveH = Steps(sem("dveH"), "f0 f1 k gs d1 d2 kt qe at s10 s11 s20 s21 s30 s31 ms o1 o2 lo")
        poolH = Steps(sem("poolH"), "ks qi zs")
        poolR = Steps(sem("poolR"), "ra rb")

        block = ctx.enter_context(nc.Block())

        V_N0, V_N1, V_LB, V_B1, V_QG, V_KG, V_OG = 0, 16, 32, 64, 68, 69, 72
        NV = 73
        SSX, RSX, KGQ, LB, OMLB, LBT = 0, 2, 4, 8, 24, 40
        KSS, KRS, GSUM, GTAB, RSSQ, MX, NM, SUMS, COEF = 136, 140, 0, 144, 200, 204, 210, 216, 222
        BST, BAG = 228, 252

        REGIONS = [(0, 128), (128, 256), (256, 512), (512, 768), (768, 783), (783, 798)]

        ltmp = [small[:, LBT + 16 * n:LBT + 16 * n + 16] for n in range(6)]

        def src(w, col, q, swap=False):
            q = (q + 2) % NQ if swap else q
            return w[q * KQ * P:(q + 1) * KQ * P, bass.ds(col, SW)].rearrange("(k p) n -> p k n", p=P)

        @block.sync
        def _(sp):
            def load(s, part, first=False, static=True):
                for q in range(NQ):
                    if not first:
                        if isinstance(s, int) and s == 1:
                            sp.wait_ge(lo_pool, q + 1)
                        else:
                            sp.wait_ge(lo_done, 4 * (s - 1) + q + 1)
                        if not static:
                            sp.sem_inc(seen, 1)
                    sp.dma_start(raw[:, q], part(q)).then_inc(landed[q], 16)

            def load_x(half):
                w = slice(half * D // 2, (half + 1) * D // 2)
                return [(xnat[:, a, w], x[0, a * P:(a + 1) * P, w]) for a in range(TT)]

            for a, (to, at) in enumerate(load_x(0)):
                sp.dma_start(to, at).then_inc(x_in[a], 16)
            for n in range(2):
                load(n, lambda q, n=n: src(even_w_in, KV0 + SW * n, q), first=n == 0)
            for i in range(2):
                for half in range(2):
                    load(2 + 2 * i + half, lambda q, i=i, half=half: cmp_w1[
                        i, (half * 16 + q * KQ) * P:(half * 16 + (q + 1) * KQ) * P, :]
                        .rearrange("(k p) n -> p k n", p=P))
            for n, g in enumerate((2, 4, 3, 5)):
                load(6 + n, lambda q, g=g: src(even_w_in, KV0 + SW * g, q))
            with sp.Fori(0, 4) as p:
                for j, base in enumerate((3 * A_WIDTH, 3 * A_WIDTH + B_WIDTH, A_WIDTH, 0)):
                    load(p * 4 + (S_ATT + j), lambda q, base=base: src(even_w_in, p * SW + base, q),
                         static=False)
            for j in range(4):
                load(S_SGU + j, lambda q, j=j: src(even_w_in, 2 * A_WIDTH + SW * j, q))
            with sp.Fori(0, 4) as p:
                for j in range(2):
                    load(p * 2 + (S_OUT0 + j), lambda q, j=j: src(even_w_out, p * (2 * SW) + j * SW, q, True),
                         static=False)
            with sp.Fori(0, 8) as p:
                for j, base in enumerate((D, 0, 2 * D, 3 * D)):
                    load(p * 4 + (S_HGRN + j), lambda q, base=base: src(odd_w_in, p * SW + base, q),
                         static=False)

            def store(n, j):
                sp.wait_ge(strip_out, n * 2 + (S_OUT1 + j + 1))
                sp.sem_inc(seen, 1)
                sp.dma_start(out[:, bass.ds(n * (2 * SW) + j * SW, SW)].rearrange("(a p) n -> p a n", p=P),
                             Z[:, j]).then_inc(y_out[j], 16)

            for j in range(2):
                load(S_OUT1 + j, lambda q, j=j: src(odd_w_out, j * SW, q))
            with sp.Fori(0, 3) as p:
                for j in range(2):
                    load(p * 2 + (S_OUT1 + 2 + j), lambda q, j=j: src(odd_w_out, p * (2 * SW) + (2 + j) * SW, q),
                         static=False)
                for j in range(2):
                    store(p, j)
            for j in range(2):
                store(3, j)
            for j in range(2):
                sp.wait_ge(y_out[j], 16 * 4)

        def lo_part(eng, layer, c):
            eng.wait_ge(xhi_done, 4 * layer + c + 1)
            eng.tensor_tensor(xhl[:, KQ * c:KQ * c + KQ, 1, :], xn[:, c],
                              xhl[:, KQ * c:KQ * c + KQ, 0, :].bitcast(F32), ALU.subtract)\
                .then_inc(xlo_pool if c == 1 else xlo_done, 1)

        @block.gpsimd
        def _(pool):
            pool.memset(ident[:], 0.0).then_inc(pool0.sem, pool0.did("ms"))
            pool.wait_ge(pool0.sem, pool0.at("ms"))
            pool.affine_select(out=ident[:], in_=ident[:], compare_op=ALU.not_equal, fill=1.0, base=0,
                               pattern=[[-1, P]], channel_multiplier=1).then_inc(pool0.sem, pool0.did("ident"))
            pool.memset(ones[:], 1.0).then_inc(pool0.sem, pool0.did("ms1"))
            pool.memset(vecs[:], 0.0).then_inc(pool0.sem, pool0.did("vecs"))
            pool.wait_ge(pool0.sem, pool0.at("vecs"))
            for row, a in ((V_N0, even_norm.rearrange("a (k p) -> (a k) p", p=P)),
                           (V_N1, odd_norm.rearrange("a (k p) -> (a k) p", p=P)),
                           (V_LB, hgrn_lb.rearrange("a (k p) -> (a k) p", p=P)),
                           (V_B1, cmp_b1.rearrange("a (k p) -> (a k) p", p=P)),
                           (V_QG, q_gain), (V_KG, k_gain), (V_OG, out_gain)):
                pool.dma_start(vecs[row:row + a.shape[0], :], a).then_inc(gain_in if row == V_N0 else vec_in, 16)
            pool.dma_start(posr[:], cmp_pos.rearrange("a l d -> (a l) d")).then_inc(vec_in, 16)
            pool.memset(fold[:], 0.0).then_inc(pool0.sem, pool0.did("fz"))
            for n, before in enumerate(("fz", "fold0")):
                pool.wait_ge(pool0.sem, pool0.at(before))
                pool.affine_select(out=fold[:], in_=fold[:], compare_op=ALU.not_equal, fill=1.0, base=-n * CW,
                                   pattern=[[-1, CW]], channel_multiplier=1).then_inc(pool0.sem, pool0.did(f"fold{n}"))
            pool.affine_select(out=tri64[:], in_=ones[:], compare_op=ALU.is_ge, fill=0.0, base=0,
                               pattern=[[1, P]], channel_multiplier=-1).then_inc(pool0.sem, pool0.did("triF"))
            pool.wait_ge(pool0.sem, pool0.at("triF"))
            pool.tensor_copy(tri_i[:], tri64[:]).then_inc(pool0.sem, pool0.did("tri64a"))
            pool.wait_ge(pool0.sem, pool0.at("tri64a"))
            pool.memset(tri64[0:CH, CH:P], 0.0).then_inc(pool0.sem, pool0.did("tri64"))
            pool.wait_ge(pool0.sem, pool0.at("tri64"))
            pool.tensor_copy(tri64_i[:], tri64[:]).then_inc(pool0.sem, pool0.did("tri64i"))
            for q in range(NQ):
                if q == 2:
                    lo_part(pool, 0, 1)
                pool.wait_ge(hi_done, q + 1)
                pool.tensor_tensor(whl[:, q, :, 1, :], raw[:, q], whl[:, q, :, 0, :].bitcast(F32), ALU.subtract)\
                    .then_inc(lo_pool, 1)
            pool.dma_start(sgw, sgu_w.rearrange("g t s -> t g s")).then_inc(sg_in, 16)
            pool.dma_start(sgub[:], sgu_b.rearrange("(a g) t -> a (g t)", a=1)).then_inc(misc_in, 16)
            pool.dma_start(w2[:], cmp_w2.rearrange("i (a p) n -> p i a n", p=P)).then_inc(misc_in, 16)
            for n, v in enumerate((sgu_ln_g, sgu_ln_b)):
                pool.dma_start(lngb[:, n, :], v.partition_broadcast(P)).then_inc(misc_in, 16)
            di = scr[:, 0:414].bitcast(I32)
            parts = (("0", 0, P, -1, 0), ("1", P, T, -1, P), ("c0", 3 * P, NC, -16, 1 - NL),
                     ("c1", 3 * P + NC, NC, -16, P + 1 - NL))
            for n, (name, at, w, step, base) in enumerate(parts):
                pool.iota(di[:, at:at + w], pattern=[[step, w]], base=base, channel_multiplier=1)\
                    .then_inc(pool0.sem, pool0.did("i" + (name if name[0] == "c" else "d" + name)))
            pool.wait_ge(pool0.sem, pool0.at("ic1"))
            pool.tensor_copy(dist, di).then_inc(pool0.sem, pool0.did("df"))
            pool.wait_ge(pool0.sem, pool0.at("df"))
            for name, at, w, step, base in parts:
                pool.affine_select(out=dist[:, at:at + w], in_=dist[:, at:at + w], compare_op=ALU.is_ge, fill=BIG,
                                   base=base, pattern=[[step, w]], channel_multiplier=1)\
                    .then_inc(pool0.sem, pool0.did("sel" + name))
            pool.memset(w_sT[:], 0.0).then_inc(pool0.sem, pool0.did("zw"))
            pool.wait_ge(pool0.sem, pool0.at("selc1"))
            for a in range(2):
                pool.tensor_scalar(bias[:, a, :], dist, -0.5 ** (a + 1), None, ALU.mult)\
                    .then_inc(poolA.sem, poolA.did(f"b{a}"))
            pool.wait_ge(poolA.sem, poolA.at("b1"))
            with pool.Fori(0, 4) as p:
                for a in range(2):
                    pool.wait_ge(dveA.sem, dveA.at(f"a{a}3", p))
                    pool.sem_inc(seen, 1)
                    pool.tensor_scalar(bias[:, a, :], bias[:, a, :], 0.25, None, ALU.mult)\
                        .then_inc(poolA.sem, poolA.did(f"b{a}"))
            lo_part(pool, 1, 1)
            with pool.Fori(0, 8) as i:
                pool.wait_ge(actH.sem, actH.at("e4", i))
                pool.tensor_tensor(hKS, hK, hD2, ALU.mult).then_inc(poolH.sem, poolH.did("ks"))
                pool.wait_ge(strip_out, i * 4 + (S_HGRN + 2))
                pool.tensor_tensor(hQI, Z[:, 1].rearrange("p a n -> p (a n)"), hE3, ALU.mult)\
                    .then_inc(poolH.sem, poolH.did("qi"))
                pool.wait_ge(actH.sem, actH.at("sg", i))
                pool.tensor_tensor(hZS, Z[:, 3].rearrange("p a n -> p (a n)"), hSG, ALU.mult)\
                    .then_inc(poolH.sem, poolH.did("zs"))
            pool.wait_ge(actH.sem, actH.at("g", 7))
            pool.wait_ge(dveH.sem, dveH.at("kt", 7))
            with pool.Fori(0, 4) as p:
                for j in range(2):
                    pool.wait_ge(pe_q, p * 8 + 4 * (S_OUT1 + j - 1))
                    pool.tensor_copy(xres[:, j], xT[:, bass.ds(p * 4 + 2 * j, 2), :])\
                        .then_inc(poolR.sem, poolR.did("ra" if j == 0 else "rb"))

        def kv_at(h, c):
            return px[:, 1, h * HD:(h + 1) * HD] if c == 1 else px[:, 0, (2 * h + c // 2) * HD:(2 * h + c // 2 + 1) * HD]

        def cast(act, s, qs, first=False):
            for q in qs:
                act.wait_ge(landed[q], s * 16 + 16)
                if not first:
                    act.wait_ge(pe_q, s * 4 + (q - 3))
                act.activation(whl[:, q, :, 0, :], raw[:, q], ACT.Copy).then_inc(hi_done, 1)

        def take_lo(act, s, par, n=1, cols=slice(256, 512), first=False):
            act.wait_ge(pe_q, s * 4 + 4)
            if not first:
                act.wait_ge(strip_out, s - 1)
            w = cols.stop - cols.start
            act.activation(tmp[:, par, :, 0:w], pp[:, 2 * par:2 * par + 2, cols], ACT.Copy).then_inc(lo_out, n)

        @block.scalar
        def _(act):
            for a in range(TT):
                act.dma_start(xnat[:, a, D // 2:], x[0, a * P:(a + 1) * P, D // 2:]).then_inc(x_in[a], 16)
            act.dma_start(wg[:], even_w_in[:, GATE0:GATE0 + NG].rearrange("(k p) n -> p k n", p=P)).then_inc(wg_in, 16)
            act.preload_act_table_set(LN_EXP)
            for a in range(TT):
                act.wait_ge(x_in[a], 32)
                act.activation(cathl[:, 4 * a:4 * a + 4].rearrange("p k a n -> p (k a n)"), xnat[:, a, :], ACT.Square,
                               accum_out=small[:, SSX + a:SSX + a + 1]).then_inc(act0.sem, act0.did(f"ss{a}"))

            def take_x(b):
                act.wait_ge(pe0.sem, pe0.at(f"xT{b}"))
                act.activation(xT[:, 2 * b:2 * b + 2, :], (pp if b < 4 else px)[:, b % 4, :]
                               .rearrange("p (a n) -> p a n", a=2), ACT.Copy).then_inc(act0.sem, act0.did(f"xT{b}"))

            take_x(0)
            act.wait_ge(dve0.sem, dve0.at("ms"))
            act.activation(small[:, RSX:RSX + 2], small[:, SSX:SSX + 2], ACT.Ln).then_inc(act0.sem, act0.did("ln"))
            act.wait_ge(act0.sem, act0.at("ln"))
            act.activation(small[:, RSX:RSX + 2], small[:, RSX:RSX + 2], ACT.Exp, scale=-0.5)\
                .then_inc(act0.sem, act0.did("rs"))
            for b in (2, 4, 6):
                take_x(b)

            def xhi(layer, between=None):
                for c in range(4):
                    act.wait_ge(xn_done, 16 * layer + 4 * c + 4)
                    act.activation(xhl[:, KQ * c:KQ * c + KQ, 0, :], xn[:, c], ACT.Copy).then_inc(xhi_done, 1)
                    if between:
                        between(c)

            cast(act, S_PRE, (0,), first=True)
            xhi(0, between=lambda c: cast(act, S_PRE, (c + 1,), first=True) if c < 3 else None)

            def side_inputs():
                act.wait_ge(wg_in, 16)
                act.activation(wghl[:, :, 0, :], wg[:], ACT.Copy).then_inc(act0.sem, act0.did("wg"))
                for n in range(2):
                    act.wait_ge(dve0.sem, dve0.at("lba" if n == 0 else "lbb"))
                    act.activation(ltmp[1 + n], ltmp[1 + n], ACT.Exp).then_inc(act0.sem, act0.did(f"lbe{n}"))

            def rstd(steps, names, dve, dname, ap, scale=-0.5, i=0):
                act.wait_ge(dve.sem, dve.at(dname, i))
                act.activation(ap, ap, ACT.Ln).then_inc(steps.sem, steps.did(names[0]))
                act.wait_ge(steps.sem, steps.at(names[0], i))
                act.activation(ap, ap, ACT.Exp, scale=scale).then_inc(steps.sem, steps.did(names[1]))

            kph = [cathl[:, 4 * i:4 * i + 4].rearrange("p k a n -> p (k a n)")[:, 0:NL * 2 * CW]
                   .rearrange("p (l a n) -> p l a n", l=NL, a=2) for i in range(2)]
            for s in range(S_PRE, S_ATT):
                cast(act, s + 1, (0,))
                if s in (4, 6):
                    i = (s - 4) // 2
                    act.wait_ge(strip_out, s if s == 4 else S_PRE + 6)
                    act.wait_ge(pool0.sem, pool0.at("df"))
                    for g in range(2):
                        act.activation(scr[:, 128 + 64 * i + CW * g:128 + 64 * i + CW * g + CW], Z[:, i, g, 0:CW],
                                       ACT.Gelu_apprx_tanh, bias=vT[:, V_B1 + 2 * i + g:V_B1 + 2 * i + g + 1])\
                            .then_inc(actP.sem, actP.did(f"h{'kv'[i]}{g}"))
                if s == 6:
                    rstd(actP, ("lnc", "rsc"), dveP, "msc", small[0:NC, KRS:KRS + 2])
                cast(act, s + 1, (1, 2))
                if s in (2, 4):
                    cast(act, s + 1, (3,))
                    continue
                if s in (3, 5):
                    i = (s - 3) // 2
                    act.wait_ge(pe_q, s * 4 + 4)
                    act.wait_ge(strip_out, s - 1)
                    act.activation(tmp[0:2 * CW, i].rearrange("p a n -> p (a n)"), pp[0:2 * CW, i, :], ACT.Copy)\
                        .then_inc(lo_out, 2)
                else:
                    take_lo(act, s, s % 2, first=s < 2)
                cast(act, s + 1, (3,))
                if s in (0, 1):
                    act.wait_ge(dveP.sem, dveP.at(f"kpd{s}"))
                    act.activation(kph[s][:, :, 0, :], kpos.rearrange("p (l n) -> p l n", l=NL), ACT.Copy)\
                        .then_inc(actP.sem, actP.did(f"kp{s}"))
                if s == 3:
                    side_inputs()
                if s in (6, 7):
                    n = s - 6
                    rstd(actP, (f"ln{n}", f"rs{n}"), dveP, f"ms{n}", small[:, KRS:KRS + 4])
                if s == 8:
                    act.wait_ge(peP.sem, peP.at("gates"))
                    act.activation(scr[:, 0:48].rearrange("p (a n) -> p a n", a=2),
                                   px[:, 3, 0:128].rearrange("p (a n) -> p a n", a=2)[:, :, NG:2 * NG], ACT.Copy)\
                        .then_inc(actP.sem, actP.did("gc"))
                    act.wait_ge(dveP.sem, dveP.at("ga"))
                    act.activation(scr[:, 48:96], scr[:, 48:96], ACT.Sigmoid).then_inc(actP.sem, actP.did("gs"))

            with act.Fori(0, 4) as p:
                s0 = p * 4 + S_ATT
                act.preload_act_table_set(LN_EXP)

                def exps(a):
                    act.wait_ge(dveA.sem, dveA.at(f"n{a}", p))
                    for r, (lo, hi) in enumerate(REGIONS):
                        act.activation(prob[:, lo:hi], prob[:, lo:hi], ACT.Exp, bias=small[:, NM + r:NM + r + 1],
                                       accum_out=small[:, SUMS + r:SUMS + r + 1])\
                            .then_inc(actA.sem, actA.did(f"e{a}{r}"))

                def take_pT(a):
                    act.wait_ge(peA.sem, peA.at(f"t{a}", p))
                    act.activation(probT[:, 0, 0:384], px[:, 2, 0:384], ACT.Copy)\
                        .then_inc(actA.sem, actA.did(f"pt{a}"))
                    act.activation(probT[0:NC, 0, 384:512], px[0:NC, 2, 384:512], ACT.Copy)\
                        .then_inc(actA.sem, actA.did(f"pc{a}"))

                cast(act, s0 + 1, (0, 1, 2))
                take_lo(act, s0, 0)
                cast(act, s0 + 1, (3,))
                act.wait_ge(strip_out, s0 + 1)
                act.activation(obuf[:], Z[:, 0], ACT.Square).then_inc(actA.sem, actA.did("sq"))
                cast(act, s0 + 2, (0, 1))
                rstd(actA, ("ln", "rq"), dveA, "ms", small[:, RSSQ:RSSQ + 4], i=p)
                cast(act, s0 + 2, (2,))
                exps(0)
                take_lo(act, s0 + 1, 1)
                cast(act, s0 + 2, (3,))
                cast(act, s0 + 3, (0, 1))
                take_pT(0)
                cast(act, s0 + 3, (2,))
                exps(1)
                take_lo(act, s0 + 2, 0)
                act.wait_ge(strip_out, s0 + 2)
                act.activation(sgz[:], Z[:, 1], ACT.Tanh, scale=0.5).then_inc(actA.sem, actA.did("sg"))
                cast(act, s0 + 3, (3,))
                act.wait_ge(strip_out, s0 + 3)
                act.activation(gav[:, :, bass.ds(p * SW, SW)], Z[:, 2], ACT.Gelu_apprx_tanh)\
                    .then_inc(actA.sem, actA.did("av"))
                cast(act, s0 + 4, (0, 1))
                take_pT(1)
                cast(act, s0 + 4, (2,))
                take_lo(act, s0 + 3, 1)
                cast(act, s0 + 4, (3,))
                act.wait_ge(strip_out, s0 + 4)
                act.activation(gu[:, bass.ds(p * 2, 2), :], Z[:, 3], ACT.Gelu_apprx_tanh)\
                    .then_inc(actA.sem, actA.did("gu"))
                act.wait_ge(dveA.sem, dveA.at("o1", p))
                act.activation(cathl[:, bass.ds(p * 2 + 8, 2), 0, :], obuf[:], ACT.Copy)\
                    .then_inc(actA.sem, actA.did("cat"))

            for j in range(4):
                s = S_SGU + j
                if j == 0:
                    rstd(actG, ("ln", "rs"), dveG, "ms", small[:, RSX:RSX + 2])
                cast(act, s + 1, (0, 1, 2))
                take_lo(act, s, j % 2)
                cast(act, s + 1, (3,))
                act.wait_ge(strip_out, s + 1)
                act.activation(sgz[:], Z[:, j], ACT.Sigmoid).then_inc(actG.sem, actG.did(f"sg{j}"))
                if j >= 1:
                    act.wait_ge(dveG.sem, dveG.at(f"w{j - 1}"))
                    act.activation(cathl[:, 2 * j - 2:2 * j, 0, :], obuf[:], ACT.Copy)\
                        .then_inc(actG.sem, actG.did(f"c{j}"))
            act.wait_ge(dveG.sem, dveG.at("w3"))
            act.activation(cathl[:, 6:8, 0, :], obuf[:], ACT.Copy).then_inc(actG.sem, actG.did("c4"))

            act.preload_act_table_set(LN_EXP)
            with act.Fori(0, 4) as p:
                for j in range(2):
                    s = p * 2 + (S_OUT0 + j)
                    cast(act, s + 1, (0, 1, 2))
                    take_lo(act, s, j)
                    cast(act, s + 1, (3,))
                    act.wait_ge(dveO.sem, dveO.at("xa" if j == 0 else "xb", p))
                    act.activation(sq, xT[:, bass.ds(p * 4 + 2 * j, 2), :], ACT.Square)\
                        .then_inc(actO.sem, actO.did("sqa" if j == 0 else "sqb"))
            rstd(actR, ("ln", "rs"), dveR, "ms", hRS[:, 0:T])
            xhi(1)

            act.preload_act_table_set("sigmoid_and_others")
            cast(act, S_HGRN + 1, (0, 1, 2))
            with act.Fori(0, 8) as i:
                s0 = i * 4 + S_HGRN
                take_lo(act, s0, 0)
                cast(act, s0 + 1, (3,))
                act.wait_ge(strip_out, s0 + 1)
                act.activation(hF, Z[:, 0].rearrange("p a n -> p (a n)"), ACT.Sigmoid).then_inc(actH.sem, actH.did("sf"))
                act.preload_act_table_set(LN_EXP)
                act.wait_ge(dveH.sem, dveH.at("f1", i))
                act.activation(hG, hF, ACT.Ln).then_inc(actH.sem, actH.did("g"))
                cast(act, s0 + 2, (0, 1))
                act.wait_ge(peH.sem, peH.at("gT", i))
                act.activation(hGN, px[:, 0, :], ACT.Copy).then_inc(actH.sem, actH.did("gn"))
                cast(act, s0 + 2, (2, 3))
                act.wait_ge(dveH.sem, dveH.at("d1", i))
                act.activation(hE2, hD1, ACT.Exp, scale=-1.0).then_inc(actH.sem, actH.did("e2"))
                act.wait_ge(actH.sem, actH.at("e2", i))
                act.activation(hD1, hD1, ACT.Exp).then_inc(actH.sem, actH.did("e1"))
                act.activation(hE3, hGS, ACT.Exp).then_inc(actH.sem, actH.did("e3"))
                act.wait_ge(dveH.sem, dveH.at("d2", i))
                act.activation(hD2, hD2, ACT.Exp).then_inc(actH.sem, actH.did("e4"))
                take_lo(act, s0 + 1, 1)
                cast(act, s0 + 3, (0, 1, 2))
                act.wait_ge(peH.sem, peH.at("ksT", i))
                act.activation(hKN, px[:, 3, :], ACT.Copy).then_inc(actH.sem, actH.did("kn"))
                take_lo(act, s0 + 2, 0)
                cast(act, s0 + 3, (3,))
                cast(act, s0 + 4, (0, 1, 2))
                act.wait_ge(peH.sem, peH.at("o", i))
                act.activation(hSQ, px[:, 2, :], ACT.Square).then_inc(actH.sem, actH.did("sq"))
                take_lo(act, s0 + 3, 1)
                cast(act, s0 + 4, (3,))
                rstd(actH, ("ln", "rs"), dveH, "ms", hRS, i=i)
                act.wait_ge(strip_out, s0 + 4)
                act.activation(hSG, Z[:, 3].rearrange("p a n -> p (a n)"), ACT.Sigmoid).then_inc(actH.sem, actH.did("sg"))
                cast(act, s0 + 5, (0,))
                act.wait_ge(dveH.sem, dveH.at("o2", i))
                act.activation(cathl[:, bass.ds(i * 2, 2), 0, :], hO.rearrange("p (a n) -> p a n", a=2), ACT.Copy)\
                    .then_inc(actH.sem, actH.did("cat"))
                cast(act, s0 + 5, (1, 2))

            def out1(p, j, last=False, first=False):
                s = p * 2 + (S_OUT1 + j)
                if not last:
                    cast(act, s + 1, () if first else (0, 1, 2))
                take_lo(act, s, j)
                if not last:
                    cast(act, s + 1, (3,))

            for j in range(2):
                out1(0, j, first=j == 0)
            with act.Fori(1, 3) as p:
                for j in range(2):
                    out1(p, j)
            for j in range(2):
                out1(3, j, last=j == 1)

        def lows(dve, s, qs):
            for q in qs:
                dve.wait_ge(hi_done, s * 4 + (q + 1))
                pooled = isinstance(s, int) and s == 1 and q == 0
                dve.tensor_tensor(whl[:, q, :, 1, :], raw[:, q], whl[:, q, :, 0, :].bitcast(F32), ALU.subtract)\
                    .then_inc(lo_done, NQ + 1 if pooled else 1)

        def take(dve, s, par, dst, n=1, w=SW):
            dve.wait_ge(lo_out, s + 1)
            dve.tensor_tensor(dst, pp[:, 2 * par:2 * par + 2, 0:w], tmp[:, par, :, 0:w], ALU.add)\
                .then_inc(strip_out, n)

        @block.vector
        def _(dve):
            def take_x(b):
                dve.wait_ge(pe0.sem, pe0.at(f"xT{b}"))
                dve.tensor_copy(xT[:, 2 * b:2 * b + 2, :], (pp if b < 4 else px)[:, b % 4, :]
                                .rearrange("p (a n) -> p a n", a=2)).then_inc(dve0.sem, dve0.did(f"xT{b}"))

            take_x(1)
            dve.wait_ge(act0.sem, act0.at("ss1"))
            dve.tensor_scalar(small[:, SSX:SSX + 2], small[:, SSX:SSX + 2], 1.0 / D, EPS, ALU.mult, ALU.add)\
                .then_inc(dve0.sem, dve0.did("ms"))
            for b in (3, 5, 7):
                take_x(b)
            dve.wait_ge(act0.sem, act0.at("rs"))
            for a in range(TT):
                dve.tensor_scalar(tmp[:, 0, 0, a * P:(a + 1) * P], ident[:], small[:, RSX + a:RSX + a + 1], None,
                                  ALU.mult).then_inc(dve0.sem, dve0.did(f"diag{a}"))
            dve.wait_ge(pe0.sem, pe0.at("gT"))
            dve.tensor_copy(vT[:, V_N0:V_N0 + KT], px[:, 3, 0:KT]).then_inc(dve0.sem, dve0.did("gT"))
            dve.tensor_copy(tmp[:, 1, 0, :], pp[:, 1, 0:T]).then_inc(dve0.sem, dve0.did("rsb"))
            dve.wait_ge(dve0.sem, dve0.at("rsb"))
            dve.wait_ge(act0.sem, act0.at("xT6"))

            def norm(layer, vcol, rsb):
                for c in range(4):
                    for j in range(KQ):
                        k = KQ * c + j
                        dve.scalar_tensor_tensor(xn[:, c, j, :], xT[:, k, :], vT[:, vcol + k:vcol + k + 1], rsb,
                                                 ALU.mult, ALU.mult).then_inc(xn_done, 1)
                    if c == 1:
                        lo_part(dve, layer, 0)
                lo_part(dve, layer, 2)
                lo_part(dve, layer, 3)

            norm(0, V_N0, tmp[:, 1, 0, :])
            def side_inputs():
                dve.wait_ge(act0.sem, act0.at("wg"))
                dve.tensor_tensor(wghl[:, :, 1, :], wg[:], wghl[:, :, 0, :].bitcast(F32), ALU.subtract)\
                    .then_inc(dve0.sem, dve0.did("wg"))
                la, lb = vT[:, V_LB:V_LB + 16], vT[:, V_LB + 16:V_LB + 32]

                def lbstep(name, o, a, b, op):
                    dve.tensor_tensor(o, a, b, op).then_inc(dve0.sem, dve0.did(name))
                    dve.wait_ge(dve0.sem, dve0.at(name))

                lbstep("lbm", ltmp[0], la, lb, ALU.max)
                lbstep("lba", ltmp[1], la, ltmp[0], ALU.subtract)
                lbstep("lbb", ltmp[2], lb, ltmp[0], ALU.subtract)
                dve.wait_ge(act0.sem, act0.at("lbe1"))
                lbstep("lbs", ltmp[3], ltmp[1], ltmp[2], ALU.add)
                dve.reciprocal(ltmp[3], ltmp[3]).then_inc(dve0.sem, dve0.did("lbr"))
                dve.wait_ge(dve0.sem, dve0.at("lbr"))
                lbstep("lbp0", ltmp[1], ltmp[1], ltmp[3], ALU.mult)
                lbstep("lbp1", ltmp[2], ltmp[2], ltmp[3], ALU.mult)
                lbstep("lbc", ltmp[4], ltmp[1], ltmp[2], ALU.add)
                lbstep("lb", small[:, LB:LB + 16], ltmp[4], ltmp[1], ALU.subtract)
                dve.tensor_scalar(small[:, OMLB:OMLB + 16], small[:, LB:LB + 16], -1.0, 1.0, ALU.mult, ALU.add)\
                    .then_inc(dve0.sem, dve0.did("omlb"))

            def take_spatial_weights():
                dve.wait_ge(pool0.sem, pool0.at("zw"))
                for b in range(2):
                    dve.wait_ge(pe0.sem, pe0.at(f"wsT{b}"))
                    dve.copy_predicated(w_sT[:, 4 * b:4 * b + 4, :], tri_i[:].unsqueeze(1).broadcast_to([P, 4, P]),
                                        px[:, b, :].rearrange("p (a n) -> p a n", a=4))\
                        .then_inc(dve0.sem, dve0.did(f"wsT{b}"))

            def take_vectors():
                dve.wait_ge(pe0.sem, pe0.at("posT"))
                dve.tensor_copy(vT[:, KT:NV], px[:, 3, KT:NV]).then_inc(dve0.sem, dve0.did("vT"))
                dve.tensor_copy(posT[:], px[:, 3, 128:128 + 2 * NL]).then_inc(dve0.sem, dve0.did("posT"))
                dve.wait_ge(dve0.sem, dve0.at("posT"))
                dve.tensor_scalar(small[:, KGQ:KGQ + 3], vT[:, V_KG:V_KG + 3], vT[:, V_QG:V_QG + 1], None, ALU.mult)\
                    .then_inc(dve0.sem, dve0.did("gain"))

            def key_norm(n, kz, s):
                k4 = kz.rearrange("p a (h d) -> p (a h) d", h=2)
                sq4 = scr.rearrange("p (a d) -> p a d", a=4)
                dve.wait_ge(strip_out, s + 1)
                dve.wait_ge(pool0.sem, pool0.at("df"))
                dve.tensor_tensor(sq4, k4, k4, ALU.mult).then_inc(dveP.sem, dveP.did(f"sq{n}"))
                dve.wait_ge(dveP.sem, dveP.at(f"sq{n}"))
                dve.tensor_reduce(small[:, KSS:KSS + 4], sq4, AX.X, ALU.add).then_inc(dveP.sem, dveP.did(f"ss{n}"))
                dve.wait_ge(dveP.sem, dveP.at(f"ss{n}"))
                dve.tensor_scalar(small[:, KRS:KRS + 4], small[:, KSS:KSS + 4], 1.0 / HD, EPS, ALU.mult, ALU.add)\
                    .then_inc(dveP.sem, dveP.did(f"ms{n}"))
                dve.wait_ge(actP.sem, actP.at(f"rs{n}"))
                for m in range(4):
                    dve.tensor_scalar(k4[:, m, :], k4[:, m, :], small[:, KRS + m:KRS + m + 1], None, ALU.mult)\
                        .then_inc(dveP.sem, dveP.did(f"k{n}{m}"))
                dve.wait_ge(peP.sem, peP.at(f"kT{n}"))
                dve.tensor_scalar(keysT[:, :, n * T:(n + 1) * T], px[:, n, :].rearrange("p (h t) -> p h t", h=2),
                                  small[:, KGQ + 1 + n:KGQ + 2 + n], None, ALU.mult)\
                    .then_inc(dveP.sem, dveP.did(f"kT{n}"))

            kph = [cathl[:, 4 * i:4 * i + 4].rearrange("p k a n -> p (k a n)")[:, 0:NL * 2 * CW]
                   .rearrange("p (l a n) -> p l a n", l=NL, a=2) for i in range(2)]
            kc = scr[0:NC, 256:512].rearrange("p (h d) -> p h d", h=2)

            def compressed_rms():
                dve.wait_ge(peP.sem, peP.at("ck1"))
                dve.tensor_copy(kc, px[0:NC, 2, 0:2 * HD].rearrange("p (h d) -> p h d", h=2))\
                    .then_inc(dveP.sem, dveP.did("kc"))
                dve.wait_ge(dveP.sem, dveP.at("kc"))
                ksq = Z[0:NC, 2, :, 0:HD]
                dve.tensor_tensor(ksq, kc, kc, ALU.mult).then_inc(dveP.sem, dveP.did("sqc"))
                dve.wait_ge(dveP.sem, dveP.at("sqc"))
                dve.tensor_reduce(small[0:NC, KSS:KSS + 2], ksq, AX.X, ALU.add).then_inc(dveP.sem, dveP.did("ssc"))
                dve.wait_ge(dveP.sem, dveP.at("ssc"))
                dve.tensor_scalar(small[0:NC, KRS:KRS + 2], small[0:NC, KSS:KSS + 2], 1.0 / HD, EPS, ALU.mult, ALU.add)\
                    .then_inc(dveP.sem, dveP.did("msc"))

            def compressed_norm():
                dve.wait_ge(actP.sem, actP.at("rsc"))
                for h in range(2):
                    dve.tensor_scalar(kc[:, h, :], kc[:, h, :], small[0:NC, KRS + h:KRS + h + 1], None, ALU.mult)\
                        .then_inc(dveP.sem, dveP.did(f"kn{h}"))

            def take_compressed():
                dve.wait_ge(peP.sem, peP.at("kcT"))
                dve.tensor_scalar(keysT[:, :, 2 * T:2 * T + NC], px[:, 1, 0:2 * 16].rearrange("p (h n) -> p h n", h=2)
                                  [:, :, 0:NC], small[:, KGQ:KGQ + 1], None, ALU.mult)\
                    .then_inc(dveP.sem, dveP.did("kcT"))
                dve.wait_ge(peP.sem, peP.at("cv1"))
                dve.tensor_copy(vcmp[0:NC], px[0:NC, 3, 0:2 * HD].rearrange("p (h d) -> p h d", h=2))\
                    .then_inc(dveP.sem, dveP.did("vc"))

            kpos4 = kpos.rearrange("p (a b h n) -> p a b h n", a=2, b=16, h=2)
            for s in range(S_PRE, S_ATT):
                lows(dve, s + 1, (0,))
                if s in (4, 6):
                    i = (s - 4) // 2
                    dve.wait_ge(peP.sem, peP.at(("fk", "fv")[i]))
                    dve.tensor_copy(Z[:, i, :, 0:CW], px[:, 3, 256 + 64 * i:256 + 64 * i + 64]
                                    .rearrange("p (g n) -> p g n", g=2)[:, :, 0:CW]).then_inc(strip_out, 2)
                if s == 0:
                    take_vectors()
                if s == 6:
                    compressed_rms()
                lows(dve, s + 1, (1,))
                if s == 6:
                    compressed_norm()
                lows(dve, s + 1, (2,))
                if 2 <= s <= 5:
                    lows(dve, s + 1, (3,))
                    if s == 3:
                        side_inputs()
                    continue
                if s >= 8:
                    take(dve, s, s % 2, vals[:, s - 8])
                else:
                    take(dve, s, s % 2, Z[:, s % 4])
                lows(dve, s + 1, (3,))
                if s in (0, 1):
                    dve.wait_ge(strip_out, s + 1)
                    if s == 1:
                        dve.wait_ge(dveP.sem, dveP.at("kpl0"))
                        dve.wait_ge(actP.sem, actP.at("kp0"))
                    for n, (a, h) in enumerate(((0, 0), (0, 1), (1, 0), (1, 1))):
                        tok = Z[:, s, h, :].rearrange("p (m b) -> p b m", b=16)[:, :, a:a + NC]
                        pos = posT[:, s * NL + 16 * a:s * NL + 16 * a + 16].unsqueeze(2).broadcast_to([P, 16, NC])
                        dve.tensor_tensor(kpos4[:, a, :, h, :], tok, pos, ALU.add)\
                            .then_inc(dveP.sem, dveP.did(f"kp{'abcd'[n]}{s}"))
                    dve.wait_ge(actP.sem, actP.at(f"kp{s}"))
                    dve.tensor_tensor(kph[s][:, :, 1, :], kpos.rearrange("p (l n) -> p l n", l=NL),
                                      kph[s][:, :, 0, :].bitcast(F32), ALU.subtract)\
                        .then_inc(dveP.sem, dveP.did(f"kpl{s}"))
                if s == 1:
                    take_spatial_weights()
                if s == 6:
                    take_compressed()
                if s in (6, 7):
                    key_norm(s - 6, Z[:, s % 4], s)
                if s == 8:
                    dve.wait_ge(actP.sem, actP.at("gc"))
                    dve.tensor_tensor(scr[:, 48:96].rearrange("p (a n) -> p a n", a=2),
                                      px[:, 3, 0:128].rearrange("p (a n) -> p a n", a=2)[:, :, 0:NG],
                                      scr[:, 0:48].rearrange("p (a n) -> p a n", a=2), ALU.add)\
                        .then_inc(dveP.sem, dveP.did("ga"))
                    dve.wait_ge(actP.sem, actP.at("gs"))
                    dve.tensor_copy(scr[:, 96:97], scr[:, 48:49]).then_inc(dveP.sem, dveP.did("gb"))
                    for r, (tile, br) in enumerate(((0, 1), (0, 2), (1, 1), (1, 2), (0, 0), (1, 0))):
                        dve.tensor_copy(small[:, GTAB:GTAB + 48].rearrange("p (h r) -> p h r", r=6)[:, :, r],
                                        scr[:, 48 + tile * NG + br * 8:48 + tile * NG + br * 8 + 8])\
                            .then_inc(dveP.sem, dveP.did(f"gt{r}"))
            with dve.Fori(0, 4) as p:
                s0 = p * 4 + S_ATT

                def scores(a):
                    dve.wait_ge(peA.sem, peA.at(f"s{a}", p))
                    dve.wait_ge(actA.sem, actA.at("rq", p))
                    dve.wait_ge(poolA.sem, poolA.at(f"b{a}", p))
                    if a == 1:
                        dve.wait_ge(peA.sem, peA.at("t0", p))
                    for n, (lo, hi, tile, ps, bl, bh) in enumerate((
                            (0, 256, 0, px[:, 0, 0:256], 0, 128), (256, 768, 1, px[:, 1, 0:512], 128, 384),
                            (768, 783, 0, px[:, 0, 256:271], 384, 399), (783, 798, 1, px[:, 0, 271:286], 399, 414))):
                        r = 2 if n < 2 else 1
                        w = bh - bl
                        dve.scalar_tensor_tensor(
                            prob[:, lo:hi].rearrange("p (r n) -> p r n", r=r), ps.rearrange("p (r n) -> p r n", r=r),
                            small[:, RSSQ + 2 * a + tile:RSSQ + 2 * a + tile + 1],
                            bias[:, a, bl:bh].unsqueeze(1).broadcast_to([P, r, w]), ALU.mult, ALU.add)\
                            .then_inc(dveA.sem, dveA.did(f"a{a}{n}"))
                    dve.wait_ge(dveA.sem, dveA.at(f"a{a}3", p))
                    for n, (lo, hi) in enumerate(((0, 256), (256, 768), (768, 798))):
                        dve.tensor_reduce(small[:, MX + 2 * n:MX + 2 * n + 2],
                                          prob[:, lo:hi].rearrange("p (r n) -> p r n", r=2), AX.X, ALU.max)\
                            .then_inc(dveA.sem, dveA.did(f"m{a}{n}"))
                    dve.wait_ge(dveA.sem, dveA.at(f"m{a}2", p))
                    dve.tensor_scalar(small[:, NM:NM + 6], small[:, MX:MX + 6], -1.0, 1e20, ALU.mult, ALU.min)\
                        .then_inc(dveA.sem, dveA.did(f"n{a}"))

                def weigh(a):
                    dve.wait_ge(actA.sem, actA.at(f"e{a}5", p))
                    dve.tensor_scalar(small[:, SUMS:SUMS + 6], small[:, SUMS:SUMS + 6], 1e-30, None, ALU.max)\
                        .then_inc(dveA.sem, dveA.did(f"r{a}x"))
                    dve.wait_ge(dveA.sem, dveA.at(f"r{a}x", p))
                    dve.reciprocal(small[:, SUMS:SUMS + 6], small[:, SUMS:SUMS + 6])\
                        .then_inc(dveA.sem, dveA.did(f"r{a}"))
                    dve.wait_ge(dveA.sem, dveA.at(f"r{a}", p))
                    dve.tensor_tensor(small[:, COEF:COEF + 6], small[:, SUMS:SUMS + 6],
                                      small[:, bass.ds(p * 12 + (GTAB + 6 * a), 6)], ALU.mult)\
                        .then_inc(dveA.sem, dveA.did(f"c{a}"))
                    dve.wait_ge(dveA.sem, dveA.at(f"c{a}", p))
                    for n, (lo, hi) in enumerate(((0, 256), (256, 768), (768, 798))):
                        w = (hi - lo) // 2
                        v = prob[:, lo:hi].rearrange("p (r n) -> p r n", r=2)
                        dve.tensor_tensor(v, v, small[:, COEF + 2 * n:COEF + 2 * n + 2].unsqueeze(2)
                                          .broadcast_to([P, 2, w]), ALU.mult)\
                            .then_inc(dveA.sem, dveA.did(f"p{a}{n}"))

                def take_pT(a):
                    dve.wait_ge(peA.sem, peA.at(f"t{a}", p))
                    dve.tensor_copy(probT[:, 1, 0:384], px[:, 3, 0:384]).then_inc(dveA.sem, dveA.did(f"pt{a}"))
                    dve.tensor_copy(probT[0:NC, 1, 384:512], px[0:NC, 3, 384:512])\
                        .then_inc(dveA.sem, dveA.did(f"pd{a}"))

                def gate(a):
                    dve.wait_ge(peA.sem, peA.at(f"o{a}", p))
                    dve.wait_ge(dveA.sem, dveA.at("sz", p))
                    dve.scalar_tensor_tensor(obuf[:, a, :], px[:, 2, 0:T], 0.5, sgz[:, a, :], ALU.mult, ALU.mult)\
                        .then_inc(dveA.sem, dveA.did(f"o{a}"))

                lows(dve, s0 + 1, (0, 1, 2))
                take(dve, s0, 0, Z[:, 0])
                lows(dve, s0 + 1, (3,))
                lows(dve, s0 + 2, (0,))
                dve.wait_ge(peA.sem, peA.at("rms", p))
                dve.tensor_scalar(small[:, RSSQ:RSSQ + 4], px[:, 3, 0:4], 1.0, EPS * HD, ALU.mult, ALU.add)\
                    .then_inc(dveA.sem, dveA.did("ms"))
                lows(dve, s0 + 2, (1,))
                scores(0)
                lows(dve, s0 + 2, (2,))
                weigh(0)
                take(dve, s0 + 1, 1, Z[:, 1])
                lows(dve, s0 + 2, (3,))
                lows(dve, s0 + 3, (0, 1))
                take_pT(0)
                scores(1)
                lows(dve, s0 + 3, (2,))
                weigh(1)
                take(dve, s0 + 2, 0, Z[:, 2])
                dve.wait_ge(actA.sem, actA.at("sg", p))
                dve.scalar_tensor_tensor(sgz[:], sgz[:], 1.0, Z[:, 1], ALU.add, ALU.mult)\
                    .then_inc(dveA.sem, dveA.did("sz"))
                gate(0)
                lows(dve, s0 + 3, (3,))
                lows(dve, s0 + 4, (0, 1))
                take_pT(1)
                lows(dve, s0 + 4, (2,))
                take(dve, s0 + 3, 1, Z[:, 3])
                lows(dve, s0 + 4, (3,))
                gate(1)
                dve.wait_ge(actA.sem, actA.at("cat", p))
                dve.tensor_tensor(cathl[:, bass.ds(p * 2 + 8, 2), 1, :], obuf[:],
                                  cathl[:, bass.ds(p * 2 + 8, 2), 0, :].bitcast(F32), ALU.subtract)\
                    .then_inc(dveA.sem, dveA.did("cat"))

            dve.wait_ge(actA.sem, actA.at("cat", 3))
            st = small[:, BST:BST + 24].rearrange("p (a b c) -> p a b c", a=2, b=2)
            for a in range(TT):
                for b in range(2):
                    dve.bn_stats(st[:, a, b, :], gav[:, a, 512 * b:512 * b + 512])\
                        .then_inc(dveG.sem, dveG.did(f"st{2 * a + b}"))
            dve.wait_ge(dveG.sem, dveG.at("st3"))
            mv = small[:, KSS:KSS + 4].rearrange("p (a n) -> p a n", a=2)
            for a in range(TT):
                dve.bn_aggr(mv[:, a, :], st[:, a].rearrange("p b c -> p (b c)")).then_inc(dveG.sem, dveG.did(f"ag{a}"))
            dve.wait_ge(dveG.sem, dveG.at("ag1"))
            dve.tensor_scalar(small[:, RSX:RSX + 2], mv[:, :, 1], EPS, None, ALU.add)\
                .then_inc(dveG.sem, dveG.did("ms"))
            def gain_or_bias(n):
                for a in range(TT):
                    dve.wait_ge(dveG.sem, dveG.at(f"v{2 * n + a}"))
                    dve.tensor_tensor(gav[:, a, :], gav[:, a, :], lngb[:, n, :], (ALU.mult, ALU.add)[n])\
                        .then_inc(dveG.sem, dveG.did(f"v{2 * n + 2 + a}"))

            def spatial(j):
                dve.wait_ge(peG.sem, peG.at(f"g{j}"))
                if j >= 1:
                    dve.wait_ge(dveG.sem, dveG.at(f"l{j - 1}"))
                dve.tensor_tensor(obuf[:], px[:, j, :].rearrange("p (a n) -> p a n", a=2), gu[:, 2 * j:2 * j + 2, :],
                                  ALU.mult).then_inc(dveG.sem, dveG.did(f"u{j}"))
                dve.wait_ge(dveG.sem, dveG.at(f"u{j}"))
                dve.tensor_tensor(obuf[:], obuf[:], Z[:, j], ALU.mult).then_inc(dveG.sem, dveG.did(f"w{j}"))
                dve.wait_ge(actG.sem, actG.at(f"c{j + 1}"))
                dve.tensor_tensor(cathl[:, 2 * j:2 * j + 2, 1, :], obuf[:],
                                  cathl[:, 2 * j:2 * j + 2, 0, :].bitcast(F32), ALU.subtract)\
                    .then_inc(dveG.sem, dveG.did(f"l{j}"))

            lows(dve, S_SGU + 1, (0,))
            dve.wait_ge(actG.sem, actG.at("rs"))
            dve.wait_ge(misc_in, 64)
            for a in range(TT):
                dve.tensor_scalar(gav[:, a, :], gav[:, a, :], mv[:, a, 0:1], small[:, RSX + a:RSX + a + 1],
                                  ALU.subtract, ALU.mult).then_inc(dveG.sem, dveG.did(f"v{a}"))
            lows(dve, S_SGU + 1, (1,))
            gain_or_bias(0)
            lows(dve, S_SGU + 1, (2,))
            for j in range(4):
                s = S_SGU + j
                if j >= 1:
                    lows(dve, s + 1, (0, 1, 2))
                take(dve, s, j % 2, Z[:, j])
                lows(dve, s + 1, (3,))
                if j == 0:
                    gain_or_bias(1)
                dve.wait_ge(actG.sem, actG.at(f"sg{j}"))
                dve.tensor_tensor(Z[:, j], Z[:, j], sgz[:], ALU.mult).then_inc(dveG.sem, dveG.did(f"z{j}"))
                dve.wait_ge(dveG.sem, dveG.at(f"z{j}"))
                if j >= 1:
                    spatial(j - 1)
            spatial(3)

            dve.memset(acc, 0.0).then_inc(dveG.sem, dveG.did("acc"))
            dve.wait_ge(dveG.sem, dveG.at("acc"))
            with dve.Fori(0, 4) as p:
                for j in range(2):
                    s = p * 2 + (S_OUT0 + j)
                    lows(dve, s + 1, (0, 1, 2))
                    take(dve, s, j, Z[:, j])
                    dve.wait_ge(strip_out, s + 1)
                    r = xT[:, bass.ds(p * 4 + 2 * j, 2), :]
                    dve.tensor_tensor(r, r, Z[:, j], ALU.add).then_inc(dveO.sem, dveO.did("xa" if j == 0 else "xb"))
                    lows(dve, s + 1, (3,))
                    dve.wait_ge(actO.sem, actO.at("sqa" if j == 0 else "sqb", p))
                    dve.tensor_tensor(acc, acc, sq, ALU.add).then_inc(dveO.sem, dveO.did("aa" if j == 0 else "ab"))
            dve.wait_ge(peR.sem, peR.at("ss"))
            dve.tensor_scalar(hRS[:, 0:T], px[:, 0, 0:T], 1.0 / D, EPS, ALU.mult, ALU.add)\
                .then_inc(dveR.sem, dveR.did("ms"))
            dve.wait_ge(actR.sem, actR.at("rs"))
            norm(1, V_N1, hRS[:, 0:T])
            dve.memset(hAT, 0.0).then_inc(dveR.sem, dveR.did("at0"))
            dve.wait_ge(dveR.sem, dveR.at("at0"))

            def chunks(ap):
                return ap.rearrange("p (c t) -> p c t", t=CH)

            lows(dve, S_HGRN + 1, (0, 1, 2))
            with dve.Fori(0, 8) as i:
                s0 = i * 4 + S_HGRN
                take(dve, s0, 0, Z[:, 0])
                lows(dve, s0 + 1, (3,))
                dve.wait_ge(actH.sem, actH.at("sf", i))
                for h in range(2):
                    dve.tensor_scalar(hF[:, h * T:(h + 1) * T], hF[:, h * T:(h + 1) * T],
                                      small[:, bass.ds(i * 2 + (OMLB + h), 1)], small[:, bass.ds(i * 2 + (LB + h), 1)],
                                      ALU.mult, ALU.add).then_inc(dveH.sem, dveH.did(f"f{h}"))
                dve.wait_ge(dveH.sem, dveH.at("f1", i))
                dve.tensor_scalar(hK, hF, -1.0, 1.0, ALU.mult, ALU.add).then_inc(dveH.sem, dveH.did("k"))
                lows(dve, s0 + 2, (0, 1, 2))
                dve.wait_ge(peH.sem, peH.at("G", i))
                dve.tensor_copy(hGS, px[:, 1, :]).then_inc(dveH.sem, dveH.did("gs"))
                dve.wait_ge(dveH.sem, dveH.at("gs", i))
                dve.tensor_tensor(chunks(hD1), chunks(hGS), chunks(hGS)[:, :, CH // 2 - 1:CH // 2]
                                  .broadcast_to([P, 8, CH]), ALU.subtract).then_inc(dveH.sem, dveH.did("d1"))
                dve.tensor_tensor(chunks(hD2), chunks(hGS)[:, :, CH - 1:CH].broadcast_to([P, 8, CH]), chunks(hGS),
                                  ALU.subtract).then_inc(dveH.sem, dveH.did("d2"))
                lows(dve, s0 + 2, (3,))
                take(dve, s0 + 1, 1, Z[:, 1])
                dve.wait_ge(actH.sem, actH.at("e1", i))
                dve.tensor_tensor(hKE, hK, hE2, ALU.mult).then_inc(dveH.sem, dveH.did("kt"))
                dve.wait_ge(strip_out, s0 + 2)
                dve.tensor_tensor(hQE, Z[:, 1].rearrange("p a n -> p (a n)"), hD1, ALU.mult)\
                    .then_inc(dveH.sem, dveH.did("qe"))
                lows(dve, s0 + 3, (0, 1, 2))
                dve.wait_ge(peH.sem, peH.at("at", i))
                dve.sem_inc(seen, 1)
                dve.copy_predicated(hAT.rearrange("p (b t) -> p b t", b=4),
                                    tri64_i[:].unsqueeze(1).broadcast_to([P, 4, P]),
                                    px[:, 2, :].rearrange("p (b t) -> p b t", b=4))\
                    .then_inc(dveH.sem, dveH.did("at"))
                take(dve, s0 + 2, 0, Z[:, 2])
                lows(dve, s0 + 3, (3,))
                lows(dve, s0 + 4, (0,))
                dve.wait_ge(peH.sem, peH.at("kv", i))
                for h in range(2):
                    dve.tensor_copy(hST[:, h, 0, :], kv_at(h, 0)).then_inc(dveH.sem, dveH.did(f"s1{h}"))
                for c in range(1, 3):
                    for h in range(2):
                        dve.wait_ge(dveH.sem, dveH.at(f"s{c}{h}", i))
                        end = h * T + c * CH + CH - 1
                        dve.scalar_tensor_tensor(hST[:, h, c, :], hST[:, h, c - 1, :], hE3[:, end:end + 1],
                                                 kv_at(h, c), ALU.mult, ALU.add)\
                            .then_inc(dveH.sem, dveH.did(f"s{c + 1}{h}"))
                lows(dve, s0 + 4, (1, 2))
                take(dve, s0 + 3, 1, Z[:, 3])
                dve.wait_ge(peH.sem, peH.at("ss", i))
                dve.tensor_scalar(hRS, px[:, 3, :], 1.0 / HD, EPS, ALU.mult, ALU.add)\
                    .then_inc(dveH.sem, dveH.did("ms"))
                lows(dve, s0 + 4, (3,))
                dve.wait_ge(actH.sem, actH.at("rs", i))
                dve.scalar_tensor_tensor(hO, px[:, 2, :], vT[:, V_OG:V_OG + 1], hRS, ALU.mult, ALU.mult)\
                    .then_inc(dveH.sem, dveH.did("o1"))
                dve.wait_ge(dveH.sem, dveH.at("o1", i))
                dve.wait_ge(poolH.sem, poolH.at("zs", i))
                dve.tensor_tensor(hO, hO, hZS, ALU.mult).then_inc(dveH.sem, dveH.did("o2"))
                lows(dve, s0 + 5, (0,))
                dve.wait_ge(actH.sem, actH.at("cat", i))
                dve.tensor_tensor(cathl[:, bass.ds(i * 2, 2), 1, :], hO.rearrange("p (a n) -> p a n", a=2),
                                  cathl[:, bass.ds(i * 2, 2), 0, :].bitcast(F32), ALU.subtract)\
                    .then_inc(dveH.sem, dveH.did("lo"))
                lows(dve, s0 + 5, (1, 2))

            def out1(p, j, last=False, first=False):
                s = p * 2 + (S_OUT1 + j)
                if not last:
                    lows(dve, s + 1, () if first else (0, 1, 2))
                if not (isinstance(p, int) and p == 0):
                    dve.wait_ge(y_out[j], p * 16)
                take(dve, s, j, Z[:, j])
                if not last:
                    lows(dve, s + 1, (3,))

            for j in range(2):
                out1(0, j, first=j == 0)
            with dve.Fori(1, 3) as p:
                for j in range(2):
                    out1(p, j)
            for j in range(2):
                out1(3, j, last=j == 1)

        @block.tensor
        def _(pe):
            def strip(s, par, kind, xs, order=None, first=False, hooks=None, late=None, rhs=None):
                if not first:
                    pe.wait_ge(strip_out, s - 1)
                for q in range(NQ):
                    if isinstance(s, int) and s == 0:
                        pe.wait_ge(lo_pool, q + 1)
                    else:
                        pe.wait_ge(lo_done, s * 4 + (q + 1))
                    for g in range(2):
                        bank = pp[:, 2 * par + g, :]
                        if late and q == NQ - 1:
                            late(g)
                        for k in range(KQ):
                            kt = (order or (lambda n: n))(KQ * q + k)
                            begin, end = q == 0 and k == 0, q == NQ - 1 and k == KQ - 1
                            if kind == "B":
                                full = (bank, whl[:, q, k, 0, g * P:(g + 1) * P], xs[:, kt, :, :])
                                half = (bank[:, T:], whl[:, q, k, 1, g * P:(g + 1) * P], xs[:, kt, 0, :])
                            else:
                                full = (bank, xs[:, kt, 0, g * P:(g + 1) * P], whl[:, q, k, :, :])
                                half = (bank[:, T:], xs[:, kt, 1, g * P:(g + 1) * P], whl[:, q, k, 0, :])
                            if end:
                                pe.matmul(*half, start=False, stop=False)
                                mm = pe.matmul(*full, start=False, stop=True)
                            else:
                                pe.matmul(*full, start=begin, stop=False)
                                mm = pe.matmul(*half, start=False, stop=False)
                    mm.then_inc(pe_q, 1)
                    if hooks and q in hooks:
                        hooks[q]()

            pe.wait_ge(pool0.sem, pool0.at("ident"))
            for a in range(TT):
                pe.wait_ge(x_in[a], 32)
                for b in range(8):
                    for k in range(2):
                        kt = 2 * b + k
                        mm = pe.transpose((pp if b < 4 else px)[:, b % 4, k * T + a * P:k * T + (a + 1) * P],
                                          xnat[:, a, kt * P:(kt + 1) * P], ident[:])
                    if a == TT - 1:
                        mm.then_inc(pe0.sem, pe0.did(f"xT{b}"))
            pe.wait_ge(dve0.sem, dve0.at("diag1"))
            pe.wait_ge(pool0.sem, pool0.at("ms1"))
            pe.matmul(pp[:, 1, 0:T], ones[:], tmp[:, 0, 0, :], start=True, stop=True)\
                .then_inc(pe0.sem, pe0.did("rs"))
            pe.wait_ge(gain_in, 16)
            pe.wait_ge(dve0.sem, dve0.at("xT7"))
            pe.transpose(px[:, 3, 0:KT], vecs[V_N0:V_N0 + KT, :], ident[0:KT, 0:KT]).then_inc(pe0.sem, pe0.did("gT"))
            pe.wait_ge(dve0.sem, dve0.at("rsb"))
            pe.wait_ge(act0.sem, act0.at("xT6"))
            pe.wait_ge(xlo_done, 1)

            def normed(layer):
                return {0: lambda: pe.wait_ge(xlo_pool, layer + 1), 1: lambda: pe.wait_ge(xlo_done, 3 * layer + 2),
                        2: lambda: pe.wait_ge(xlo_done, 3 * layer + 3)}

            def vectors():
                pe.wait_ge(vec_in, 16 * 7)
                pe.transpose(px[:, 3, 0:P], vecs[:], ident[:]).then_inc(pe0.sem, pe0.did("vT"))
                pe.transpose(px[:, 3, P:P + 2 * NL], posr[:], ident[0:2 * NL, 0:2 * NL])\
                    .then_inc(pe0.sem, pe0.did("posT"))

            def spatial_weights():
                pe.wait_ge(sg_in, 16)
                for b in range(2):
                    for g in range(4):
                        mm = pe.transpose(px[:, b, g * P:(g + 1) * P], sgw[:, 4 * b + g, :], ident[:])
                    mm.then_inc(pe0.sem, pe0.did(f"wsT{b}"))

            def key_T(n):
                pe.wait_ge(dve0.sem, dve0.at("wsT1"))
                pe.wait_ge(dveP.sem, dveP.at(f"k{n}3"))
                for a in range(TT):
                    for h in range(2):
                        mm = pe.transpose(px[:, n, h * T + a * P:h * T + (a + 1) * P],
                                          Z[:, 2 + n, a, h * HD:(h + 1) * HD], ident[:])
                mm.then_inc(peP.sem, peP.did(f"kT{n}"))

            def branch_gates():
                pe.wait_ge(dve0.sem, dve0.at("wg"))
                pe.wait_ge(dveP.sem, dveP.at("vc"))
                for a in range(TT):
                    o = px[:, 3, 64 * a:64 * a + 2 * NG]
                    for k in range(KT):
                        full = (o, xhl[:, k, 0, a * P:(a + 1) * P], wghl[:, k, :, :])
                        half = (o[:, NG:], xhl[:, k, 1, a * P:(a + 1) * P], wghl[:, k, 0, :])
                        if k == KT - 1:
                            pe.matmul(*half, start=False, stop=False)
                            mm = pe.matmul(*full, start=False, stop=True)
                        else:
                            pe.matmul(*full, start=k == 0, stop=False)
                            pe.matmul(*half, start=False, stop=False)
                mm.then_inc(peP.sem, peP.did("gates"))

            def compress_out(i):
                pe.wait_ge(actP.sem, actP.at(f"h{'kv'[i]}1"))
                pe.wait_ge(misc_in, 64)
                for h in range(2):
                    for g in range(2):
                        c = 128 + 64 * i + CW * g + NC * h
                        mm = pe.matmul(px[0:NC, 2 + i, h * HD:(h + 1) * HD], scr[:, c:c + NC], w2[:, i, g, :],
                                       start=g == 0, stop=g == 1)
                    mm.then_inc(peP.sem, peP.did(f"c{'kv'[i]}{h}"))

            def fold_hidden(i):
                pe.wait_ge(pool0.sem, pool0.at("fold1"))
                pe.wait_ge(lo_out, 4 + 2 * i)
                for g in range(2):
                    for n in range(2):
                        c = 256 + 64 * i + 32 * g
                        mm = pe.matmul(px[:, 3, c:c + CW], tmp[0:2 * CW, i, n, g * P:(g + 1) * P], fold[:],
                                       start=n == 0, stop=n == 1)
                mm.then_inc(peP.sem, peP.did(("fk", "fv")[i]))

            def compressed_key_T():
                pe.wait_ge(dveP.sem, dveP.at("kn1"))
                for h in range(2):
                    mm = pe.transpose(px[:, 1, 16 * h:16 * h + NC], scr[0:NC, 256 + h * HD:256 + (h + 1) * HD],
                                      ident[0:NC, 0:NC])
                mm.then_inc(peP.sem, peP.did("kcT"))

            first = normed(0)
            strip(0, 0, "B", xhl, first=True, hooks={0: lambda: (first[0](), vectors()), 1: first[1], 2: first[2]})
            strip(1, 1, "B", xhl, first=True, hooks={3: spatial_weights})
            kph = [cathl[:, 4 * i:4 * i + 4].rearrange("p k a n -> p (k a n)")[:, 0:NL * 2 * CW]
                   .rearrange("p (l a n) -> p l a n", l=NL, a=2) for i in range(2)]
            for i in range(2):
                pe.wait_ge(dveP.sem, dveP.at(f"kpl{i}"))
                for half in range(2):
                    s = 2 + 2 * i + half
                    if half == 0:
                        pe.wait_ge(strip_out, 1)
                    for q in range(NQ):
                        pe.wait_ge(lo_done, s * 4 + q + 1)
                        for k in range(KQ):
                            li = 16 * half + KQ * q + k
                            mm = pe.matmul(pp[0:2 * CW, i, :], kph[i][:, li].rearrange("p a n -> p (a n)"),
                                           whl[:, q, k, :, :], start=li == 0, stop=li == NL - 1)
                        mm.then_inc(pe_q, 1)
                        if i == 1 and half == 0 and q == 1:
                            fold_hidden(0)
            pe.wait_ge(lo_out, 6)
            strip(6, 0, "A", xhl, first=True, hooks={0: lambda: (fold_hidden(1), compress_out(0)),
                                                     2: lambda: compress_out(1), 3: compressed_key_T})
            strip(7, 1, "A", xhl, hooks={2: lambda: key_T(0)})
            strip(8, 0, "A", xhl, hooks={2: lambda: key_T(1), 3: branch_gates})
            strip(9, 1, "A", xhl)
            pe.wait_ge(dveP.sem, dveP.at("gt5"))

            for kv in range(2):
                with pe.Fori(0, 2) as r:
                    p = r + 2 * kv
                    s0 = p * 4 + S_ATT
                    kT = keysT[:, kv, :]

                    def rms():
                        pe.wait_ge(actA.sem, actA.at("sq", p))
                        for h in range(2):
                            for a in range(TT):
                                mm = pe.matmul(px[:, 3, 2 * h + a:2 * h + a + 1], obuf[:, h, a * P:(a + 1) * P],
                                               ones[:, 0:1], start=True, stop=True)
                        mm.then_inc(peA.sem, peA.did("rms"))

                    def score(h):
                        if h == 1:
                            pe.wait_ge(dveA.sem, dveA.at("a03", p))
                        q0, q1 = Z[:, 0, h, 0:P], Z[:, 0, h, P:T]
                        pe.matmul(px[:, 0, 0:T].rearrange("p (b n) -> p b n", b=2), q0,
                                  kT[:, 0:2 * T].rearrange("p (b n) -> p b n", b=2)[:, :, 0:P], start=True, stop=True)
                        pe.matmul(px[:, 1, 0:2 * T], q1, kT[:, 0:2 * T], start=True, stop=True)
                        pe.matmul(px[:, 0, T:T + NC], q0, kT[:, 2 * T:2 * T + NC], start=True, stop=True)
                        pe.matmul(px[:, 0, T + NC:T + 2 * NC], q1, kT[:, 2 * T:2 * T + NC], start=True, stop=True)\
                            .then_inc(peA.sem, peA.did(f"s{h}"))

                    def turn(h):
                        pe.wait_ge(dveA.sem, dveA.at(f"p{h}2", p))
                        if h == 1:
                            pe.wait_ge(dveA.sem, dveA.at("o0", p))
                        for b, (t0, tile1) in enumerate(((0, 256), (128, 512))):
                            for n, c in enumerate((t0, tile1, tile1 + P)):
                                pe.transpose(px[:, 2 + b, n * P:(n + 1) * P], prob[:, c:c + P], ident[:])
                        pe.transpose(px[0:NC, 2, 384:512], prob[:, 768:783], ident[:])
                        pe.transpose(px[0:NC, 3, 384:512], prob[:, 783:798], ident[:])\
                            .then_inc(peA.sem, peA.did(f"t{h}"))

                    def mix(h):
                        pe.wait_ge(actA.sem, actA.at(f"pc{h}", p))
                        pe.wait_ge(dveA.sem, dveA.at(f"pd{h}", p))
                        hv = slice(kv * HD, (kv + 1) * HD)
                        for tile in range(TT):
                            terms = []
                            for b in range(2):
                                if tile == 0:
                                    terms.append((vals[:, b, 0, hv], probT[:, b, 0:P]))
                                else:
                                    terms.append((vals[:, b, 0, hv], probT[:, b, P:2 * P]))
                                    terms.append((vals[:, b, 1, hv], probT[:, b, 2 * P:3 * P]))
                            terms.append((vcmp[0:NC, kv, :], probT[0:NC, tile, 384:512]))
                            for n, (v, pr) in enumerate(terms):
                                mm = pe.matmul(px[:, 2, tile * P:(tile + 1) * P], v, pr, start=n == 0,
                                               stop=n == len(terms) - 1)
                        mm.then_inc(peA.sem, peA.did(f"o{h}"))

                    strip(s0, 0, "B", xhl)
                    strip(s0 + 1, 1, "B", xhl, hooks={1: lambda: (rms(), score(0))})
                    strip(s0 + 2, 0, "A", xhl, hooks={1: lambda: (turn(0), score(1)), 3: lambda: mix(0)})
                    strip(s0 + 3, 1, "B", xhl, hooks={2: lambda: turn(1), 3: lambda: mix(1)})

            def groups(j):
                pe.wait_ge(dveG.sem, dveG.at("v5"))
                pe.wait_ge(misc_in, 64)
                for n in range(2):
                    g = 2 * j + n
                    for a in range(TT):
                        o = px[:, j, n * T + a * P:n * T + (a + 1) * P]
                        pe.matmul(o, gav[:, a, g * P:(g + 1) * P], w_sT[:, g, :], start=True, stop=False)
                        mm = pe.matmul(o, ones[0:1, :], sgub[0:1, g * P:(g + 1) * P], start=False, stop=True)
                mm.then_inc(peG.sem, peG.did(f"g{j}"))

            strip(S_SGU, 0, "B", xhl)
            for j in range(1, 4):
                strip(S_SGU + j, j % 2, "B", xhl, hooks={2: lambda j=j: groups(j - 1)})
            groups(3)

            def swapped(k):
                return (k + KT // 2) % KT

            def wait_cat(name):
                pe.wait_ge(dveG.sem, dveG.at(name))

            pe.wait_ge(dveA.sem, dveA.at("cat", 3))
            strip(S_OUT0, 0, "B", cathl, order=swapped, hooks={1: lambda: wait_cat("l1"), 2: lambda: wait_cat("l3")})
            strip(S_OUT0 + 1, 1, "B", cathl, order=swapped)
            with pe.Fori(1, 4) as p:
                for j in range(2):
                    strip(p * 2 + (S_OUT0 + j), j, "B", cathl, order=swapped)
            pe.wait_ge(dveO.sem, dveO.at("ab", 3))
            for n in range(2):
                mm = pe.matmul(px[:, 0, 0:T], ones[:], acc[:, n * T:(n + 1) * T], start=n == 0, stop=n == 1)
            mm.then_inc(peR.sem, peR.did("ss"))
            pe.wait_ge(xlo_done, 4)

            with pe.Fori(0, 8) as i:
                s0 = i * 4 + S_HGRN

                def turn_g():
                    pe.wait_ge(actH.sem, actH.at("g", i))
                    for b in range(4):
                        mm = pe.transpose(px[:, 0, b * P:(b + 1) * P], hG[:, b * P:(b + 1) * P], ident[:])
                    mm.then_inc(peH.sem, peH.did("gT"))

                def sum_g():
                    pe.wait_ge(actH.sem, actH.at("gn", i))
                    for b in range(4):
                        mm = pe.matmul(px[:, 1, b * P:(b + 1) * P], hGN[:, b * P:(b + 1) * P], tri64[:],
                                       start=True, stop=True)
                    mm.then_inc(peH.sem, peH.did("G"))

                def intra():
                    pe.wait_ge(poolH.sem, poolH.at("ks", i))
                    for b in range(4):
                        mm = pe.transpose(px[:, 3, b * P:(b + 1) * P], hKS[:, b * P:(b + 1) * P], ident[:])
                    mm.then_inc(peH.sem, peH.did("ksT"))
                    pe.wait_ge(dveH.sem, dveH.at("qe", i))
                    for b in range(4):
                        mm = pe.matmul(px[:, 2, b * P:(b + 1) * P], hKE[:, b * P:(b + 1) * P],
                                       hQE[:, b * P:(b + 1) * P], start=True, stop=True)
                    mm.then_inc(peH.sem, peH.did("at"))

                def chunk_kv():
                    pe.wait_ge(actH.sem, actH.at("kn", i))
                    pe.wait_ge(strip_out, s0 + 3)
                    for h in range(2):
                        for c in range(3):
                            r0, a = CH * (c % 2), c // 2
                            b = 2 * h + a
                            mm = pe.matmul(kv_at(h, c), hKN[r0:r0 + CH, b * P:(b + 1) * P],
                                           Z[r0:r0 + CH, 2, a, h * HD:(h + 1) * HD], start=True, stop=True)
                    mm.then_inc(peH.sem, peH.did("kv"))

                def outputs():
                    pe.wait_ge(dveH.sem, dveH.at("s31", i))
                    pe.wait_ge(poolH.sem, poolH.at("qi", i))
                    for h in range(2):
                        for a in range(TT):
                            b = 2 * h + a
                            pe.matmul(px[:, 2, b * P:(b + 1) * P], Z[:, 2, a, h * HD:(h + 1) * HD],
                                      hAT[:, b * P:(b + 1) * P], start=True, stop=False, skip_group_check=True)
                            for c in (1,) if a == 0 else (2, 3):
                                mm = pe.matmul(px[:, 2, h * T + c * CH:h * T + (c + 1) * CH], hST[:, h, c - 1, :],
                                               hQI[:, h * T + c * CH:h * T + (c + 1) * CH], start=False,
                                               stop=c != 2, skip_group_check=True)
                    mm.then_inc(peH.sem, peH.did("o"))

                def squares():
                    pe.wait_ge(actH.sem, actH.at("sq", i))
                    pe.matmul(px[:, 3, :], ones[:], hSQ, start=True, stop=True).then_inc(peH.sem, peH.did("ss"))

                strip(s0, 0, "B", xhl, hooks=normed(1))
                strip(s0 + 1, 1, "B", xhl, hooks={1: turn_g, 2: sum_g})
                strip(s0 + 2, 0, "A", xhl, hooks={1: intra})
                strip(s0 + 3, 1, "B", xhl, hooks={0: chunk_kv, 2: outputs, 3: squares})

            def residual(p, j):
                def late(g):
                    if g == 0:
                        pe.wait_ge(poolR.sem, poolR.at("ra" if j == 0 else "rb", p))
                    for c in range(2):
                        pe.matmul(pp[:, 2 * j + g, c * P:(c + 1) * P], xres[:, j, c, g * P:(g + 1) * P], ident[:],
                                  start=False, stop=False)
                return late

            def last_heads():
                pe.wait_ge(dveH.sem, dveH.at("lo", 7))

            pe.wait_ge(dveH.sem, dveH.at("lo", 6))
            for j in range(2):
                strip(S_OUT1 + j, j, "A", cathl, late=residual(0, j), hooks={2: last_heads} if j == 0 else None)
            with pe.Fori(1, 4) as p:
                for j in range(2):
                    strip(p * 2 + (S_OUT1 + j), j, "A", cathl, late=residual(p, j))


_INS = ['x', 'even_norm', 'even_w_in', 'sgu_ln_g', 'sgu_ln_b', 'sgu_w', 'sgu_b', 'nsa_q_gain', 'nsa_k_gain',
        'cmp_pos', 'cmp_w1', 'cmp_b1', 'cmp_w2', 'even_w_out', 'odd_norm', 'odd_w_in', 'hgrn_lb',
        'hgrn_out_gain', 'odd_w_out']
_ONE = {'even_w_in', 'sgu_w', 'sgu_b', 'nsa_k_gain', 'cmp_pos', 'cmp_w1', 'cmp_b1', 'cmp_w2', 'even_w_out',
        'odd_w_in', 'odd_w_out', 'sgu_ln_g', 'sgu_ln_b'}


def kernel(**inputs):
    import numpy as _np
    import concourse.bacc as _bacc
    from concourse import mybir as _mybir
    from concourse.bass_utils import run_bass_kernel_spmd as _run

    nc = _bacc.Bacc("TRN2", target_bir_lowering=False, num_devices=1)
    arrays, args = {}, []
    for name in _INS:
        a = _np.ascontiguousarray(inputs[name])
        if name in _ONE:
            a = a[0]
        arrays[f"in_{name}"] = a
        args.append(nc.dram_tensor(f"in_{name}", a.shape, _mybir.dt.from_np(a.dtype), kind="ExternalInput").ap())
    out = nc.dram_tensor("out_y", (T, D), F32, kind="ExternalOutput").ap()
    trunk(nc, *args, out)
    r = _run(nc, [arrays], core_ids=[0])
    return r.results[0]["out_y"].reshape(1, T, D)
```

```python
from contextlib import ExitStack

import concourse.bass as bass
from concourse import mybir
from concourse.alu_op_type import AluOpType as ALU

F32 = mybir.dt.float32
F32R = mybir.dt.float32r
I32 = mybir.dt.int32
ACT = mybir.ActivationFunctionType
AX = mybir.AxisListType

P = 128
D = 2048
KT = D // P
T = 256
TT = T // P
SW = 256
NQ = 4
KQ = KT // NQ
HD = 128
A_WIDTH = 1024
B_WIDTH = 1024
KV0 = 3 * A_WIDTH + 2 * B_WIDTH
NG = 24
GATE0 = KV0 + 6 * SW
NL = 32
NC = (T - NL) // 16 + 1
CW = 2 * NC
EPS = 1e-6
BIG = 1e30
CH = 64
LN_EXP = "natural_log_exp_and_others"
ARENA = 14104

S_PRE, S_ATT, S_SGU, S_OUT0, S_HGRN, S_OUT1 = 0, 10, 26, 30, 38, 70

KV_GROUP = {0: 0, 1: 1, 3: 2, 5: 4, 7: 3, 9: 5}
PAR = {0: 0, 1: 1, 3: 0, 5: 1, 7: 0, 9: 1}
COUNT = {0: 1, 1: 1, 3: 2, 5: 2, 7: 3, 9: 1}
COMPRESS = {2: (0, 0), 4: (0, 1), 6: (1, 0), 8: (1, 1)}


class Steps:

    def __init__(self, sem, names):
        self.sem, self.names, self.n = sem, names.split(), 0
        assert len(set(self.names)) == len(self.names)

    def did(self, name):
        assert self.names[self.n % len(self.names)] == name, (self.names[self.n % len(self.names)], name)
        self.n += 1
        return 1

    def at(self, name, i=0):
        return i * len(self.names) + self.names.index(name) + 1


def trunk(nc, x, even_norm, even_w_in, sgu_ln_g, sgu_ln_b, sgu_w, sgu_b, q_gain, k_gain, cmp_pos,
          cmp_w1, cmp_b1, cmp_w2, even_w_out, odd_norm, odd_w_in, hgrn_lb, out_gain, odd_w_out, out):
    with ExitStack() as ctx:
        def sb(name, shape, dt=F32):
            return ctx.enter_context(nc.sbuf_tensor(name, shape, dt))

        def sem(name):
            return ctx.enter_context(nc.semaphore(name))

        raw = sb("raw", [P, NQ, KQ, SW])
        whl = sb("whl", [P, NQ, KQ, 2, SW], F32R)
        xhl = sb("xhl", [P, KT, 2, T], F32R)
        cathl = sb("cathl", [P, KT, 2, T], F32R)
        xT = sb("xT", [P, KT, T])
        ident = sb("ident", [P, P])
        ones = sb("ones", [P, P])
        tri64 = sb("tri64", [P, P])
        tri64_i = sb("tri64_i", [P, P], I32)
        tri_i = sb("tri_i", [P, P], I32)
        fold_g = sb("fold_g", [2 * NG, NG])
        fold = sb("fold", [2 * CW, CW])
        vecs = sb("vecs", [P, P])
        vT = sb("vT", [P, P])
        posr = sb("posr", [2 * NL, HD])
        posT = sb("posT", [P, 2 * NL])
        sgub = sb("sgub", [1, 8 * P])
        small = sb("small", [P, 256])
        tmp = sb("tmp", [P, 2, 2, SW])
        Z = sb("Z", [P, 4, 2, SW])
        arena = sb("arena", [P, ARENA])

        class Carve:
            def __init__(self):
                self.o = 0

            def __call__(self, n):
                self.o += n
                assert self.o <= ARENA, self.o
                return arena[:, self.o - n:self.o]

        c0 = Carve()
        gav = c0(2048).rearrange("p (a n) -> p a n", a=2)
        gu = c0(2048).rearrange("p (a n) -> p a n", a=8)
        xnat = arena[:, 0:4096].rearrange("p (a n) -> p a n", a=2)
        lngb = c0(2048).rearrange("p (a n) -> p a n", a=2)
        keysT = c0(2 * 527).rearrange("p (a n) -> p a n", a=2)
        vals = c0(1024).rearrange("p (b a n) -> p b a n", b=2, a=2)
        vcmp = c0(256).rearrange("p (a n) -> p a n", a=2)
        w_sT = c0(1024).rearrange("p (a n) -> p a n", a=8)
        dist = c0(414)
        bias = c0(828).rearrange("p (a n) -> p a n", a=2)
        prob = c0(800)[:, 0:798]
        probT = c0(1024).rearrange("p (a n) -> p a n", a=2)
        sgw = arena[:, c0.o - 1024:c0.o].rearrange("p (a n) -> p a n", a=8)
        w2 = c0(512).rearrange("p (i a n) -> p i a n", i=2, a=2)
        obuf = c0(512).rearrange("p (a n) -> p a n", a=2)
        scr = arena[:, c0.o - 512:c0.o]
        wg = prob[:, 0:KT * NG].rearrange("p (k n) -> p k n", k=KT)
        wghl = cathl[:, 8:10].rearrange("p k a n -> p (k a n)")[:, 0:KT * 2 * NG]\
            .rearrange("p (k a n) -> p k a n", k=KT, a=2)
        sgz = c0(512).rearrange("p (a n) -> p a n", a=2)
        xn = arena[:, 0:4096].rearrange("p (r a n) -> p r a n", r=4, a=KQ)
        hid = arena[:, 2048:2176].rearrange("p (i g n) -> p i g n", i=2, g=2)
        kcz = arena[:, 2176:2432]
        gsc = arena[:, 2432:2560]
        cpart = arena[:, 2560:3072]
        gpart = arena[:, 3072:3584]
        kpos = arena[:, 0:960]

        c1 = Carve()
        (hF, hK, hG, hGS, hD1, hE2, hD2, hE3, hKE, hKS, hQE, hQI, hAT, hKN, hSQ, hRS, hSG, hZS,
         hO, starts) = (c1(512) for _ in range(20))
        hST = c1(768).rearrange("p (h c v) -> p h c v", h=2, c=3)
        acc = c1(512)
        sq = c1(512)
        xres = arena[:, 0:1024].rearrange("p (b a n) -> p b a n", b=2, a=2)

        pp = ctx.enter_context(nc.psum_tensor("pp", [P, 4, 512], F32))
        px = ctx.enter_context(nc.psum_tensor("px", [P, 4, 512], F32))

        landed = [sem(f"landed{q}") for q in range(NQ)]
        hi_done, lo_done = sem("hi_done"), sem("lo_done")
        pe_q = sem("pe_q")
        lo_pool = sem("lo_pool")
        lo_out, strip_out = sem("lo_out"), sem("strip_out")
        seen = sem("seen")
        x_in = [sem("x_in0"), sem("x_in1")]
        wg_in, gain_in, vec_in = sem("wg_in"), sem("gain_in"), sem("vec_in")
        sg_in, misc_in = sem("sg_in"), sem("misc_in")
        y_out = [sem("y_out0"), sem("y_out1")]

        pool0 = Steps(sem("pool0"), "ms ident ms1 vecs fz fold0 fold1 gz foldg0 foldg1 triF tri64a tri64 tri64i "
                      "id0 id1 ic0 ic1 df sel0 sel1 selc0 selc1 zw")
        pe0 = Steps(sem("pe0"), "xT0 xT1 xT2 xT3 xT4 xT5 xT6 xT7 rs gT vT posT wsT0 wsT1")
        act0 = Steps(sem("act0"), "ss0 ss1 xT0 ln rs xT2 xT4 xT6 wg lbe0 lbe1")
        dve0 = Steps(sem("dve0"), "xT1 ms xT3 xT5 xT7 diag0 diag1 gT rsb vT posT gain "
                     "wsT0 wsT1 wg lbm lba lbb lbs lbr lbp0 lbp1 lbc lb omlb")
        xn_done, xhi_done, xlo_done, xlo_pool = sem("xn_done"), sem("xhi_done"), sem("xlo_done"), sem("xlo_pool")
        peP = Steps(sem("peP"), "fk kT0 ck0 ck1 kcT gates fv kT1 cv0 cv1")
        actP = Steps(sem("actP"), "kp0 kp1 cs0 ln0 rs0 hk0 hk1 lnc rsc ln1 rs1 gc cs1 hv0 hv1 gs")
        dveP = Steps(sem("dveP"), "kpa0 kpb0 kpc0 kpd0 kpl0 kpa1 kpb1 kpc1 kpd1 kpl1 "
                     "sq0 ss0 ms0 k00 k01 k02 k03 kT0 kc sqc ssc msc kn0 kn1 sq1 ss1 ms1 k10 k11 k12 k13 kcT "
                     "kT1 vc gt0 gt1 gt2 gt3 gt4 gt5")
        peA = Steps(sem("peA"), "rms s0 t0 s1 o0 t1 o1")
        actA = Steps(sem("actA"), "sq ln rq e00 e01 e02 e03 e04 e05 pt0 pc0 e10 e11 e12 e13 e14 e15 sg av "
                     "pt1 pc1 gu cat")
        dveA = Steps(sem("dveA"), "ms a00 a01 a02 a03 m00 m01 m02 n0 r0x r0 c0 p00 p01 p02 pt0 pd0 "
                     "a10 a11 a12 a13 m10 m11 m12 n1 r1x r1 c1 p10 p11 p12 sz o0 pt1 pd1 o1 cat")
        poolA = Steps(sem("poolA"), "b0 b1")
        peG = Steps(sem("peG"), "g0 g1 g2 g3")
        actG = Steps(sem("actG"), "ln rs sg0 sg1 c1 sg2 c2 sg3 c3 c4")
        dveG = Steps(sem("dveG"), "st0 st1 st2 st3 ag0 ag1 ms v0 v1 v2 v3 v4 v5 "
                     "z0 z1 u0 w0 l0 z2 u1 w1 l1 z3 u2 w2 l2 u3 w3 l3 acc")
        actO = Steps(sem("actO"), "sqa sqb")
        dveO = Steps(sem("dveO"), "xa aa xb ab")
        peR, actR, dveR = Steps(sem("peR"), "ss"), Steps(sem("actR"), "ln rs"), Steps(sem("dveR"), "ms at0")
        peH = Steps(sem("peH"), "ksT at kv o ss")
        actH = Steps(sem("actH"), "sf g e2 e1 e3 e4 kn sq ln rs sg cat")
        dveH = Steps(sem("dveH"), "f0 f1 k gs d1 d2 kt qe at s10 s11 s20 s21 s30 s31 ms o1 o2 lo")
        poolH = Steps(sem("poolH"), "ks qi zs")
        poolM = Steps(sem("poolM"), "one zero")
        poolR = Steps(sem("poolR"), "ra rb")

        block = ctx.enter_context(nc.Block())

        V_N0, V_N1, V_LB, V_B1, V_QG, V_KG, V_OG = 0, 16, 32, 64, 68, 69, 72
        NV = 73
        SSX, RSX, KGQ, LB, OMLB, LBT = 0, 2, 4, 8, 24, 40
        KSS, KRS, GTAB, RSSQ, MX, NM, SUMS, COEF = 136, 140, 144, 200, 204, 210, 216, 222
        BST = 228

        REGIONS = [(0, 128), (128, 256), (256, 512), (512, 768), (768, 783), (783, 798)]

        ltmp = [small[:, LBT + 16 * n:LBT + 16 * n + 16] for n in range(6)]

        def src(w, col, q, swap=False):
            q = (q + 2) % NQ if swap else q
            return w[q * KQ * P:(q + 1) * KQ * P, bass.ds(col, SW)].rearrange("(k p) n -> p k n", p=P)

        @block.sync
        def _(sp):
            def load(s, part, first=False, static=True):
                for q in range(NQ):
                    if not first:
                        if isinstance(s, int) and s == 1:
                            sp.wait_ge(lo_pool, q + 1)
                        else:
                            sp.wait_ge(lo_done, 4 * (s - 1) + q + 1)
                        if not static:
                            sp.sem_inc(seen, 1)
                    sp.dma_start(raw[:, q], part(q)).then_inc(landed[q], 16)

            for a in range(TT):
                sp.dma_start(xnat[:, a, :D // 2], x[0, a * P:(a + 1) * P, :D // 2]).then_inc(x_in[a], 16)
            for s in range(S_PRE, S_ATT):
                if s in COMPRESS:
                    i, half = COMPRESS[s]
                    load(s, lambda q: cmp_w1[i, (half * 16 + q * KQ) * P:(half * 16 + (q + 1) * KQ) * P, :]
                         .rearrange("(k p) n -> p k n", p=P))
                else:
                    load(s, lambda q: src(even_w_in, KV0 + SW * KV_GROUP[s], q), first=s == 0)
            with sp.Fori(0, 4) as p:
                for j, base in enumerate((3 * A_WIDTH, 3 * A_WIDTH + B_WIDTH, A_WIDTH, 0)):
                    load(p * 4 + (S_ATT + j), lambda q, base=base: src(even_w_in, p * SW + base, q),
                         static=False)
            for j in range(4):
                load(S_SGU + j, lambda q, j=j: src(even_w_in, 2 * A_WIDTH + SW * j, q))
            with sp.Fori(0, 4) as p:
                for j in range(2):
                    load(p * 2 + (S_OUT0 + j), lambda q, j=j: src(even_w_out, p * (2 * SW) + j * SW, q, True),
                         static=False)
            with sp.Fori(0, 8) as p:
                for j, base in enumerate((D, 0, 2 * D, 3 * D)):
                    load(p * 4 + (S_HGRN + j), lambda q, base=base: src(odd_w_in, p * SW + base, q),
                         static=False)

            def store(n, j):
                sp.wait_ge(strip_out, n * 2 + (S_OUT1 + j + 1))
                sp.sem_inc(seen, 1)
                sp.dma_start(out[:, bass.ds(n * (2 * SW) + j * SW, SW)].rearrange("(a p) n -> p a n", p=P),
                             Z[:, j]).then_inc(y_out[j], 16)

            for j in range(2):
                load(S_OUT1 + j, lambda q, j=j: src(odd_w_out, j * SW, q))
            with sp.Fori(0, 3) as p:
                for j in range(2):
                    load(p * 2 + (S_OUT1 + 2 + j), lambda q, j=j: src(odd_w_out, p * (2 * SW) + (2 + j) * SW, q),
                         static=False)
                for j in range(2):
                    store(p, j)
            for j in range(2):
                store(3, j)
            for j in range(2):
                sp.wait_ge(y_out[j], 16 * 4)

        def lo_part(eng, layer, c):
            eng.wait_ge(xhi_done, 4 * layer + c + 1)
            eng.tensor_tensor(xhl[:, KQ * c:KQ * c + KQ, 1, :], xn[:, c],
                              xhl[:, KQ * c:KQ * c + KQ, 0, :].bitcast(F32), ALU.subtract)\
                .then_inc(xlo_pool if c == 1 else xlo_done, 1)

        @block.gpsimd
        def _(pool):
            pool.memset(ident[:], 0.0).then_inc(pool0.sem, pool0.did("ms"))
            pool.wait_ge(pool0.sem, pool0.at("ms"))
            pool.affine_select(out=ident[:], in_=ident[:], compare_op=ALU.not_equal, fill=1.0, base=0,
                               pattern=[[-1, P]], channel_multiplier=1).then_inc(pool0.sem, pool0.did("ident"))
            pool.memset(ones[:], 1.0).then_inc(pool0.sem, pool0.did("ms1"))
            pool.memset(vecs[:], 0.0).then_inc(pool0.sem, pool0.did("vecs"))
            pool.wait_ge(pool0.sem, pool0.at("vecs"))
            for row, a in ((V_N0, even_norm.rearrange("a (k p) -> (a k) p", p=P)),
                           (V_N1, odd_norm.rearrange("a (k p) -> (a k) p", p=P)),
                           (V_LB, hgrn_lb.rearrange("a (k p) -> (a k) p", p=P)),
                           (V_B1, cmp_b1.rearrange("a (k p) -> (a k) p", p=P)),
                           (V_QG, q_gain), (V_KG, k_gain), (V_OG, out_gain)):
                pool.dma_start(vecs[row:row + a.shape[0], :], a).then_inc(gain_in if row == V_N0 else vec_in, 16)
            pool.dma_start(posr[:], cmp_pos.rearrange("a l d -> (a l) d")).then_inc(vec_in, 16)
            for to, w, zero, name in ((fold, CW, "fz", "fold"), (fold_g, NG, "gz", "foldg")):
                pool.memset(to[:], 0.0).then_inc(pool0.sem, pool0.did(zero))
                for n, before in enumerate((zero, name + "0")):
                    pool.wait_ge(pool0.sem, pool0.at(before))
                    pool.affine_select(out=to[:], in_=to[:], compare_op=ALU.not_equal, fill=1.0, base=-n * w,
                                       pattern=[[-1, w]], channel_multiplier=1)\
                        .then_inc(pool0.sem, pool0.did(f"{name}{n}"))
            pool.affine_select(out=tri64[:], in_=ones[:], compare_op=ALU.is_ge, fill=0.0, base=0,
                               pattern=[[1, P]], channel_multiplier=-1).then_inc(pool0.sem, pool0.did("triF"))
            pool.wait_ge(pool0.sem, pool0.at("triF"))
            pool.tensor_copy(tri_i[:], tri64[:]).then_inc(pool0.sem, pool0.did("tri64a"))
            pool.wait_ge(pool0.sem, pool0.at("tri64a"))
            pool.memset(tri64[0:CH, CH:P], 0.0).then_inc(pool0.sem, pool0.did("tri64"))
            pool.wait_ge(pool0.sem, pool0.at("tri64"))
            pool.tensor_copy(tri64_i[:], tri64[:]).then_inc(pool0.sem, pool0.did("tri64i"))
            for q in range(NQ):
                if q == 2:
                    lo_part(pool, 0, 1)
                pool.wait_ge(hi_done, q + 1)
                pool.tensor_tensor(whl[:, q, :, 1, :], raw[:, q], whl[:, q, :, 0, :].bitcast(F32), ALU.subtract)\
                    .then_inc(lo_pool, 1)
            pool.dma_start(sgw, sgu_w.rearrange("g t s -> t g s")).then_inc(sg_in, 16)
            pool.dma_start(sgub[:], sgu_b.rearrange("(a g) t -> a (g t)", a=1)).then_inc(misc_in, 16)
            pool.dma_start(w2[:], cmp_w2.rearrange("i (a p) n -> p i a n", p=P)).then_inc(misc_in, 16)
            for n, v in enumerate((sgu_ln_g, sgu_ln_b)):
                pool.dma_start(lngb[:, n, :], v.partition_broadcast(P)).then_inc(misc_in, 16)
            di = scr[:, 0:414].bitcast(I32)
            parts = (("0", 0, P, -1, 0), ("1", P, T, -1, P), ("c0", 3 * P, NC, -16, 1 - NL),
                     ("c1", 3 * P + NC, NC, -16, P + 1 - NL))
            for n, (name, at, w, step, base) in enumerate(parts):
                pool.iota(di[:, at:at + w], pattern=[[step, w]], base=base, channel_multiplier=1)\
                    .then_inc(pool0.sem, pool0.did("i" + (name if name[0] == "c" else "d" + name)))
            pool.wait_ge(pool0.sem, pool0.at("ic1"))
            pool.tensor_copy(dist, di).then_inc(pool0.sem, pool0.did("df"))
            pool.wait_ge(pool0.sem, pool0.at("df"))
            for name, at, w, step, base in parts:
                pool.affine_select(out=dist[:, at:at + w], in_=dist[:, at:at + w], compare_op=ALU.is_ge, fill=BIG,
                                   base=base, pattern=[[step, w]], channel_multiplier=1)\
                    .then_inc(pool0.sem, pool0.did("sel" + name))
            pool.memset(w_sT[:], 0.0).then_inc(pool0.sem, pool0.did("zw"))
            pool.wait_ge(pool0.sem, pool0.at("selc1"))
            for a in range(2):
                pool.tensor_scalar(bias[:, a, :], dist, -0.5 ** (a + 1), None, ALU.mult)\
                    .then_inc(poolA.sem, poolA.did(f"b{a}"))
            pool.wait_ge(poolA.sem, poolA.at("b1"))
            with pool.Fori(0, 4) as p:
                for a in range(2):
                    pool.wait_ge(dveA.sem, dveA.at(f"a{a}3", p))
                    pool.sem_inc(seen, 1)
                    pool.tensor_scalar(bias[:, a, :], bias[:, a, :], 0.25, None, ALU.mult)\
                        .then_inc(poolA.sem, poolA.did(f"b{a}"))
            pool.wait_ge(poolA.sem, poolA.at("b1", 4))
            pool.memset(starts, 1.0).then_inc(poolM.sem, poolM.did("one"))
            pool.wait_ge(poolM.sem, poolM.at("one"))
            pool.memset(starts.rearrange("p (c t) -> p c t", t=CH)[:, :, 0:1], 0.0)\
                .then_inc(poolM.sem, poolM.did("zero"))
            lo_part(pool, 1, 1)
            with pool.Fori(0, 8) as i:
                pool.wait_ge(actH.sem, actH.at("e4", i))
                pool.tensor_tensor(hKS, hK, hD2, ALU.mult).then_inc(poolH.sem, poolH.did("ks"))
                pool.wait_ge(strip_out, i * 4 + (S_HGRN + 2))
                pool.tensor_tensor(hQI, Z[:, 1].rearrange("p a n -> p (a n)"), hE3, ALU.mult)\
                    .then_inc(poolH.sem, poolH.did("qi"))
                pool.wait_ge(actH.sem, actH.at("sg", i))
                pool.tensor_tensor(hZS, Z[:, 3].rearrange("p a n -> p (a n)"), hSG, ALU.mult)\
                    .then_inc(poolH.sem, poolH.did("zs"))
            pool.wait_ge(actH.sem, actH.at("g", 7))
            pool.wait_ge(dveH.sem, dveH.at("kt", 7))
            with pool.Fori(0, 4) as p:
                for j in range(2):
                    pool.wait_ge(pe_q, p * 8 + 4 * (S_OUT1 + j - 1))
                    pool.tensor_copy(xres[:, j], xT[:, bass.ds(p * 4 + 2 * j, 2), :])\
                        .then_inc(poolR.sem, poolR.did("ra" if j == 0 else "rb"))

        def kv_at(h, c):
            bank, n = (1, h) if c == 1 else (0, 2 * h + c // 2)
            return px[:, bank, n * HD:(n + 1) * HD]

        def cast(act, s, qs, first=False):
            for q in qs:
                act.wait_ge(landed[q], s * 16 + 16)
                if not first:
                    act.wait_ge(pe_q, s * 4 + (q - 3))
                act.activation(whl[:, q, :, 0, :], raw[:, q], ACT.Copy).then_inc(hi_done, 1)

        def take_lo(act, s, par, n=1, first=False):
            act.wait_ge(pe_q, s * 4 + 4)
            if not first:
                act.wait_ge(strip_out, s - 1)
            act.activation(tmp[:, par], pp[:, 2 * par:2 * par + 2, SW:2 * SW], ACT.Copy).then_inc(lo_out, n)

        @block.scalar
        def _(act):
            for a in range(TT):
                act.dma_start(xnat[:, a, D // 2:], x[0, a * P:(a + 1) * P, D // 2:]).then_inc(x_in[a], 16)
            act.dma_start(wg[:], even_w_in[:, GATE0:GATE0 + NG].rearrange("(k p) n -> p k n", p=P)).then_inc(wg_in, 16)
            act.preload_act_table_set(LN_EXP)
            for a in range(TT):
                act.wait_ge(x_in[a], 32)
                act.activation(cathl[:, 4 * a:4 * a + 4].rearrange("p k a n -> p (k a n)"), xnat[:, a, :], ACT.Square,
                               accum_out=small[:, SSX + a:SSX + a + 1]).then_inc(act0.sem, act0.did(f"ss{a}"))

            def take_x(b):
                act.wait_ge(pe0.sem, pe0.at(f"xT{b}"))
                act.activation(xT[:, 2 * b:2 * b + 2, :], (pp if b < 4 else px)[:, b % 4, :]
                               .rearrange("p (a n) -> p a n", a=2), ACT.Copy).then_inc(act0.sem, act0.did(f"xT{b}"))

            take_x(0)
            act.wait_ge(dve0.sem, dve0.at("ms"))
            act.activation(small[:, RSX:RSX + 2], small[:, SSX:SSX + 2], ACT.Ln).then_inc(act0.sem, act0.did("ln"))
            act.wait_ge(act0.sem, act0.at("ln"))
            act.activation(small[:, RSX:RSX + 2], small[:, RSX:RSX + 2], ACT.Exp, scale=-0.5)\
                .then_inc(act0.sem, act0.did("rs"))
            for b in (2, 4, 6):
                take_x(b)

            def xhi(layer, between=None):
                for c in range(4):
                    act.wait_ge(xn_done, 16 * layer + 4 * c + 4)
                    act.activation(xhl[:, KQ * c:KQ * c + KQ, 0, :], xn[:, c], ACT.Copy).then_inc(xhi_done, 1)
                    if between:
                        between(c)

            cast(act, S_PRE, (0,), first=True)
            xhi(0, between=lambda c: cast(act, S_PRE, (c + 1,), first=True) if c < 3 else None)

            def split_gate_columns():
                act.wait_ge(wg_in, 16)
                act.activation(wghl[:, :, 0, :], wg[:], ACT.Copy).then_inc(act0.sem, act0.did("wg"))

            def lower_bound():
                for n in range(2):
                    act.wait_ge(dve0.sem, dve0.at("lba" if n == 0 else "lbb"))
                    act.activation(ltmp[1 + n], ltmp[1 + n], ACT.Exp).then_inc(act0.sem, act0.did(f"lbe{n}"))

            def rstd(steps, names, dve, dname, ap, scale=-0.5, i=0):
                act.wait_ge(dve.sem, dve.at(dname, i))
                act.activation(ap, ap, ACT.Ln).then_inc(steps.sem, steps.did(names[0]))
                act.wait_ge(steps.sem, steps.at(names[0], i))
                act.activation(ap, ap, ACT.Exp, scale=scale).then_inc(steps.sem, steps.did(names[1]))

            kph = [cathl[:, 4 * i:4 * i + 4].rearrange("p k a n -> p (k a n)")[:, 0:NL * 2 * CW]
                   .rearrange("p (l a n) -> p l a n", l=NL, a=2) for i in range(2)]
            for s in range(S_PRE, S_ATT):
                cast(act, s + 1, (0,))
                if s in (5, 9):
                    i = (s - 5) // 4
                    act.wait_ge(peP.sem, peP.at(("fk", "fv")[i]))
                    for g in range(2):
                        act.activation(hid[:, i, g, 0:CW], px[:, 3, 256 + 64 * i + 32 * g:256 + 64 * i + 32 * g + CW],
                                       ACT.Gelu_apprx_tanh, bias=vT[:, V_B1 + 2 * i + g:V_B1 + 2 * i + g + 1])\
                            .then_inc(actP.sem, actP.did(f"h{'kv'[i]}{g}"))
                if s == 9:
                    act.activation(gsc[:, 0:2 * NG].rearrange("p (a n) -> p a n", a=2),
                                   px[:, 3, 0:64].rearrange("p (a n) -> p a n", a=2)[:, :, 0:NG], ACT.Sigmoid)\
                        .then_inc(actP.sem, actP.did("gs"))
                cast(act, s + 1, (1, 2))
                if s in (4, 8):
                    i = (s - 4) // 4
                    act.wait_ge(pe_q, s * 4 + 4)
                    if i == 1:
                        act.wait_ge(peP.sem, peP.at("fk"))
                    act.activation(cpart[0:2 * CW], px[0:2 * CW, 2, :], ACT.Copy).then_inc(actP.sem, actP.did(f"cs{i}"))
                if s in KV_GROUP:
                    take_lo(act, s, PAR[s], n=COUNT[s], first=s < 2)
                cast(act, s + 1, (3,))
                if s in (0, 2):
                    i = s // 2
                    act.wait_ge(dveP.sem, dveP.at(f"kpd{i}"))
                    act.activation(kph[i][:, :, 0, :], kpos.rearrange("p (l n) -> p l n", l=NL), ACT.Copy)\
                        .then_inc(actP.sem, actP.did(f"kp{i}"))
                if s == 2:
                    split_gate_columns()
                if s in (4, 6):
                    act.preload_act_table_set(LN_EXP)
                    if s == 6:
                        rstd(actP, ("lnc", "rsc"), dveP, "msc", small[0:NC, KRS:KRS + 2])
                    n = (s - 4) // 2
                    rstd(actP, (f"ln{n}", f"rs{n}"), dveP, f"ms{n}", small[:, KRS:KRS + 4])
                if s == 8:
                    lower_bound()
                if s == 7:
                    act.wait_ge(peP.sem, peP.at("gates"))
                    act.activation(gpart[0:2 * NG], px[0:2 * NG, 3, :], ACT.Copy).then_inc(actP.sem, actP.did("gc"))

            with act.Fori(0, 4) as p:
                s0 = p * 4 + S_ATT
                act.preload_act_table_set(LN_EXP)

                def exps(a):
                    act.wait_ge(dveA.sem, dveA.at(f"n{a}", p))
                    for r, (lo, hi) in enumerate(REGIONS):
                        act.activation(prob[:, lo:hi], prob[:, lo:hi], ACT.Exp, bias=small[:, NM + r:NM + r + 1],
                                       accum_out=small[:, SUMS + r:SUMS + r + 1])\
                            .then_inc(actA.sem, actA.did(f"e{a}{r}"))

                def take_pT(a):
                    act.wait_ge(peA.sem, peA.at(f"t{a}", p))
                    act.activation(probT[:, 0, 0:384], px[:, 2, 0:384], ACT.Copy)\
                        .then_inc(actA.sem, actA.did(f"pt{a}"))
                    act.activation(probT[0:NC, 0, 384:512], px[0:NC, 2, 384:512], ACT.Copy)\
                        .then_inc(actA.sem, actA.did(f"pc{a}"))

                cast(act, s0 + 1, (0, 1, 2))
                take_lo(act, s0, 0)
                cast(act, s0 + 1, (3,))
                act.wait_ge(strip_out, s0 + 1)
                act.activation(obuf[:], Z[:, 0], ACT.Square).then_inc(actA.sem, actA.did("sq"))
                cast(act, s0 + 2, (0, 1))
                rstd(actA, ("ln", "rq"), dveA, "ms", small[:, RSSQ:RSSQ + 4], i=p)
                cast(act, s0 + 2, (2,))
                exps(0)
                take_lo(act, s0 + 1, 1)
                cast(act, s0 + 2, (3,))
                cast(act, s0 + 3, (0, 1))
                take_pT(0)
                cast(act, s0 + 3, (2,))
                exps(1)
                take_lo(act, s0 + 2, 0)
                act.wait_ge(strip_out, s0 + 2)
                act.activation(sgz[:], Z[:, 1], ACT.Tanh, scale=0.5).then_inc(actA.sem, actA.did("sg"))
                cast(act, s0 + 3, (3,))
                act.wait_ge(strip_out, s0 + 3)
                act.activation(gav[:, :, bass.ds(p * SW, SW)], Z[:, 2], ACT.Gelu_apprx_tanh)\
                    .then_inc(actA.sem, actA.did("av"))
                cast(act, s0 + 4, (0, 1))
                take_pT(1)
                cast(act, s0 + 4, (2,))
                take_lo(act, s0 + 3, 1)
                cast(act, s0 + 4, (3,))
                act.wait_ge(strip_out, s0 + 4)
                act.activation(gu[:, bass.ds(p * 2, 2), :], Z[:, 3], ACT.Gelu_apprx_tanh)\
                    .then_inc(actA.sem, actA.did("gu"))
                act.wait_ge(dveA.sem, dveA.at("o1", p))
                act.activation(cathl[:, bass.ds(p * 2 + 8, 2), 0, :], obuf[:], ACT.Copy)\
                    .then_inc(actA.sem, actA.did("cat"))

            for j in range(4):
                s = S_SGU + j
                if j == 0:
                    rstd(actG, ("ln", "rs"), dveG, "ms", small[:, RSX:RSX + 2])
                cast(act, s + 1, (0, 1, 2))
                take_lo(act, s, j % 2)
                cast(act, s + 1, (3,))
                act.wait_ge(strip_out, s + 1)
                act.activation(sgz[:], Z[:, j], ACT.Sigmoid).then_inc(actG.sem, actG.did(f"sg{j}"))
                if j >= 1:
                    act.wait_ge(dveG.sem, dveG.at(f"w{j - 1}"))
                    act.activation(cathl[:, 2 * j - 2:2 * j, 0, :], obuf[:], ACT.Copy)\
                        .then_inc(actG.sem, actG.did(f"c{j}"))
            act.wait_ge(dveG.sem, dveG.at("w3"))
            act.activation(cathl[:, 6:8, 0, :], obuf[:], ACT.Copy).then_inc(actG.sem, actG.did("c4"))

            act.preload_act_table_set(LN_EXP)
            with act.Fori(0, 4) as p:
                for j in range(2):
                    s = p * 2 + (S_OUT0 + j)
                    cast(act, s + 1, (0, 1, 2))
                    take_lo(act, s, j)
                    cast(act, s + 1, (3,))
                    act.wait_ge(dveO.sem, dveO.at("xa" if j == 0 else "xb", p))
                    act.activation(sq, xT[:, bass.ds(p * 4 + 2 * j, 2), :], ACT.Square)\
                        .then_inc(actO.sem, actO.did("sqa" if j == 0 else "sqb"))
            rstd(actR, ("ln", "rs"), dveR, "ms", hRS[:, 0:T])
            xhi(1)

            act.preload_act_table_set("sigmoid_and_others")
            cast(act, S_HGRN + 1, (0, 1, 2))
            with act.Fori(0, 8) as i:
                s0 = i * 4 + S_HGRN
                take_lo(act, s0, 0)
                cast(act, s0 + 1, (3,))
                act.wait_ge(strip_out, s0 + 1)
                act.activation(hF, Z[:, 0].rearrange("p a n -> p (a n)"), ACT.Sigmoid)\
                    .then_inc(actH.sem, actH.did("sf"))
                act.preload_act_table_set(LN_EXP)
                act.wait_ge(dveH.sem, dveH.at("f1", i))
                act.activation(hG, hF, ACT.Ln).then_inc(actH.sem, actH.did("g"))
                cast(act, s0 + 2, (0, 1))
                act.wait_ge(dveH.sem, dveH.at("d1", i))
                act.activation(hE2, hD1, ACT.Exp, scale=-1.0).then_inc(actH.sem, actH.did("e2"))
                act.wait_ge(actH.sem, actH.at("e2", i))
                act.activation(hD1, hD1, ACT.Exp).then_inc(actH.sem, actH.did("e1"))
                act.activation(hE3, hGS, ACT.Exp).then_inc(actH.sem, actH.did("e3"))
                act.wait_ge(dveH.sem, dveH.at("d2", i))
                act.activation(hD2, hD2, ACT.Exp).then_inc(actH.sem, actH.did("e4"))
                cast(act, s0 + 2, (2, 3))
                take_lo(act, s0 + 1, 1)
                cast(act, s0 + 3, (0, 1, 2))
                act.wait_ge(peH.sem, peH.at("ksT", i))
                act.activation(hKN, px[:, 3, :], ACT.Copy).then_inc(actH.sem, actH.did("kn"))
                take_lo(act, s0 + 2, 0)
                cast(act, s0 + 3, (3,))
                cast(act, s0 + 4, (0, 1, 2))
                act.wait_ge(peH.sem, peH.at("o", i))
                act.activation(hSQ, px[:, 2, :], ACT.Square).then_inc(actH.sem, actH.did("sq"))
                take_lo(act, s0 + 3, 1)
                cast(act, s0 + 4, (3,))
                rstd(actH, ("ln", "rs"), dveH, "ms", hRS, i=i)
                act.wait_ge(strip_out, s0 + 4)
                act.activation(hSG, Z[:, 3].rearrange("p a n -> p (a n)"), ACT.Sigmoid)\
                    .then_inc(actH.sem, actH.did("sg"))
                cast(act, s0 + 5, (0,))
                act.wait_ge(dveH.sem, dveH.at("o2", i))
                act.activation(cathl[:, bass.ds(i * 2, 2), 0, :], hO.rearrange("p (a n) -> p a n", a=2), ACT.Copy)\
                    .then_inc(actH.sem, actH.did("cat"))
                cast(act, s0 + 5, (1, 2))

            def out1(p, j, last=False, first=False):
                s = p * 2 + (S_OUT1 + j)
                if not last:
                    cast(act, s + 1, () if first else (0, 1, 2))
                take_lo(act, s, j)
                if not last:
                    cast(act, s + 1, (3,))

            for j in range(2):
                out1(0, j, first=j == 0)
            with act.Fori(1, 3) as p:
                for j in range(2):
                    out1(p, j)
            for j in range(2):
                out1(3, j, last=j == 1)

        def lows(dve, s, qs):
            for q in qs:
                dve.wait_ge(hi_done, s * 4 + (q + 1))
                pooled = isinstance(s, int) and s == 1 and q == 0
                dve.tensor_tensor(whl[:, q, :, 1, :], raw[:, q], whl[:, q, :, 0, :].bitcast(F32), ALU.subtract)\
                    .then_inc(lo_done, NQ + 1 if pooled else 1)

        def take(dve, s, par, dst, n=1):
            dve.wait_ge(lo_out, s + 1)
            dve.tensor_tensor(dst, pp[:, 2 * par:2 * par + 2, 0:SW], tmp[:, par], ALU.add)\
                .then_inc(strip_out, n)

        @block.vector
        def _(dve):
            def take_x(b):
                dve.wait_ge(pe0.sem, pe0.at(f"xT{b}"))
                dve.tensor_copy(xT[:, 2 * b:2 * b + 2, :], (pp if b < 4 else px)[:, b % 4, :]
                                .rearrange("p (a n) -> p a n", a=2)).then_inc(dve0.sem, dve0.did(f"xT{b}"))

            take_x(1)
            dve.wait_ge(act0.sem, act0.at("ss1"))
            dve.tensor_scalar(small[:, SSX:SSX + 2], small[:, SSX:SSX + 2], 1.0 / D, EPS, ALU.mult, ALU.add)\
                .then_inc(dve0.sem, dve0.did("ms"))
            for b in (3, 5, 7):
                take_x(b)
            dve.wait_ge(act0.sem, act0.at("rs"))
            for a in range(TT):
                dve.tensor_scalar(tmp[:, 0, 0, a * P:(a + 1) * P], ident[:], small[:, RSX + a:RSX + a + 1], None,
                                  ALU.mult).then_inc(dve0.sem, dve0.did(f"diag{a}"))
            dve.wait_ge(pe0.sem, pe0.at("gT"))
            dve.tensor_copy(vT[:, V_N0:V_N0 + KT], px[:, 3, 0:KT]).then_inc(dve0.sem, dve0.did("gT"))
            dve.tensor_copy(tmp[:, 1, 0, :], pp[:, 1, 0:T]).then_inc(dve0.sem, dve0.did("rsb"))
            dve.wait_ge(dve0.sem, dve0.at("rsb"))
            dve.wait_ge(act0.sem, act0.at("xT6"))

            def norm(layer, vcol, rsb):
                for c in range(4):
                    for j in range(KQ):
                        k = KQ * c + j
                        dve.scalar_tensor_tensor(xn[:, c, j, :], xT[:, k, :], vT[:, vcol + k:vcol + k + 1], rsb,
                                                 ALU.mult, ALU.mult).then_inc(xn_done, 1)
                        if c == 1 and j == 2:
                            lo_part(dve, layer, 0)
                lo_part(dve, layer, 2)
                lo_part(dve, layer, 3)

            norm(0, V_N0, tmp[:, 1, 0, :])
            def split_gate_columns():
                dve.wait_ge(act0.sem, act0.at("wg"))
                dve.tensor_tensor(wghl[:, :, 1, :], wg[:], wghl[:, :, 0, :].bitcast(F32), ALU.subtract)\
                    .then_inc(dve0.sem, dve0.did("wg"))

            def lower_bound():
                la, lb = vT[:, V_LB:V_LB + 16], vT[:, V_LB + 16:V_LB + 32]

                def lbstep(name, o, a, b, op):
                    dve.tensor_tensor(o, a, b, op).then_inc(dve0.sem, dve0.did(name))
                    dve.wait_ge(dve0.sem, dve0.at(name))

                lbstep("lbm", ltmp[0], la, lb, ALU.max)
                lbstep("lba", ltmp[1], la, ltmp[0], ALU.subtract)
                lbstep("lbb", ltmp[2], lb, ltmp[0], ALU.subtract)
                dve.wait_ge(act0.sem, act0.at("lbe1"))
                lbstep("lbs", ltmp[3], ltmp[1], ltmp[2], ALU.add)
                dve.reciprocal(ltmp[3], ltmp[3]).then_inc(dve0.sem, dve0.did("lbr"))
                dve.wait_ge(dve0.sem, dve0.at("lbr"))
                lbstep("lbp0", ltmp[1], ltmp[1], ltmp[3], ALU.mult)
                lbstep("lbp1", ltmp[2], ltmp[2], ltmp[3], ALU.mult)
                lbstep("lbc", ltmp[4], ltmp[1], ltmp[2], ALU.add)
                lbstep("lb", small[:, LB:LB + 16], ltmp[4], ltmp[1], ALU.subtract)
                dve.tensor_scalar(small[:, OMLB:OMLB + 16], small[:, LB:LB + 16], -1.0, 1.0, ALU.mult, ALU.add)\
                    .then_inc(dve0.sem, dve0.did("omlb"))

            def take_spatial_weights():
                dve.wait_ge(pool0.sem, pool0.at("zw"))
                for b in range(2):
                    dve.wait_ge(pe0.sem, pe0.at(f"wsT{b}"))
                    dve.copy_predicated(w_sT[:, 4 * b:4 * b + 4, :], tri_i[:].unsqueeze(1).broadcast_to([P, 4, P]),
                                        px[:, b, :].rearrange("p (a n) -> p a n", a=4))\
                        .then_inc(dve0.sem, dve0.did(f"wsT{b}"))

            def take_vectors():
                dve.wait_ge(pe0.sem, pe0.at("posT"))
                dve.tensor_copy(vT[:, KT:NV], px[:, 3, KT:NV]).then_inc(dve0.sem, dve0.did("vT"))
                dve.tensor_copy(posT[:], px[:, 3, 128:128 + 2 * NL]).then_inc(dve0.sem, dve0.did("posT"))
                dve.wait_ge(dve0.sem, dve0.at("posT"))
                dve.tensor_scalar(small[:, KGQ:KGQ + 3], vT[:, V_KG:V_KG + 3], vT[:, V_QG:V_QG + 1], None, ALU.mult)\
                    .then_inc(dve0.sem, dve0.did("gain"))

            def key_norm(n, kz, s):
                k4 = kz.rearrange("p a (h d) -> p (a h) d", h=2)
                sq4 = scr.rearrange("p (a d) -> p a d", a=4)
                dve.wait_ge(strip_out, s + 1)
                dve.wait_ge(pool0.sem, pool0.at("df"))
                dve.tensor_tensor(sq4, k4, k4, ALU.mult).then_inc(dveP.sem, dveP.did(f"sq{n}"))
                dve.wait_ge(dveP.sem, dveP.at(f"sq{n}"))
                dve.tensor_reduce(small[:, KSS:KSS + 4], sq4, AX.X, ALU.add).then_inc(dveP.sem, dveP.did(f"ss{n}"))
                dve.wait_ge(dveP.sem, dveP.at(f"ss{n}"))
                dve.tensor_scalar(small[:, KRS:KRS + 4], small[:, KSS:KSS + 4], 1.0 / HD, EPS, ALU.mult, ALU.add)\
                    .then_inc(dveP.sem, dveP.did(f"ms{n}"))
                dve.wait_ge(actP.sem, actP.at(f"rs{n}"))
                for m in range(4):
                    dve.tensor_scalar(k4[:, m, :], k4[:, m, :], small[:, KRS + m:KRS + m + 1], None, ALU.mult)\
                        .then_inc(dveP.sem, dveP.did(f"k{n}{m}"))

            def take_key_T(n):
                dve.wait_ge(peP.sem, peP.at(f"kT{n}"))
                dve.tensor_scalar(keysT[:, :, n * T:(n + 1) * T], px[:, n, :].rearrange("p (h t) -> p h t", h=2),
                                  small[:, KGQ + 1 + n:KGQ + 2 + n], None, ALU.mult)\
                    .then_inc(dveP.sem, dveP.did(f"kT{n}"))

            kph = [cathl[:, 4 * i:4 * i + 4].rearrange("p k a n -> p (k a n)")[:, 0:NL * 2 * CW]
                   .rearrange("p (l a n) -> p l a n", l=NL, a=2) for i in range(2)]
            kc = kcz[0:NC].rearrange("p (h d) -> p h d", h=2)

            def compressed_rms():
                dve.wait_ge(peP.sem, peP.at("ck1"))
                dve.tensor_copy(kc, px[0:NC, 1, 0:2 * HD].rearrange("p (h d) -> p h d", h=2))\
                    .then_inc(dveP.sem, dveP.did("kc"))
                dve.wait_ge(dveP.sem, dveP.at("kc"))
                ksq = Z[0:NC, 2, :, 0:HD]
                dve.tensor_tensor(ksq, kc, kc, ALU.mult).then_inc(dveP.sem, dveP.did("sqc"))
                dve.wait_ge(dveP.sem, dveP.at("sqc"))
                dve.tensor_reduce(small[0:NC, KSS:KSS + 2], ksq, AX.X, ALU.add).then_inc(dveP.sem, dveP.did("ssc"))
                dve.wait_ge(dveP.sem, dveP.at("ssc"))
                dve.tensor_scalar(small[0:NC, KRS:KRS + 2], small[0:NC, KSS:KSS + 2], 1.0 / HD, EPS, ALU.mult, ALU.add)\
                    .then_inc(dveP.sem, dveP.did("msc"))

            def compressed_norm():
                dve.wait_ge(actP.sem, actP.at("rsc"))
                for h in range(2):
                    dve.tensor_scalar(kc[:, h, :], kc[:, h, :], small[0:NC, KRS + h:KRS + h + 1], None, ALU.mult)\
                        .then_inc(dveP.sem, dveP.did(f"kn{h}"))

            def take_compressed():
                dve.wait_ge(peP.sem, peP.at("kcT"))
                dve.tensor_scalar(keysT[:, :, 2 * T:2 * T + NC], px[:, 1, 0:2 * 16].rearrange("p (h n) -> p h n", h=2)
                                  [:, :, 0:NC], small[:, KGQ:KGQ + 1], None, ALU.mult)\
                    .then_inc(dveP.sem, dveP.did("kcT"))

            def take_compressed_values():
                dve.wait_ge(peP.sem, peP.at("cv1"))
                dve.tensor_copy(vcmp[0:NC], px[0:NC, 3, 0:2 * HD].rearrange("p (h d) -> p h d", h=2))\
                    .then_inc(dveP.sem, dveP.did("vc"))

            kpos4 = kpos.rearrange("p (a b h n) -> p a b h n", a=2, b=16, h=2)
            for s in range(S_PRE, S_ATT):
                lows(dve, s + 1, (0,))
                if s == 0:
                    take_vectors()
                lows(dve, s + 1, (1,))
                if s == 9:
                    take_key_T(1)
                lows(dve, s + 1, (2,))
                if s == 5:
                    take_key_T(0)
                if s == 7:
                    take_compressed()
                if s in KV_GROUP:
                    take(dve, s, PAR[s], vals[:, (s - 7) // 2] if s >= 7 else Z[:, s % 4], n=COUNT[s])
                lows(dve, s + 1, (3,))
                if s in (0, 2):
                    i = s // 2
                    dve.wait_ge(strip_out, i + 1)
                    if i == 1:
                        dve.wait_ge(dveP.sem, dveP.at("kpl0"))
                        dve.wait_ge(actP.sem, actP.at("kp0"))
                    for n, (a, h) in enumerate(((0, 0), (0, 1), (1, 0), (1, 1))):
                        tok = Z[:, i, h, :].rearrange("p (m b) -> p b m", b=16)[:, :, a:a + NC]
                        pos = posT[:, i * NL + 16 * a:i * NL + 16 * a + 16].unsqueeze(2).broadcast_to([P, 16, NC])
                        dve.tensor_tensor(kpos4[:, a, :, h, :], tok, pos, ALU.add)\
                            .then_inc(dveP.sem, dveP.did(f"kp{'abcd'[n]}{i}"))
                    dve.wait_ge(actP.sem, actP.at(f"kp{i}"))
                    dve.tensor_tensor(kph[i][:, :, 1, :], kpos.rearrange("p (l n) -> p l n", l=NL),
                                      kph[i][:, :, 0, :].bitcast(F32), ALU.subtract)\
                        .then_inc(dveP.sem, dveP.did(f"kpl{i}"))
                if s == 2:
                    take_spatial_weights()
                    split_gate_columns()
                if s == 6:
                    compressed_rms()
                    compressed_norm()
                if s in (4, 6):
                    key_norm((s - 4) // 2, Z[:, (s - 1) % 4], s - 1)
                if s == 8:
                    lower_bound()
                if s == 9:
                    take_compressed_values()
                    dve.wait_ge(actP.sem, actP.at("gs"))
                    for r, (tile, br) in enumerate(((0, 1), (0, 2), (1, 1), (1, 2), (0, 0), (1, 0))):
                        dve.tensor_copy(small[:, GTAB:GTAB + 48].rearrange("p (h r) -> p h r", r=6)[:, :, r],
                                        gsc[:, tile * NG + br * 8:tile * NG + br * 8 + 8])\
                            .then_inc(dveP.sem, dveP.did(f"gt{r}"))

            with dve.Fori(0, 4) as p:
                s0 = p * 4 + S_ATT

                def scores(a):
                    dve.wait_ge(peA.sem, peA.at(f"s{a}", p))
                    dve.wait_ge(actA.sem, actA.at("rq", p))
                    dve.wait_ge(poolA.sem, poolA.at(f"b{a}", p))
                    if a == 1:
                        dve.wait_ge(peA.sem, peA.at("t0", p))
                    for n, (lo, hi, tile, ps, bl, bh) in enumerate((
                            (0, 256, 0, px[:, 0, 0:256], 0, 128), (256, 768, 1, px[:, 1, 0:512], 128, 384),
                            (768, 783, 0, px[:, 0, 256:271], 384, 399), (783, 798, 1, px[:, 0, 271:286], 399, 414))):
                        r = 2 if n < 2 else 1
                        w = bh - bl
                        dve.scalar_tensor_tensor(
                            prob[:, lo:hi].rearrange("p (r n) -> p r n", r=r), ps.rearrange("p (r n) -> p r n", r=r),
                            small[:, RSSQ + 2 * a + tile:RSSQ + 2 * a + tile + 1],
                            bias[:, a, bl:bh].unsqueeze(1).broadcast_to([P, r, w]), ALU.mult, ALU.add)\
                            .then_inc(dveA.sem, dveA.did(f"a{a}{n}"))
                    dve.wait_ge(dveA.sem, dveA.at(f"a{a}3", p))
                    for n, (lo, hi) in enumerate(((0, 256), (256, 768), (768, 798))):
                        dve.tensor_reduce(small[:, MX + 2 * n:MX + 2 * n + 2],
                                          prob[:, lo:hi].rearrange("p (r n) -> p r n", r=2), AX.X, ALU.max)\
                            .then_inc(dveA.sem, dveA.did(f"m{a}{n}"))
                    dve.wait_ge(dveA.sem, dveA.at(f"m{a}2", p))
                    dve.tensor_scalar(small[:, NM:NM + 6], small[:, MX:MX + 6], -1.0, 1e20, ALU.mult, ALU.min)\
                        .then_inc(dveA.sem, dveA.did(f"n{a}"))

                def weigh(a):
                    dve.wait_ge(actA.sem, actA.at(f"e{a}5", p))
                    dve.tensor_scalar(small[:, SUMS:SUMS + 6], small[:, SUMS:SUMS + 6], 1e-30, None, ALU.max)\
                        .then_inc(dveA.sem, dveA.did(f"r{a}x"))
                    dve.wait_ge(dveA.sem, dveA.at(f"r{a}x", p))
                    dve.reciprocal(small[:, SUMS:SUMS + 6], small[:, SUMS:SUMS + 6])\
                        .then_inc(dveA.sem, dveA.did(f"r{a}"))
                    dve.wait_ge(dveA.sem, dveA.at(f"r{a}", p))
                    dve.tensor_tensor(small[:, COEF:COEF + 6], small[:, SUMS:SUMS + 6],
                                      small[:, bass.ds(p * 12 + (GTAB + 6 * a), 6)], ALU.mult)\
                        .then_inc(dveA.sem, dveA.did(f"c{a}"))
                    dve.wait_ge(dveA.sem, dveA.at(f"c{a}", p))
                    for n, (lo, hi) in enumerate(((0, 256), (256, 768), (768, 798))):
                        w = (hi - lo) // 2
                        v = prob[:, lo:hi].rearrange("p (r n) -> p r n", r=2)
                        dve.tensor_tensor(v, v, small[:, COEF + 2 * n:COEF + 2 * n + 2].unsqueeze(2)
                                          .broadcast_to([P, 2, w]), ALU.mult)\
                            .then_inc(dveA.sem, dveA.did(f"p{a}{n}"))

                def take_pT(a):
                    dve.wait_ge(peA.sem, peA.at(f"t{a}", p))
                    dve.tensor_copy(probT[:, 1, 0:384], px[:, 3, 0:384]).then_inc(dveA.sem, dveA.did(f"pt{a}"))
                    dve.tensor_copy(probT[0:NC, 1, 384:512], px[0:NC, 3, 384:512])\
                        .then_inc(dveA.sem, dveA.did(f"pd{a}"))

                def gate(a):
                    dve.wait_ge(peA.sem, peA.at(f"o{a}", p))
                    dve.wait_ge(dveA.sem, dveA.at("sz", p))
                    dve.scalar_tensor_tensor(obuf[:, a, :], px[:, 2, 0:T], 0.5, sgz[:, a, :], ALU.mult, ALU.mult)\
                        .then_inc(dveA.sem, dveA.did(f"o{a}"))

                lows(dve, s0 + 1, (0, 1, 2))
                take(dve, s0, 0, Z[:, 0])
                lows(dve, s0 + 1, (3,))
                lows(dve, s0 + 2, (0,))
                dve.wait_ge(peA.sem, peA.at("rms", p))
                dve.tensor_scalar(small[:, RSSQ:RSSQ + 4], px[:, 3, 0:4], 1.0, EPS * HD, ALU.mult, ALU.add)\
                    .then_inc(dveA.sem, dveA.did("ms"))
                lows(dve, s0 + 2, (1,))
                scores(0)
                lows(dve, s0 + 2, (2,))
                weigh(0)
                take(dve, s0 + 1, 1, Z[:, 1])
                lows(dve, s0 + 2, (3,))
                lows(dve, s0 + 3, (0, 1))
                take_pT(0)
                scores(1)
                lows(dve, s0 + 3, (2,))
                weigh(1)
                take(dve, s0 + 2, 0, Z[:, 2])
                dve.wait_ge(actA.sem, actA.at("sg", p))
                dve.scalar_tensor_tensor(sgz[:], sgz[:], 1.0, Z[:, 1], ALU.add, ALU.mult)\
                    .then_inc(dveA.sem, dveA.did("sz"))
                gate(0)
                lows(dve, s0 + 3, (3,))
                lows(dve, s0 + 4, (0, 1))
                take_pT(1)
                lows(dve, s0 + 4, (2,))
                take(dve, s0 + 3, 1, Z[:, 3])
                lows(dve, s0 + 4, (3,))
                gate(1)
                dve.wait_ge(actA.sem, actA.at("cat", p))
                dve.tensor_tensor(cathl[:, bass.ds(p * 2 + 8, 2), 1, :], obuf[:],
                                  cathl[:, bass.ds(p * 2 + 8, 2), 0, :].bitcast(F32), ALU.subtract)\
                    .then_inc(dveA.sem, dveA.did("cat"))

            dve.wait_ge(actA.sem, actA.at("cat", 3))
            st = small[:, BST:BST + 24].rearrange("p (a b c) -> p a b c", a=2, b=2)
            for a in range(TT):
                for b in range(2):
                    dve.bn_stats(st[:, a, b, :], gav[:, a, 512 * b:512 * b + 512])\
                        .then_inc(dveG.sem, dveG.did(f"st{2 * a + b}"))
            dve.wait_ge(dveG.sem, dveG.at("st3"))
            mv = small[:, KSS:KSS + 4].rearrange("p (a n) -> p a n", a=2)
            for a in range(TT):
                dve.bn_aggr(mv[:, a, :], st[:, a].rearrange("p b c -> p (b c)")).then_inc(dveG.sem, dveG.did(f"ag{a}"))
            dve.wait_ge(dveG.sem, dveG.at("ag1"))
            dve.tensor_scalar(small[:, RSX:RSX + 2], mv[:, :, 1], EPS, None, ALU.add)\
                .then_inc(dveG.sem, dveG.did("ms"))
            def gain_or_bias(n):
                for a in range(TT):
                    dve.wait_ge(dveG.sem, dveG.at(f"v{2 * n + a}"))
                    dve.tensor_tensor(gav[:, a, :], gav[:, a, :], lngb[:, n, :], (ALU.mult, ALU.add)[n])\
                        .then_inc(dveG.sem, dveG.did(f"v{2 * n + 2 + a}"))

            def spatial(j):
                dve.wait_ge(peG.sem, peG.at(f"g{j}"))
                if j >= 1:
                    dve.wait_ge(dveG.sem, dveG.at(f"l{j - 1}"))
                dve.tensor_tensor(obuf[:], px[:, j, :].rearrange("p (a n) -> p a n", a=2), gu[:, 2 * j:2 * j + 2, :],
                                  ALU.mult).then_inc(dveG.sem, dveG.did(f"u{j}"))
                dve.wait_ge(dveG.sem, dveG.at(f"u{j}"))
                dve.tensor_tensor(obuf[:], obuf[:], Z[:, j], ALU.mult).then_inc(dveG.sem, dveG.did(f"w{j}"))
                dve.wait_ge(actG.sem, actG.at(f"c{j + 1}"))
                dve.tensor_tensor(cathl[:, 2 * j:2 * j + 2, 1, :], obuf[:],
                                  cathl[:, 2 * j:2 * j + 2, 0, :].bitcast(F32), ALU.subtract)\
                    .then_inc(dveG.sem, dveG.did(f"l{j}"))

            lows(dve, S_SGU + 1, (0,))
            dve.wait_ge(actG.sem, actG.at("rs"))
            dve.wait_ge(misc_in, 64)
            for a in range(TT):
                dve.tensor_scalar(gav[:, a, :], gav[:, a, :], mv[:, a, 0:1], small[:, RSX + a:RSX + a + 1],
                                  ALU.subtract, ALU.mult).then_inc(dveG.sem, dveG.did(f"v{a}"))
            lows(dve, S_SGU + 1, (1,))
            gain_or_bias(0)
            lows(dve, S_SGU + 1, (2,))
            for j in range(4):
                s = S_SGU + j
                if j >= 1:
                    lows(dve, s + 1, (0, 1, 2))
                take(dve, s, j % 2, Z[:, j])
                lows(dve, s + 1, (3,))
                if j == 0:
                    gain_or_bias(1)
                dve.wait_ge(actG.sem, actG.at(f"sg{j}"))
                dve.tensor_tensor(Z[:, j], Z[:, j], sgz[:], ALU.mult).then_inc(dveG.sem, dveG.did(f"z{j}"))
                dve.wait_ge(dveG.sem, dveG.at(f"z{j}"))
                if j >= 1:
                    spatial(j - 1)
            spatial(3)

            dve.memset(acc, 0.0).then_inc(dveG.sem, dveG.did("acc"))
            dve.wait_ge(dveG.sem, dveG.at("acc"))

            def out0(p, j, last=False):
                s = p * 2 + (S_OUT0 + j)
                lows(dve, s + 1, (0, 1, 2))
                take(dve, s, j, Z[:, j])
                dve.wait_ge(strip_out, s + 1)
                r = xT[:, bass.ds(p * 4 + 2 * j, 2), :]
                dve.tensor_tensor(r, r, Z[:, j], ALU.add).then_inc(dveO.sem, dveO.did("xa" if j == 0 else "xb"))
                lows(dve, s + 1, (3,))
                if last:
                    return
                dve.wait_ge(actO.sem, actO.at("sqa" if j == 0 else "sqb", p))
                dve.tensor_tensor(acc, acc, sq, ALU.add).then_inc(dveO.sem, dveO.did("aa" if j == 0 else "ab"))

            with dve.Fori(0, 3) as p:
                for j in range(2):
                    out0(p, j)
            for j in range(2):
                out0(3, j, last=j == 1)
            dve.wait_ge(peR.sem, peR.at("ss"))
            dve.tensor_scalar(hRS[:, 0:T], px[:, 0, 0:T], 1.0 / D, EPS, ALU.mult, ALU.add)\
                .then_inc(dveR.sem, dveR.did("ms"))
            dve.wait_ge(actR.sem, actR.at("rs"))
            norm(1, V_N1, hRS[:, 0:T])
            dve.memset(hAT, 0.0).then_inc(dveR.sem, dveR.did("at0"))
            dve.wait_ge(dveR.sem, dveR.at("at0"))
            dve.wait_ge(poolM.sem, poolM.at("zero"))

            def chunks(ap):
                return ap.rearrange("p (c t) -> p c t", t=CH)

            lows(dve, S_HGRN + 1, (0, 1, 2))
            with dve.Fori(0, 8) as i:
                s0 = i * 4 + S_HGRN
                take(dve, s0, 0, Z[:, 0])
                lows(dve, s0 + 1, (3,))
                dve.wait_ge(actH.sem, actH.at("sf", i))
                for h in range(2):
                    dve.tensor_scalar(hF[:, h * T:(h + 1) * T], hF[:, h * T:(h + 1) * T],
                                      small[:, bass.ds(i * 2 + (OMLB + h), 1)], small[:, bass.ds(i * 2 + (LB + h), 1)],
                                      ALU.mult, ALU.add).then_inc(dveH.sem, dveH.did(f"f{h}"))
                dve.wait_ge(dveH.sem, dveH.at("f1", i))
                dve.tensor_scalar(hK, hF, -1.0, 1.0, ALU.mult, ALU.add).then_inc(dveH.sem, dveH.did("k"))
                lows(dve, s0 + 2, (0,))
                dve.wait_ge(actH.sem, actH.at("g", i))
                dve.tensor_tensor_scan(hGS, starts, hG, 0.0, ALU.mult, ALU.add).then_inc(dveH.sem, dveH.did("gs"))
                dve.wait_ge(dveH.sem, dveH.at("gs", i))
                dve.tensor_tensor(chunks(hD1), chunks(hGS), chunks(hGS)[:, :, CH // 2 - 1:CH // 2]
                                  .broadcast_to([P, 8, CH]), ALU.subtract).then_inc(dveH.sem, dveH.did("d1"))
                dve.tensor_tensor(chunks(hD2), chunks(hGS)[:, :, CH - 1:CH].broadcast_to([P, 8, CH]), chunks(hGS),
                                  ALU.subtract).then_inc(dveH.sem, dveH.did("d2"))
                lows(dve, s0 + 2, (1, 2))
                take(dve, s0 + 1, 1, Z[:, 1])
                lows(dve, s0 + 2, (3,))
                dve.wait_ge(actH.sem, actH.at("e1", i))
                dve.tensor_tensor(hKE, hK, hE2, ALU.mult).then_inc(dveH.sem, dveH.did("kt"))
                dve.wait_ge(strip_out, s0 + 2)
                dve.tensor_tensor(hQE, Z[:, 1].rearrange("p a n -> p (a n)"), hD1, ALU.mult)\
                    .then_inc(dveH.sem, dveH.did("qe"))
                lows(dve, s0 + 3, (0, 1, 2))
                dve.wait_ge(peH.sem, peH.at("at", i))
                dve.sem_inc(seen, 1)
                dve.copy_predicated(hAT.rearrange("p (b t) -> p b t", b=4),
                                    tri64_i[:].unsqueeze(1).broadcast_to([P, 4, P]),
                                    px[:, 2, :].rearrange("p (b t) -> p b t", b=4))\
                    .then_inc(dveH.sem, dveH.did("at"))
                take(dve, s0 + 2, 0, Z[:, 2])
                lows(dve, s0 + 3, (3,))
                lows(dve, s0 + 4, (0,))
                dve.wait_ge(peH.sem, peH.at("kv", i))
                for h in range(2):
                    dve.tensor_copy(hST[:, h, 0, :], kv_at(h, 0)).then_inc(dveH.sem, dveH.did(f"s1{h}"))
                for c in range(1, 3):
                    for h in range(2):
                        dve.wait_ge(dveH.sem, dveH.at(f"s{c}{h}", i))
                        end = h * T + c * CH + CH - 1
                        dve.scalar_tensor_tensor(hST[:, h, c, :], hST[:, h, c - 1, :], hE3[:, end:end + 1],
                                                 kv_at(h, c), ALU.mult, ALU.add)\
                            .then_inc(dveH.sem, dveH.did(f"s{c + 1}{h}"))
                lows(dve, s0 + 4, (1, 2))
                take(dve, s0 + 3, 1, Z[:, 3])
                dve.wait_ge(peH.sem, peH.at("ss", i))
                dve.tensor_scalar(hRS, px[:, 3, :], 1.0 / HD, EPS, ALU.mult, ALU.add)\
                    .then_inc(dveH.sem, dveH.did("ms"))
                lows(dve, s0 + 4, (3,))
                dve.wait_ge(actH.sem, actH.at("rs", i))
                dve.scalar_tensor_tensor(hO, px[:, 2, :], vT[:, V_OG:V_OG + 1], hRS, ALU.mult, ALU.mult)\
                    .then_inc(dveH.sem, dveH.did("o1"))
                dve.wait_ge(dveH.sem, dveH.at("o1", i))
                dve.wait_ge(poolH.sem, poolH.at("zs", i))
                dve.tensor_tensor(hO, hO, hZS, ALU.mult).then_inc(dveH.sem, dveH.did("o2"))
                lows(dve, s0 + 5, (0,))
                dve.wait_ge(actH.sem, actH.at("cat", i))
                dve.tensor_tensor(cathl[:, bass.ds(i * 2, 2), 1, :], hO.rearrange("p (a n) -> p a n", a=2),
                                  cathl[:, bass.ds(i * 2, 2), 0, :].bitcast(F32), ALU.subtract)\
                    .then_inc(dveH.sem, dveH.did("lo"))
                lows(dve, s0 + 5, (1, 2))

            def out1(p, j, last=False, first=False):
                s = p * 2 + (S_OUT1 + j)
                if not last:
                    lows(dve, s + 1, () if first else (0, 1, 2))
                if not (isinstance(p, int) and p == 0):
                    dve.wait_ge(y_out[j], p * 16)
                take(dve, s, j, Z[:, j])
                if not last:
                    lows(dve, s + 1, (3,))

            for j in range(2):
                out1(0, j, first=j == 0)
            with dve.Fori(1, 3) as p:
                for j in range(2):
                    out1(p, j)
            for j in range(2):
                out1(3, j, last=j == 1)

        @block.tensor
        def _(pe):
            def strip(s, par, kind, xs, order=None, first=False, hooks=None, late=None, free=None):
                if not first:
                    pe.wait_ge(strip_out, s - 1 if free is None else free)
                for q in range(NQ):
                    if isinstance(s, int) and s == 0:
                        pe.wait_ge(lo_pool, q + 1)
                    else:
                        pe.wait_ge(lo_done, s * 4 + (q + 1))
                    for g in range(2):
                        bank = pp[:, 2 * par + g, :]
                        if late and q == NQ - 1:
                            late(g)
                        for k in range(KQ):
                            kt = (order or (lambda n: n))(KQ * q + k)
                            begin, end = q == 0 and k == 0, q == NQ - 1 and k == KQ - 1
                            if kind == "B":
                                full = (bank, whl[:, q, k, 0, g * P:(g + 1) * P], xs[:, kt, :, :])
                                half = (bank[:, T:], whl[:, q, k, 1, g * P:(g + 1) * P], xs[:, kt, 0, :])
                            else:
                                full = (bank, xs[:, kt, 0, g * P:(g + 1) * P], whl[:, q, k, :, :])
                                half = (bank[:, T:], xs[:, kt, 1, g * P:(g + 1) * P], whl[:, q, k, 0, :])
                            if end:
                                pe.matmul(*half, start=False, stop=False)
                                mm = pe.matmul(*full, start=False, stop=True)
                            else:
                                pe.matmul(*full, start=begin, stop=False)
                                mm = pe.matmul(*half, start=False, stop=False)
                    mm.then_inc(pe_q, 1)
                    if hooks and q in hooks:
                        hooks[q]()

            pe.wait_ge(pool0.sem, pool0.at("ident"))
            for a in range(TT):
                pe.wait_ge(x_in[a], 32)
                for b in range(8):
                    for k in range(2):
                        kt = 2 * b + k
                        mm = pe.transpose((pp if b < 4 else px)[:, b % 4, k * T + a * P:k * T + (a + 1) * P],
                                          xnat[:, a, kt * P:(kt + 1) * P], ident[:])
                    if a == TT - 1:
                        mm.then_inc(pe0.sem, pe0.did(f"xT{b}"))
            pe.wait_ge(dve0.sem, dve0.at("diag1"))
            pe.wait_ge(pool0.sem, pool0.at("ms1"))
            pe.matmul(pp[:, 1, 0:T], ones[:], tmp[:, 0, 0, :], start=True, stop=True)\
                .then_inc(pe0.sem, pe0.did("rs"))
            pe.wait_ge(gain_in, 16)
            pe.wait_ge(dve0.sem, dve0.at("xT7"))
            pe.transpose(px[:, 3, 0:KT], vecs[V_N0:V_N0 + KT, :], ident[0:KT, 0:KT]).then_inc(pe0.sem, pe0.did("gT"))
            pe.wait_ge(dve0.sem, dve0.at("rsb"))
            pe.wait_ge(act0.sem, act0.at("xT6"))
            pe.wait_ge(xlo_done, 1)

            def normed(layer):
                return {0: lambda: pe.wait_ge(xlo_pool, layer + 1), 1: lambda: pe.wait_ge(xlo_done, 3 * layer + 2),
                        2: lambda: pe.wait_ge(xlo_done, 3 * layer + 3)}

            def vectors():
                pe.wait_ge(vec_in, 16 * 7)
                pe.transpose(px[:, 3, 0:P], vecs[:], ident[:]).then_inc(pe0.sem, pe0.did("vT"))
                pe.transpose(px[:, 3, P:P + 2 * NL], posr[:], ident[0:2 * NL, 0:2 * NL])\
                    .then_inc(pe0.sem, pe0.did("posT"))

            def spatial_weights():
                pe.wait_ge(sg_in, 16)
                for b in range(2):
                    for g in range(4):
                        mm = pe.transpose(px[:, b, g * P:(g + 1) * P], sgw[:, 4 * b + g, :], ident[:])
                    mm.then_inc(pe0.sem, pe0.did(f"wsT{b}"))

            def key_T(n):
                if n == 1:
                    pe.wait_ge(dveP.sem, dveP.at("kcT"))
                pe.wait_ge(dve0.sem, dve0.at("wsT1"))
                pe.wait_ge(dveP.sem, dveP.at(f"k{n}3"))
                for a in range(TT):
                    for h in range(2):
                        mm = pe.transpose(px[:, n, h * T + a * P:h * T + (a + 1) * P],
                                          Z[:, 3 - 2 * n, a, h * HD:(h + 1) * HD], ident[:])
                mm.then_inc(peP.sem, peP.did(f"kT{n}"))

            def branch_gates():
                pe.wait_ge(dve0.sem, dve0.at("wg"))
                for k in range(KT):
                    mm = pe.matmul(px[0:2 * NG, 3, :], wghl[:, k].rearrange("p a n -> p (a n)"), xhl[:, k],
                                   start=k == 0, stop=k == KT - 1)
                mm.then_inc(peP.sem, peP.did("gates"))

            def fold_gates():
                pe.wait_ge(actP.sem, actP.at("gc"))
                pe.wait_ge(pool0.sem, pool0.at("foldg1"))
                for a in range(TT):
                    for n in range(2):
                        pe.matmul(px[:, 3, 32 * a:32 * a + NG], gpart[0:2 * NG, n * T + a * P:n * T + (a + 1) * P],
                                  fold_g[:], start=n == 0, stop=n == 1)

            def compress_out(i):
                pe.wait_ge(actP.sem, actP.at("hk1" if i == 0 else "gs"))
                pe.wait_ge(misc_in, 64)
                for h in range(2):
                    for g in range(2):
                        mm = pe.matmul(px[0:NC, 1 + 2 * i, h * HD:(h + 1) * HD], hid[:, i, g, NC * h:NC * h + NC],
                                       w2[:, i, g, :],
                                       start=g == 0, stop=g == 1)
                    mm.then_inc(peP.sem, peP.did(f"c{'kv'[i]}{h}"))

            def fold_hidden(i):
                pe.wait_ge(pool0.sem, pool0.at("fold1"))
                pe.wait_ge(actP.sem, actP.at(f"cs{i}"))
                for g in range(2):
                    for n in range(2):
                        c = 256 + 64 * i + 32 * g
                        mm = pe.matmul(px[:, 3, c:c + CW], cpart[0:2 * CW, n * SW + g * P:n * SW + (g + 1) * P],
                                       fold[:], start=n == 0, stop=n == 1)
                mm.then_inc(peP.sem, peP.did(("fk", "fv")[i]))

            def compressed_key_T():
                pe.wait_ge(dveP.sem, dveP.at("kn1"))
                for h in range(2):
                    mm = pe.transpose(px[:, 1, 16 * h:16 * h + NC], kcz[0:NC, h * HD:(h + 1) * HD],
                                      ident[0:NC, 0:NC])
                mm.then_inc(peP.sem, peP.did("kcT"))

            first = normed(0)
            strip(0, 0, "B", xhl, first=True, hooks={0: lambda: (first[0](), vectors()), 1: first[1], 2: first[2]})
            strip(1, 1, "B", xhl, first=True, hooks={3: spatial_weights})
            kph = [cathl[:, 4 * i:4 * i + 4].rearrange("p k a n -> p (k a n)")[:, 0:NL * 2 * CW]
                   .rearrange("p (l a n) -> p l a n", l=NL, a=2) for i in range(2)]

            def compress(s):
                i, half = COMPRESS[s]
                pe.wait_ge(dveP.sem, dveP.at(f"kpl{i}"))
                if i == 1:
                    pe.wait_ge(actP.sem, actP.at("cs0"))
                for q in range(NQ):
                    pe.wait_ge(lo_done, s * 4 + q + 1)
                    for k in range(KQ):
                        li = 16 * half + KQ * q + k
                        mm = pe.matmul(px[0:2 * CW, 2, :], kph[i][:, li].rearrange("p a n -> p (a n)"),
                                       whl[:, q, k, :, :], start=li == 0, stop=li == NL - 1)
                    mm.then_inc(pe_q, 1)

            compress(2)
            strip(3, 0, "A", xhl, free=1)
            compress(4)
            strip(5, 1, "A", xhl, free=2,
                  hooks={0: lambda: fold_hidden(0), 2: lambda: key_T(0), 3: lambda: compress_out(0)})
            compress(6)
            strip(7, 0, "A", xhl, free=4, hooks={2: compressed_key_T, 3: branch_gates})
            compress(8)
            strip(9, 1, "A", xhl, free=6, hooks={0: lambda: (fold_gates(), fold_hidden(1)),
                                                     1: lambda: key_T(1), 2: lambda: compress_out(1)})
            for kv in range(2):
                with pe.Fori(0, 2) as r:
                    p = r + 2 * kv
                    s0 = p * 4 + S_ATT
                    kT = keysT[:, kv, :]

                    def rms():
                        pe.wait_ge(dveP.sem, dveP.at("vc"))
                        pe.wait_ge(actA.sem, actA.at("sq", p))
                        for h in range(2):
                            for a in range(TT):
                                mm = pe.matmul(px[:, 3, 2 * h + a:2 * h + a + 1], obuf[:, h, a * P:(a + 1) * P],
                                               ones[:, 0:1], start=True, stop=True)
                        mm.then_inc(peA.sem, peA.did("rms"))

                    def score(h):
                        if h == 1:
                            pe.wait_ge(dveA.sem, dveA.at("a03", p))
                        q0, q1 = Z[:, 0, h, 0:P], Z[:, 0, h, P:T]
                        pe.matmul(px[:, 0, 0:T].rearrange("p (b n) -> p b n", b=2), q0,
                                  kT[:, 0:2 * T].rearrange("p (b n) -> p b n", b=2)[:, :, 0:P], start=True, stop=True)
                        pe.matmul(px[:, 1, 0:2 * T], q1, kT[:, 0:2 * T], start=True, stop=True)
                        pe.matmul(px[:, 0, T:T + NC], q0, kT[:, 2 * T:2 * T + NC], start=True, stop=True)
                        pe.matmul(px[:, 0, T + NC:T + 2 * NC], q1, kT[:, 2 * T:2 * T + NC], start=True, stop=True)\
                            .then_inc(peA.sem, peA.did(f"s{h}"))

                    def turn(h):
                        pe.wait_ge(dveA.sem, dveA.at(f"p{h}2", p))
                        if h == 1:
                            pe.wait_ge(dveA.sem, dveA.at("o0", p))
                        for b, (t0, tile1) in enumerate(((0, 256), (128, 512))):
                            for n, c in enumerate((t0, tile1, tile1 + P)):
                                pe.transpose(px[:, 2 + b, n * P:(n + 1) * P], prob[:, c:c + P], ident[:])
                        pe.transpose(px[0:NC, 2, 384:512], prob[:, 768:783], ident[:])
                        pe.transpose(px[0:NC, 3, 384:512], prob[:, 783:798], ident[:])\
                            .then_inc(peA.sem, peA.did(f"t{h}"))

                    def mix(h):
                        pe.wait_ge(actA.sem, actA.at(f"pc{h}", p))
                        pe.wait_ge(dveA.sem, dveA.at(f"pd{h}", p))
                        hv = slice(kv * HD, (kv + 1) * HD)
                        for tile in range(TT):
                            terms = []
                            for b in range(2):
                                if tile == 0:
                                    terms.append((vals[:, b, 0, hv], probT[:, b, 0:P]))
                                else:
                                    terms.append((vals[:, b, 0, hv], probT[:, b, P:2 * P]))
                                    terms.append((vals[:, b, 1, hv], probT[:, b, 2 * P:3 * P]))
                            terms.append((vcmp[0:NC, kv, :], probT[0:NC, tile, 384:512]))
                            for n, (v, pr) in enumerate(terms):
                                mm = pe.matmul(px[:, 2, tile * P:(tile + 1) * P], v, pr, start=n == 0,
                                               stop=n == len(terms) - 1)
                        mm.then_inc(peA.sem, peA.did(f"o{h}"))

                    strip(s0, 0, "B", xhl)
                    strip(s0 + 1, 1, "B", xhl, hooks={1: lambda: (rms(), score(0))})
                    strip(s0 + 2, 0, "A", xhl, hooks={1: lambda: (turn(0), score(1)), 3: lambda: mix(0)})
                    strip(s0 + 3, 1, "B", xhl, hooks={2: lambda: turn(1), 3: lambda: mix(1)})

            def groups(j):
                pe.wait_ge(dveG.sem, dveG.at("v5"))
                pe.wait_ge(misc_in, 64)
                for n in range(2):
                    g = 2 * j + n
                    for a in range(TT):
                        o = px[:, j, n * T + a * P:n * T + (a + 1) * P]
                        pe.matmul(o, gav[:, a, g * P:(g + 1) * P], w_sT[:, g, :], start=True, stop=False)
                        mm = pe.matmul(o, ones[0:1, :], sgub[0:1, g * P:(g + 1) * P], start=False, stop=True)
                mm.then_inc(peG.sem, peG.did(f"g{j}"))

            strip(S_SGU, 0, "B", xhl)
            for j in range(1, 4):
                strip(S_SGU + j, j % 2, "B", xhl, hooks={3: lambda j=j: groups(j - 1)})
            groups(3)

            def swapped(k):
                return (k + KT // 2) % KT

            def wait_cat(name):
                pe.wait_ge(dveG.sem, dveG.at(name))

            pe.wait_ge(dveA.sem, dveA.at("cat", 3))
            strip(S_OUT0, 0, "B", cathl, order=swapped, hooks={1: lambda: wait_cat("l1"), 2: lambda: wait_cat("l3")})
            strip(S_OUT0 + 1, 1, "B", cathl, order=swapped)
            with pe.Fori(1, 4) as p:
                for j in range(2):
                    strip(p * 2 + (S_OUT0 + j), j, "B", cathl, order=swapped)
            pe.wait_ge(dveO.sem, dveO.at("aa", 3))
            for n in range(2):
                pe.matmul(px[:, 0, 0:T], ones[:], acc[:, n * T:(n + 1) * T], start=n == 0, stop=False)
            pe.wait_ge(actO.sem, actO.at("sqb", 3))
            for n in range(2):
                mm = pe.matmul(px[:, 0, 0:T], ones[:], sq[:, n * T:(n + 1) * T], start=False, stop=n == 1)
            mm.then_inc(peR.sem, peR.did("ss"))
            pe.wait_ge(xlo_done, 4)

            with pe.Fori(0, 8) as i:
                s0 = i * 4 + S_HGRN

                def intra():
                    pe.wait_ge(poolH.sem, poolH.at("ks", i))
                    for b in range(4):
                        mm = pe.transpose(px[:, 3, b * P:(b + 1) * P], hKS[:, b * P:(b + 1) * P], ident[:])
                    mm.then_inc(peH.sem, peH.did("ksT"))
                    pe.wait_ge(dveH.sem, dveH.at("qe", i))
                    for b in range(4):
                        mm = pe.matmul(px[:, 2, b * P:(b + 1) * P], hKE[:, b * P:(b + 1) * P],
                                       hQE[:, b * P:(b + 1) * P], start=True, stop=True)
                    mm.then_inc(peH.sem, peH.did("at"))

                def chunk_kv():
                    pe.wait_ge(actH.sem, actH.at("kn", i))
                    pe.wait_ge(strip_out, s0 + 3)
                    for h in range(2):
                        for c in range(3):
                            r0, a = CH * (c % 2), c // 2
                            b = 2 * h + a
                            mm = pe.matmul(kv_at(h, c), hKN[r0:r0 + CH, b * P:(b + 1) * P],
                                           Z[r0:r0 + CH, 2, a, h * HD:(h + 1) * HD], start=True, stop=True)
                    mm.then_inc(peH.sem, peH.did("kv"))

                def outputs():
                    pe.wait_ge(dveH.sem, dveH.at("s31", i))
                    pe.wait_ge(poolH.sem, poolH.at("qi", i))
                    for h in range(2):
                        for a in range(TT):
                            b = 2 * h + a
                            pe.matmul(px[:, 2, b * P:(b + 1) * P], Z[:, 2, a, h * HD:(h + 1) * HD],
                                      hAT[:, b * P:(b + 1) * P], start=True, stop=False, skip_group_check=True)
                            for c in (1,) if a == 0 else (2, 3):
                                mm = pe.matmul(px[:, 2, h * T + c * CH:h * T + (c + 1) * CH], hST[:, h, c - 1, :],
                                               hQI[:, h * T + c * CH:h * T + (c + 1) * CH], start=False,
                                               stop=c != 2, skip_group_check=True)
                    mm.then_inc(peH.sem, peH.did("o"))

                def squares():
                    pe.wait_ge(actH.sem, actH.at("sq", i))
                    pe.matmul(px[:, 3, :], ones[:], hSQ, start=True, stop=True).then_inc(peH.sem, peH.did("ss"))

                strip(s0, 0, "B", xhl, hooks=normed(1))
                strip(s0 + 1, 1, "B", xhl)
                strip(s0 + 2, 0, "A", xhl, hooks={1: intra})
                strip(s0 + 3, 1, "B", xhl, hooks={0: chunk_kv, 2: outputs, 3: squares})

            def residual(p, j):
                def late(g):
                    if g == 0:
                        pe.wait_ge(poolR.sem, poolR.at("ra" if j == 0 else "rb", p))
                    for c in range(2):
                        pe.matmul(pp[:, 2 * j + g, c * P:(c + 1) * P], xres[:, j, c, g * P:(g + 1) * P], ident[:],
                                  start=False, stop=False)
                return late

            def last_heads():
                pe.wait_ge(dveH.sem, dveH.at("lo", 7))

            pe.wait_ge(dveH.sem, dveH.at("lo", 6))
            for j in range(2):
                strip(S_OUT1 + j, j, "A", cathl, late=residual(0, j), hooks={2: last_heads} if j == 0 else None)
            with pe.Fori(1, 4) as p:
                for j in range(2):
                    strip(p * 2 + (S_OUT1 + j), j, "A", cathl, late=residual(p, j))


_INS = ['x', 'even_norm', 'even_w_in', 'sgu_ln_g', 'sgu_ln_b', 'sgu_w', 'sgu_b', 'nsa_q_gain', 'nsa_k_gain',
        'cmp_pos', 'cmp_w1', 'cmp_b1', 'cmp_w2', 'even_w_out', 'odd_norm', 'odd_w_in', 'hgrn_lb',
        'hgrn_out_gain', 'odd_w_out']
_ONE = {'even_w_in', 'sgu_w', 'sgu_b', 'nsa_k_gain', 'cmp_pos', 'cmp_w1', 'cmp_b1', 'cmp_w2', 'even_w_out',
        'odd_w_in', 'odd_w_out', 'sgu_ln_g', 'sgu_ln_b'}


def kernel(**inputs):
    import numpy as _np
    import concourse.bacc as _bacc
    from concourse import mybir as _mybir
    from concourse.bass_utils import run_bass_kernel_spmd as _run

    nc = _bacc.Bacc("TRN2", target_bir_lowering=False, num_devices=1)
    arrays, args = {}, []
    for name in _INS:
        a = _np.ascontiguousarray(inputs[name])
        if name in _ONE:
            a = a[0]
        arrays[f"in_{name}"] = a
        args.append(nc.dram_tensor(f"in_{name}", a.shape, _mybir.dt.from_np(a.dtype), kind="ExternalInput").ap())
    out = nc.dram_tensor("out_y", (T, D), F32, kind="ExternalOutput").ap()
    trunk(nc, *args, out)
    r = _run(nc, [arrays], core_ids=[0])
    return r.results[0]["out_y"].reshape(1, T, D)
```
